# Optimizing a Trainium2 kernel written in Bass

```python
import math
import jax
import jax.numpy as jnp
from jax import lax
import numpy as np

D_MODEL = 1024
BATCH = 1
SEQ = 512
DEPTH = 2

HEAD_DIM = 64
D_FF = 2816
ROPE_THETA = 10000.0
NORM_EPS = 1e-6
NEG_INF = -1e30

A_HEADS = 4
A_VDIM = 2 * HEAD_DIM
A_OUT = A_HEADS * A_VDIM
A_QBLOCK = 128
A_SIZES = (2 * A_HEADS * HEAD_DIM, 2 * A_HEADS * HEAD_DIM, A_OUT)
A_COLS = sum(A_SIZES)

B_HEADS = 8
B_DIM = B_HEADS * HEAD_DIM
B_W_RANK = 64
B_A_RANK = 64
B_G_RANK = 128
B_GN_EPS = 64e-5
B_SIZES = (B_DIM, B_DIM, B_DIM, B_W_RANK, B_A_RANK, B_G_RANK)
B_COLS = sum(B_SIZES)
AB_COLS = A_COLS + B_COLS

C_HEADS = 8
C_KV_GROUPS = 2
C_HPG = C_HEADS // C_KV_GROUPS
C_OUT = C_HEADS * HEAD_DIM
C_KVW = C_KV_GROUPS * HEAD_DIM
CMP_BLOCK = 32
CMP_STRIDE = 16
CMP_HIDDEN = 256
SLC_BLOCK = 64
N_SELECT = 16
WINDOW = 512
C_QBLOCK = 64
FORCE_BONUS = 1e4
C_SIZES = (C_OUT, C_KVW, C_KVW, C_KVW, C_KVW, C_KVW, C_KVW, 3 * C_HEADS)
C_COLS = sum(C_SIZES)

D_HEADS = 4
D_QK = 64
D_V = 128
D_OUT = D_HEADS * D_V
D_CHUNK = 64
D_CONV = 4
D_SIZES = (D_HEADS * D_QK, D_HEADS * D_QK, D_OUT, D_HEADS, D_HEADS, D_OUT)
D_COLS = sum(D_SIZES)
CD_COLS = C_COLS + D_COLS


def rmsnorm(x, w, eps=NORM_EPS):
    xf = x.astype(jnp.float32)
    y = xf * lax.rsqrt(jnp.mean(xf * xf, axis=-1, keepdims=True) + eps)
    return (y * w.astype(jnp.float32)).astype(x.dtype)

def split_cols(p, sizes):
    return jnp.split(p, [int(c) for c in np.cumsum(sizes)[:-1]], axis=-1)

def rope_tables(pos):
    inv = jnp.asarray(ROPE_THETA ** (-np.arange(0, HEAD_DIM, 2, dtype=np.float32) / HEAD_DIM), jnp.float32)
    ang = pos[:, None] * inv[None, :]
    ang = jnp.concatenate([ang, ang], axis=-1)
    return jnp.cos(ang), jnp.sin(ang)

def apply_rope(x, cos, sin):
    x1, x2 = jnp.split(x, 2, axis=-1)
    rot = jnp.concatenate([-x2, x1], axis=-1)
    return (x * cos + rot * sin).astype(x.dtype)

def swiglu(x, wg, wu, wd):
    return (jax.nn.silu(x @ wg) * (x @ wu)) @ wd

def lambda_init(layer):
    return 0.8 - 0.6 * math.exp(-0.3 * layer)

def diff_attention(qa, ka, va, lam, subln_w, lam_init, cos, sin):
    B, T, _ = qa.shape
    q = apply_rope(qa.reshape(B, T, A_HEADS, 2, HEAD_DIM).transpose(0, 2, 3, 1, 4), cos, sin) * (HEAD_DIM ** -0.5)
    k = apply_rope(ka.reshape(B, T, A_HEADS, 2, HEAD_DIM).transpose(0, 2, 3, 1, 4), cos, sin)
    v = va.reshape(B, T, A_HEADS, A_VDIM).transpose(0, 2, 1, 3)
    lam32 = lam.astype(jnp.float32)
    lam_full = jnp.exp(jnp.sum(lam32[0] * lam32[1])) - jnp.exp(jnp.sum(lam32[2] * lam32[3])) + lam_init
    nb = T // A_QBLOCK
    qb = q.reshape(B, A_HEADS, 2, nb, A_QBLOCK, HEAD_DIM).transpose(3, 0, 1, 2, 4, 5)
    kpos = jnp.arange(T)

    def block(args):
        qi, i = args
        s = jnp.einsum('bhcqd,bhckd->bhcqk', qi, k).astype(jnp.float32)
        qpos = i * A_QBLOCK + jnp.arange(A_QBLOCK)
        mask = kpos[None, :] <= qpos[:, None]
        p = jax.nn.softmax(jnp.where(mask, s, NEG_INF), axis=-1)
        attn = p[:, :, 0] - lam_full * p[:, :, 1]
        return jnp.einsum('bhqk,bhke->bhqe', attn.astype(v.dtype), v)

    o = lax.map(block, (qb, jnp.arange(nb)))
    o = o.transpose(1, 0, 3, 2, 4).reshape(B, T, A_HEADS, A_VDIM)
    o = rmsnorm(o, subln_w) * (1.0 - lam_init)
    return o.reshape(B, T, A_OUT)

def rwkv7_time_mix(p, mu, w0, w2, a0, a2, g2, k_k, k_a, r_k, ln_w, ln_b):
    B, T, _ = p.shape
    prev = jnp.pad(p[:, :-1], ((0, 0), (1, 0), (0, 0)))
    xm = p + (prev - p) * mu
    r, k, v, wl, al, gl = split_cols(xm, B_SIZES)
    w = -jax.nn.softplus(-(w0 + jnp.tanh(wl) @ w2)) - 0.5
    a = jax.nn.sigmoid(a0 + al @ a2)
    g = jax.nn.sigmoid(gl) @ g2

    def heads(z):
        return z.reshape(B, T, B_HEADS, HEAD_DIM).astype(jnp.float32)

    kk = heads(k * k_k)
    kk = kk * lax.rsqrt(jnp.sum(kk * kk, axis=-1, keepdims=True) + 1e-12)
    k = k * (1.0 + (a - 1.0) * k_a)
    r_h, k_h, v_h, a_h = heads(r), heads(k), heads(v), heads(a)
    decay = jnp.exp(-jnp.exp(heads(w)))

    def step(S, inp):
        r_t, w_t, k_t, v_t, kk_t, a_t = inp
        S = (S * w_t[:, :, None, :]
             - jnp.einsum('bhvk,bhk->bhv', S, kk_t)[..., None] * (kk_t * a_t)[:, :, None, :]
             + v_t[..., None] * k_t[:, :, None, :])
        return S, jnp.einsum('bhvk,bhk->bhv', S, r_t)

    def tm(z):
        return z.transpose(1, 0, 2, 3)

    S0 = jnp.zeros((B, B_HEADS, HEAD_DIM, HEAD_DIM), jnp.float32)
    _, y = lax.scan(step, S0, (tm(r_h), tm(decay), tm(k_h), tm(v_h), tm(kk), tm(a_h)))
    y = y.transpose(1, 0, 2, 3)
    mean = jnp.mean(y, axis=-1, keepdims=True)
    var = jnp.mean(jnp.square(y - mean), axis=-1, keepdims=True)
    y = (y - mean) * lax.rsqrt(var + B_GN_EPS) * ln_w.reshape(B_HEADS, HEAD_DIM) + ln_b.reshape(B_HEADS, HEAD_DIM)
    bonus = jnp.sum(r_h * k_h * r_k, axis=-1, keepdims=True) * v_h
    out = (y + bonus).reshape(B, T, B_DIM).astype(p.dtype)
    return out * g

def compress_blocks(z, pe, w1, w2):
    B, G, T, d = z.shape
    n_cmp = (T - CMP_BLOCK) // CMP_STRIDE + 1
    idx = CMP_STRIDE * np.arange(n_cmp)[:, None] + np.arange(CMP_BLOCK)[None, :]
    blocks = (z[:, :, idx] + pe).reshape(B, G, n_cmp, CMP_BLOCK * d)
    return jax.nn.gelu(blocks @ w1) @ w2

def selection_map(n_cmp, n_slc):
    c0 = CMP_STRIDE * np.arange(n_cmp)[:, None]
    s0 = SLC_BLOCK * np.arange(n_slc)[None, :]
    shared = np.clip(np.minimum(c0 + CMP_BLOCK, s0 + SLC_BLOCK) - np.maximum(c0, s0), 0, None)
    return jnp.asarray(shared / CMP_BLOCK, jnp.float32)

def native_sparse_attention(q, kc, vc, ks, vs, kw, vw, gate_logits,
                            pe_k, w1_k, w2_k, pe_v, w1_v, w2_v, cos, sin):
    B, T, _ = q.shape
    dt = q.dtype
    q = apply_rope(q.reshape(B, T, C_KV_GROUPS, C_HPG, HEAD_DIM).transpose(0, 2, 3, 1, 4), cos, sin) * (HEAD_DIM ** -0.5)

    def groups(z):
        return z.reshape(B, T, C_KV_GROUPS, HEAD_DIM).transpose(0, 2, 1, 3)

    kc, vc, ks, vs, kw, vw = [groups(z) for z in (kc, vc, ks, vs, kw, vw)]
    ks = apply_rope(ks, cos, sin)
    kw = apply_rope(kw, cos, sin)
    n_cmp = (T - CMP_BLOCK) // CMP_STRIDE + 1
    cmp_end = CMP_STRIDE * np.arange(n_cmp) + CMP_BLOCK - 1
    ccos, csin = rope_tables(jnp.asarray(cmp_end, jnp.float32))
    k_cmp = apply_rope(compress_blocks(kc, pe_k, w1_k, w2_k), ccos, csin)
    v_cmp = compress_blocks(vc, pe_v, w1_v, w2_v)
    n_slc = T // SLC_BLOCK
    n_sel = min(N_SELECT, n_slc)
    sel_map = selection_map(n_cmp, n_slc)
    ks_blocks = ks.reshape(B, C_KV_GROUPS, n_slc, SLC_BLOCK, HEAD_DIM)
    vs_blocks = vs.reshape(B, C_KV_GROUPS, n_slc, SLC_BLOCK, HEAD_DIM)
    kw_pad = jnp.pad(kw, ((0, 0), (0, 0), (WINDOW, 0), (0, 0)))
    vw_pad = jnp.pad(vw, ((0, 0), (0, 0), (WINDOW, 0), (0, 0)))
    gates = jax.nn.sigmoid(gate_logits).reshape(B, T, C_KV_GROUPS, C_HPG, 3).transpose(0, 2, 3, 1, 4)
    b_idx = jnp.arange(B)[:, None, None, None]
    g_idx = jnp.arange(C_KV_GROUPS)[None, :, None, None]
    blk = jnp.arange(n_slc)
    cmp_end_j = jnp.asarray(cmp_end)

    def block(i):
        s0 = i * C_QBLOCK
        t = s0 + jnp.arange(C_QBLOCK)
        qi = lax.dynamic_slice_in_dim(q, s0, C_QBLOCK, axis=3)
        mc = cmp_end_j[None, :] <= t[:, None]
        sc = jnp.einsum('bghqd,bgnd->bghqn', qi, k_cmp).astype(jnp.float32)
        pc = jnp.where(mc, jax.nn.softmax(jnp.where(mc, sc, NEG_INF), axis=-1), 0.0)
        o_cmp = jnp.einsum('bghqn,bgne->bghqe', pc.astype(dt), v_cmp)
        imp = jnp.einsum('bghqn,nj->bgqj', pc, sel_map)
        cur = t // SLC_BLOCK
        forced = (blk[None, :] == 0) | (blk[None, :] == cur[:, None]) | (blk[None, :] == cur[:, None] - 1)
        valid = blk[None, :] * SLC_BLOCK <= t[:, None]
        score = jnp.where(valid, imp + jnp.where(forced, FORCE_BONUS, 0.0), NEG_INF)
        _, sel = lax.top_k(score, n_sel)
        kg = ks_blocks[b_idx, g_idx, sel]
        vg = vs_blocks[b_idx, g_idx, sel]
        pos = sel[..., None] * SLC_BLOCK + jnp.arange(SLC_BLOCK)
        ms = (pos <= t[:, None, None])[:, :, None]
        ss = jnp.where(ms, jnp.einsum('bghqd,bgqnkd->bghqnk', qi, kg).astype(jnp.float32), NEG_INF)
        ps = jax.nn.softmax(ss.reshape(B, C_KV_GROUPS, C_HPG, C_QBLOCK, -1), axis=-1).reshape(ss.shape)
        o_slc = jnp.einsum('bghqnk,bgqnke->bghqe', ps.astype(dt), vg)
        kwi = lax.dynamic_slice_in_dim(kw_pad, s0, C_QBLOCK + WINDOW, axis=2)
        vwi = lax.dynamic_slice_in_dim(vw_pad, s0, C_QBLOCK + WINDOW, axis=2)
        wpos = s0 - WINDOW + jnp.arange(C_QBLOCK + WINDOW)
        mw = (wpos[None, :] <= t[:, None]) & (wpos[None, :] > t[:, None] - WINDOW) & (wpos[None, :] >= 0)
        sw = jnp.einsum('bghqd,bgkd->bghqk', qi, kwi).astype(jnp.float32)
        pw = jax.nn.softmax(jnp.where(mw, sw, NEG_INF), axis=-1)
        o_win = jnp.einsum('bghqk,bgke->bghqe', pw.astype(dt), vwi)
        gi = lax.dynamic_slice_in_dim(gates, s0, C_QBLOCK, axis=3)
        return gi[..., 0:1] * o_cmp + gi[..., 1:2] * o_slc + gi[..., 2:3] * o_win

    o = lax.map(block, jnp.arange(T // C_QBLOCK))
    return o.transpose(1, 0, 4, 2, 3, 5).reshape(B, T, C_OUT)

def causal_conv(x, w, b):
    K, T = w.shape[0], x.shape[1]
    xp = jnp.pad(x, ((0, 0), (K - 1, 0), (0, 0)))
    return sum(xp[:, j:j + T] * w[j] for j in range(K)) + b

def mlstm(q, k, v, ig, fg, og, conv_w, conv_b, ig_b, fg_b, norm_w):
    B, T, _ = q.shape
    qk = jax.nn.silu(causal_conv(jnp.concatenate([q, k], axis=-1), conv_w, conv_b))
    q, k = qk[..., :D_HEADS * D_QK], qk[..., D_HEADS * D_QK:]
    nc = T // D_CHUNK

    def chunks(z, dim):
        return z.astype(jnp.float32).reshape(B, nc, D_CHUNK, D_HEADS, dim).transpose(1, 0, 3, 2, 4)

    def gate_chunks(z):
        return z.reshape(B, nc, D_CHUNK, D_HEADS).transpose(1, 0, 3, 2)

    qc = chunks(q, D_QK) * (D_QK ** -0.5)
    kc = chunks(k, D_QK)
    vc = chunks(v, D_V)
    li = gate_chunks((ig + ig_b).astype(jnp.float32))
    lf = gate_chunks(jax.nn.log_sigmoid((fg + fg_b).astype(jnp.float32)))
    causal = jnp.tril(jnp.ones((D_CHUNK, D_CHUNK), bool))

    def step(carry, inp):
        C, n, m = carry
        qs, ks, vs, lis, lfs = inp
        b = jnp.cumsum(lfs, axis=-1)
        dmat = jnp.where(causal, b[..., :, None] - b[..., None, :] + lis[..., None, :], -jnp.inf)
        m_s = jnp.maximum(b + m[..., None], jnp.max(dmat, axis=-1))
        carry_w = jnp.exp(b + m[..., None] - m_s)
        sqk = jnp.einsum('bhsd,bhrd->bhsr', qs, ks) * jnp.exp(dmat - m_s[..., None])
        num = carry_w[..., None] * jnp.einsum('bhsd,bhde->bhse', qs, C) + jnp.einsum('bhsr,bhre->bhse', sqk, vs)
        den = carry_w * jnp.einsum('bhsd,bhd->bhs', qs, n) + jnp.sum(sqk, axis=-1)
        h = num / jnp.maximum(jnp.abs(den), jnp.exp(-m_s))[..., None]
        b_last = b[..., -1]
        g = b_last[..., None] - b + lis
        m_new = jnp.maximum(b_last + m, jnp.max(g, axis=-1))
        decay_c = jnp.exp(b_last + m - m_new)
        wr = jnp.exp(g - m_new[..., None])
        C = decay_c[..., None, None] * C + jnp.einsum('bhr,bhrd,bhre->bhde', wr, ks, vs)
        n = decay_c[..., None] * n + jnp.einsum('bhr,bhrd->bhd', wr, ks)
        return (C, n, m_new), h

    init = (jnp.zeros((B, D_HEADS, D_QK, D_V), jnp.float32),
            jnp.zeros((B, D_HEADS, D_QK), jnp.float32),
            jnp.zeros((B, D_HEADS), jnp.float32))
    _, h = lax.scan(step, init, (qc, kc, vc, li, lf))
    h = h.transpose(1, 0, 3, 2, 4).reshape(B, T, D_HEADS, D_V)
    h = rmsnorm(h, norm_w.reshape(D_HEADS, D_V)).reshape(B, T, D_OUT)
    return h.astype(og.dtype) * jax.nn.sigmoid(og)

def first_inputs(seed: int = 0) -> dict:
    key = jax.random.key(seed)
    keys = iter(jax.random.split(key, 48))

    def nrm(shape, scale):
        return jax.random.normal(next(keys), shape, jnp.float32) * scale

    def gain(shape):
        return 1.0 + nrm(shape, 0.02)

    L, E, O = DEPTH, (DEPTH + 1) // 2, DEPTH // 2
    d, f = D_MODEL, D_FF
    return {
        'x': nrm((BATCH, SEQ, d), 1.0),
        'ffa_norm': gain((L, d)),
        'ffa_gate': nrm((L, d, f), d ** -0.5),
        'ffa_up': nrm((L, d, f), d ** -0.5),
        'ffa_down': nrm((L, f, d), f ** -0.5),
        'mix_norm': gain((L, d)),
        'ffb_norm': gain((L, d)),
        'ffb_gate': nrm((L, d, f), d ** -0.5),
        'ffb_up': nrm((L, d, f), d ** -0.5),
        'ffb_down': nrm((L, f, d), f ** -0.5),
        'ab_w_in': nrm((E, d, AB_COLS), d ** -0.5),
        'ab_w_out': nrm((E, A_OUT + B_DIM, d), (A_OUT + B_DIM) ** -0.5),
        'diff_lam': nrm((E, 4, HEAD_DIM), 0.1),
        'diff_subln': gain((E, A_VDIM)),
        'rwkv_mu': jax.random.uniform(next(keys), (E, B_COLS), jnp.float32),
        'rwkv_w0': jnp.linspace(-6.0, 1.0, B_DIM, dtype=jnp.float32)[None, :] + nrm((E, B_DIM), 0.1),
        'rwkv_w2': nrm((E, B_W_RANK, B_DIM), B_W_RANK ** -0.5),
        'rwkv_a0': nrm((E, B_DIM), 0.1),
        'rwkv_a2': nrm((E, B_A_RANK, B_DIM), B_A_RANK ** -0.5),
        'rwkv_g2': nrm((E, B_G_RANK, B_DIM), B_G_RANK ** -0.5),
        'rwkv_kk': 0.85 + nrm((E, B_DIM), 0.05),
        'rwkv_ka': 1.0 + nrm((E, B_DIM), 0.05),
        'rwkv_rk': nrm((E, B_HEADS, HEAD_DIM), 0.1),
        'rwkv_lnw': gain((E, B_DIM)),
        'rwkv_lnb': nrm((E, B_DIM), 0.02),
        'cd_w_in': nrm((O, d, CD_COLS), d ** -0.5),
        'cd_w_out': nrm((O, C_OUT + D_OUT, d), (C_OUT + D_OUT) ** -0.5),
        'nsa_pe_k': nrm((O, CMP_BLOCK, HEAD_DIM), 0.1),
        'nsa_w1_k': nrm((O, CMP_BLOCK * HEAD_DIM, CMP_HIDDEN), (CMP_BLOCK * HEAD_DIM) ** -0.5),
        'nsa_w2_k': nrm((O, CMP_HIDDEN, HEAD_DIM), CMP_HIDDEN ** -0.5),
        'nsa_pe_v': nrm((O, CMP_BLOCK, HEAD_DIM), 0.1),
        'nsa_w1_v': nrm((O, CMP_BLOCK * HEAD_DIM, CMP_HIDDEN), (CMP_BLOCK * HEAD_DIM) ** -0.5),
        'nsa_w2_v': nrm((O, CMP_HIDDEN, HEAD_DIM), CMP_HIDDEN ** -0.5),
        'mlstm_conv_w': nrm((O, D_CONV, 2 * D_HEADS * D_QK), 0.5),
        'mlstm_conv_b': nrm((O, 2 * D_HEADS * D_QK), 0.02),
        'mlstm_ig_b': -2.0 + nrm((O, D_HEADS), 0.1),
        'mlstm_fg_b': jnp.linspace(3.0, 6.0, D_HEADS, dtype=jnp.float32)[None, :] + nrm((O, D_HEADS), 0.1),
        'mlstm_norm': gain((O, D_OUT)),
        'final_norm': gain((d,)),
    }

def first_block(x, ffa_norm, ffa_gate, ffa_up, ffa_down, mix_norm, ffb_norm, ffb_gate, ffb_up, ffb_down,
              ab_w_in, ab_w_out, diff_lam, diff_subln,
              rwkv_mu, rwkv_w0, rwkv_w2, rwkv_a0, rwkv_a2, rwkv_g2, rwkv_kk, rwkv_ka, rwkv_rk, rwkv_lnw, rwkv_lnb,
              cd_w_in, cd_w_out, nsa_pe_k, nsa_w1_k, nsa_w2_k, nsa_pe_v, nsa_w1_v, nsa_w2_v,
              mlstm_conv_w, mlstm_conv_b, mlstm_ig_b, mlstm_fg_b, mlstm_norm, final_norm):
    T = x.shape[1]
    cos, sin = rope_tables(jnp.arange(T, dtype=jnp.float32))
    for layer in range(DEPTH):
        j = layer // 2
        x = x + 0.5 * swiglu(rmsnorm(x, ffa_norm[layer]), ffa_gate[layer], ffa_up[layer], ffa_down[layer])
        h = rmsnorm(x, mix_norm[layer])
        if layer % 2 == 0:
            p = h @ ab_w_in[j]
            qa, ka, va = split_cols(p[..., :A_COLS], A_SIZES)
            oa = diff_attention(qa, ka, va, diff_lam[j], diff_subln[j], lambda_init(layer), cos, sin)
            ob = rwkv7_time_mix(p[..., A_COLS:], rwkv_mu[j], rwkv_w0[j], rwkv_w2[j], rwkv_a0[j], rwkv_a2[j],
                                rwkv_g2[j], rwkv_kk[j], rwkv_ka[j], rwkv_rk[j], rwkv_lnw[j], rwkv_lnb[j])
            mix = jnp.concatenate([oa, ob], axis=-1) @ ab_w_out[j]
        else:
            p = h @ cd_w_in[j]
            cq, ckc, cvc, cks, cvs, ckw, cvw, cg = split_cols(p[..., :C_COLS], C_SIZES)
            dq, dk, dv, di, df, dog = split_cols(p[..., C_COLS:], D_SIZES)
            oc = native_sparse_attention(cq, ckc, cvc, cks, cvs, ckw, cvw, cg,
                                         nsa_pe_k[j], nsa_w1_k[j], nsa_w2_k[j],
                                         nsa_pe_v[j], nsa_w1_v[j], nsa_w2_v[j], cos, sin)
            od = mlstm(dq, dk, dv, di, df, dog, mlstm_conv_w[j], mlstm_conv_b[j],
                       mlstm_ig_b[j], mlstm_fg_b[j], mlstm_norm[j])
            mix = jnp.concatenate([oc, od], axis=-1) @ cd_w_out[j]
        x = x + mix
        x = x + 0.5 * swiglu(rmsnorm(x, ffb_norm[layer]), ffb_gate[layer], ffb_up[layer], ffb_down[layer])
    return rmsnorm(x, final_norm)


N_GROUPS = 4
GROUP_WIDTH = D_MODEL // N_GROUPS
D_MIX = N_GROUPS * GROUP_WIDTH
CHUNK = 64
EPS = 1e-6
MASK_VALUE = -1e30
MIN_POS = 1e-30

HA = GROUP_WIDTH // HEAD_DIM
DK_A = HEAD_DIM
DV_A = HEAD_DIM
HB = GROUP_WIDTH // HEAD_DIM
DK_B = HEAD_DIM // 2
DV_B = HEAD_DIM
GLA_GATE_RANK = 16
GLA_GATE_NORMALIZER = 16.0
HC = GROUP_WIDTH // HEAD_DIM
MLA_Q_RANK = 256
MLA_KV_RANK = 128
MLA_NOPE = 64
MLA_ROPE = 32
MLA_V = HEAD_DIM
Q_BLOCK = 128
HD = GROUP_WIDTH // HEAD_DIM
DK_D = HEAD_DIM
DV_D = HEAD_DIM
GDN_CONV = 4
FFN_CONV = 3

IN_SPLITS = (
    HA * DK_A, HA * DK_A, HA * DV_A, HA * DV_A,
    HB * DK_B, HB * DK_B, HB * DV_B, GLA_GATE_RANK, HB * DV_B,
    MLA_Q_RANK, MLA_KV_RANK, MLA_ROPE,
    HD * DK_D, HD * DK_D, HD * DV_D, HD, HD, HD * DV_D,
)
D_IN = sum(IN_SPLITS)


def rms_norm(x, g):
    xf = x.astype(jnp.float32)
    y = xf * lax.rsqrt(jnp.mean(xf * xf, axis=-1, keepdims=True) + EPS)
    return (y * g).astype(x.dtype)

def l2_norm(x):
    xf = x.astype(jnp.float32)
    return xf * lax.rsqrt(jnp.sum(xf * xf, axis=-1, keepdims=True) + EPS)

def heads(t, h, d):
    return t.reshape(t.shape[:-1] + (h, d))

def split_columns(z):
    out = []
    start = 0
    for w in IN_SPLITS:
        out.append(z[..., start:start + w])
        start += w
    return out

def causal_dwconv(x, w):
    k, c = w.shape
    return lax.conv_general_dilated(
        x, w[:, None, :].astype(x.dtype), window_strides=(1,), padding=[(k - 1, 0)],
        dimension_numbers=('NWC', 'WIO', 'NWC'), feature_group_count=c)

def rope_tables_2(s):
    inv = ROPE_THETA ** (-jnp.arange(0, MLA_ROPE, 2, dtype=jnp.float32) / MLA_ROPE)
    ang = jnp.arange(s, dtype=jnp.float32)[:, None] * inv[None, :]
    return jnp.cos(ang), jnp.sin(ang)

def apply_rope_2(x, cos, sin):
    xf = x.astype(jnp.float32)
    x1, x2 = xf[..., :MLA_ROPE // 2], xf[..., MLA_ROPE // 2:]
    return jnp.concatenate([x1 * cos - x2 * sin, x2 * cos + x1 * sin], axis=-1).astype(x.dtype)

def chunk_gla(q, k, v, log_f):
    bsz, s, h, dk = q.shape
    dv = v.shape[-1]
    n = s // CHUNK

    def to_chunks(t):
        return t.astype(jnp.float32).reshape(bsz, n, CHUNK, h, t.shape[-1]).transpose(1, 0, 3, 2, 4)

    qc, kc, vc, gc = to_chunks(q), to_chunks(k), to_chunks(v), to_chunks(log_f)
    bc = jnp.cumsum(gc, axis=3)
    causal = jnp.tril(jnp.ones((CHUNK, CHUNK), bool))[:, :, None]

    def step(state, inp):
        q_, k_, v_, b_ = inp
        diff = b_[:, :, :, None, :] - b_[:, :, None, :, :]
        decay = jnp.where(causal, jnp.exp(jnp.where(causal, diff, 0.0)), 0.0)
        attn = jnp.einsum('bhid,bhjd,bhijd->bhij', q_, k_, decay)
        b_last = b_[:, :, -1, :]
        o = (jnp.einsum('bhij,bhjv->bhiv', attn, v_)
             + jnp.einsum('bhid,bhdv->bhiv', q_ * jnp.exp(b_), state))
        state = (jnp.exp(b_last)[..., None] * state
                 + jnp.einsum('bhjd,bhjv->bhdv', k_ * jnp.exp(b_last[:, :, None, :] - b_), v_))
        return state, o

    s0 = jnp.zeros((bsz, h, dk, dv), jnp.float32)
    _, o = lax.scan(step, s0, (qc, kc, vc, bc))
    return o.transpose(1, 0, 3, 2, 4).reshape(bsz, s, h, dv)

def chunk_gated_delta(q, k, v, beta, log_g):
    bsz, s, h, dk = q.shape
    dv = v.shape[-1]
    n = s // CHUNK

    def to_chunks(t):
        t = t.astype(jnp.float32).reshape((bsz, n, CHUNK, h) + t.shape[3:])
        return jnp.moveaxis(t, (1, 3), (0, 2))

    qc, kc, vc = to_chunks(q), to_chunks(k), to_chunks(v)
    bt, gc = to_chunks(beta), to_chunks(log_g)
    b = jnp.cumsum(gc, axis=-1)
    incl = jnp.tril(jnp.ones((CHUNK, CHUNK), bool))
    strict = jnp.tril(jnp.ones((CHUNK, CHUNK), bool), -1)
    diff = b[..., :, None] - b[..., None, :]
    lmask = jnp.where(incl, jnp.exp(jnp.where(incl, diff, 0.0)), 0.0)
    kb = kc * bt[..., None]
    m = jnp.where(strict, jnp.einsum('nbhid,nbhjd->nbhij', kb, kc) * lmask, 0.0)
    eye = jnp.eye(CHUNK, dtype=jnp.float32)
    rhs = jnp.concatenate([vc * bt[..., None], kb * jnp.exp(b)[..., None]], axis=-1)
    sol = lax.linalg.triangular_solve(m + eye, rhs, left_side=True, lower=True, unit_diagonal=True)
    u, w = sol[..., :dv], sol[..., dv:]
    a_qk = jnp.einsum('nbhid,nbhjd->nbhij', qc, kc) * lmask

    def step(state, inp):
        q_, k_, u_, w_, a_, b_ = inp
        v_new = u_ - jnp.einsum('bhcd,bhdv->bhcv', w_, state)
        o = (jnp.einsum('bhcd,bhdv->bhcv', q_ * jnp.exp(b_)[..., None], state)
             + jnp.einsum('bhij,bhjv->bhiv', a_, v_new))
        b_last = b_[..., -1:]
        state = (jnp.exp(b_last)[..., None] * state
                 + jnp.einsum('bhcd,bhcv->bhdv', k_ * jnp.exp(b_last - b_)[..., None], v_new))
        return state, o

    s0 = jnp.zeros((bsz, h, dk, dv), jnp.float32)
    _, o = lax.scan(step, s0, (qc, kc, u, w, a_qk, b))
    return jnp.moveaxis(o, (0, 2), (1, 3)).reshape(bsz, s, h, dv)

def mla_attention(q_nope, q_rope, k_nope, k_rope, v):
    bsz, s, h, _ = q_nope.shape
    nb = s // Q_BLOCK
    scale = (MLA_NOPE + MLA_ROPE) ** -0.5
    key_pos = jnp.arange(s)

    def blocks(t):
        return jnp.moveaxis(t.reshape((bsz, nb, Q_BLOCK) + t.shape[2:]), 1, 0)

    def attend(args):
        qn, qr, blk = args
        sc = (jnp.einsum('bqhd,bkhd->bhqk', qn, k_nope)
              + jnp.einsum('bqhd,bkd->bhqk', qr, k_rope)).astype(jnp.float32) * scale
        q_pos = blk * Q_BLOCK + jnp.arange(Q_BLOCK)
        mask = key_pos[None, :] <= q_pos[:, None]
        p = jax.nn.softmax(jnp.where(mask, sc, MASK_VALUE), axis=-1)
        return jnp.einsum('bhqk,bkhv->bqhv', p.astype(v.dtype), v)

    o = lax.map(attend, (blocks(q_nope), blocks(q_rope), jnp.arange(nb)))
    return jnp.moveaxis(o, 0, 1).reshape(bsz, s, h, v.shape[-1])

def hgrn_lower_bounds(lb_logits):
    p = jax.nn.softmax(lb_logits.astype(jnp.float32), axis=0)
    return jnp.cumsum(p, axis=0) - p[0]

def hgrn2_mixer(q, f_logit, i, g, lb, norm_g):
    dtype = q.dtype
    zf = f_logit.astype(jnp.float32)
    f = lb + (1.0 - lb) * jax.nn.sigmoid(zf)
    log_f = jnp.log(jnp.maximum(f, MIN_POS))
    k = (1.0 - lb) * jax.nn.sigmoid(-zf)
    qh = heads(jax.nn.silu(q), HA, DK_A) * DK_A ** -0.5
    o = chunk_gla(qh, heads(k, HA, DK_A), heads(i, HA, DV_A), heads(log_f, HA, DK_A))
    o = rms_norm(o, norm_g) * jax.nn.sigmoid(heads(g, HA, DV_A).astype(jnp.float32))
    return o.reshape(o.shape[:2] + (HA * DV_A,)).astype(dtype)

def gla_mixer(q, k, v, gate_code, g, w_gk2, b_gk, norm_g):
    dtype = q.dtype
    log_gk = jax.nn.log_sigmoid((gate_code @ w_gk2 + b_gk).astype(jnp.float32)) / GLA_GATE_NORMALIZER
    o = chunk_gla(heads(q, HB, DK_B) * DK_B ** -0.5, heads(k, HB, DK_B), heads(v, HB, DV_B),
                  heads(log_gk, HB, DK_B))
    o = rms_norm(o, norm_g) * jax.nn.silu(heads(g, HB, DV_B).astype(jnp.float32))
    return o.reshape(o.shape[:2] + (HB * DV_B,)).astype(dtype)

def mla_mixer(c_q, c_kv, k_rope, q_norm_g, w_uq, kv_norm_g, w_ukv, cos, sin):
    dtype = c_q.dtype
    q = heads(rms_norm(c_q, q_norm_g) @ w_uq, HC, MLA_NOPE + MLA_ROPE)
    kv = heads(rms_norm(c_kv, kv_norm_g) @ w_ukv, HC, MLA_NOPE + MLA_V)
    q_nope = q[..., :MLA_NOPE]
    q_rope = apply_rope_2(q[..., MLA_NOPE:], cos[:, None, :], sin[:, None, :])
    k_nope, v = kv[..., :MLA_NOPE], kv[..., MLA_NOPE:]
    k_rope = apply_rope_2(k_rope, cos, sin)
    o = mla_attention(q_nope, q_rope, k_nope, k_rope, v)
    return o.reshape(o.shape[:2] + (HC * MLA_V,)).astype(dtype)

def gdn_mixer(q, k, v, beta_logit, a, z, conv_w, a_log, dt_bias, norm_g):
    dtype = q.dtype
    qkv = jax.nn.silu(causal_dwconv(jnp.concatenate([q, k, v], axis=-1), conv_w))
    qd = l2_norm(heads(qkv[..., :HD * DK_D], HD, DK_D)) * DK_D ** -0.5
    kd = l2_norm(heads(qkv[..., HD * DK_D:2 * HD * DK_D], HD, DK_D))
    vd = heads(qkv[..., 2 * HD * DK_D:], HD, DV_D)
    beta = jax.nn.sigmoid(beta_logit.astype(jnp.float32))
    log_g = -jnp.exp(a_log.astype(jnp.float32)) * jax.nn.softplus(a.astype(jnp.float32) + dt_bias)
    o = chunk_gated_delta(qd, kd, vd, beta, log_g)
    o = rms_norm(o, norm_g) * jax.nn.silu(heads(z, HD, DV_D).astype(jnp.float32))
    return o.reshape(o.shape[:2] + (HD * DV_D,)).astype(dtype)

def conv_glu_ffn(h, w_gate, w_up, conv_w, w_down):
    gate = causal_dwconv(h @ w_gate, conv_w)
    return (jax.nn.gelu(gate, approximate=True) * (h @ w_up)) @ w_down

def second_inputs(seed: int = 0) -> dict:
    key = jax.random.key(seed)
    ks = jax.random.split(key, 26)

    def nrm(k, shape, scale):
        return jax.random.normal(k, shape, jnp.float32) * scale

    def gain(k, shape):
        return 1.0 + 0.1 * jax.random.normal(k, shape, jnp.float32)

    dt = jnp.exp(jax.random.uniform(ks[19], (DEPTH, HD), jnp.float32,
                                    jnp.log(1e-3), jnp.log(1e-1)))
    return {
        'x': jax.random.normal(ks[0], (BATCH, SEQ, D_MODEL), jnp.float32),
        'w_in': nrm(ks[1], (DEPTH, D_MODEL, D_IN), D_MODEL ** -0.5),
        'w_out': nrm(ks[2], (DEPTH, D_MIX, D_MODEL), D_MIX ** -0.5),
        'pre_mix_g': gain(ks[3], (DEPTH, D_MODEL)),
        'post_mix_g': gain(ks[4], (DEPTH, D_MODEL)),
        'pre_ffn_g': gain(ks[5], (DEPTH, D_MODEL)),
        'post_ffn_g': gain(ks[6], (DEPTH, D_MODEL)),
        'hgrn_lb_logits': nrm(ks[7], (DEPTH, HA * DK_A), 1.0),
        'hgrn_norm_g': gain(ks[8], (DEPTH, DV_A)),
        'gla_w_gk2': nrm(ks[9], (DEPTH, GLA_GATE_RANK, HB * DK_B), GLA_GATE_RANK ** -0.5),
        'gla_b_gk': nrm(ks[10], (DEPTH, HB * DK_B), 0.1),
        'gla_norm_g': gain(ks[11], (DEPTH, DV_B)),
        'mla_q_norm_g': gain(ks[12], (DEPTH, MLA_Q_RANK)),
        'mla_w_uq': nrm(ks[13], (DEPTH, MLA_Q_RANK, HC * (MLA_NOPE + MLA_ROPE)), MLA_Q_RANK ** -0.5),
        'mla_kv_norm_g': gain(ks[14], (DEPTH, MLA_KV_RANK)),
        'mla_w_ukv': nrm(ks[15], (DEPTH, MLA_KV_RANK, HC * (MLA_NOPE + MLA_V)), MLA_KV_RANK ** -0.5),
        'gdn_conv_w': nrm(ks[16], (DEPTH, GDN_CONV, HD * (2 * DK_D + DV_D)), GDN_CONV ** -0.5),
        'gdn_a_log': jnp.log(jax.random.uniform(ks[17], (DEPTH, HD), jnp.float32, 1.0, 16.0)),
        'gdn_dt_bias': dt + jnp.log(-jnp.expm1(-dt)),
        'gdn_norm_g': gain(ks[18], (DEPTH, DV_D)),
        'ffn_w_gate': nrm(ks[20], (DEPTH, D_MODEL, D_FF), D_MODEL ** -0.5),
        'ffn_w_up': nrm(ks[21], (DEPTH, D_MODEL, D_FF), D_MODEL ** -0.5),
        'ffn_conv_w': nrm(ks[22], (DEPTH, FFN_CONV, D_FF), FFN_CONV ** -0.5),
        'ffn_w_down': nrm(ks[23], (DEPTH, D_FF, D_MODEL), D_FF ** -0.5),
    }

def second_block(x, w_in, w_out, pre_mix_g, post_mix_g, pre_ffn_g, post_ffn_g,
              hgrn_lb_logits, hgrn_norm_g, gla_w_gk2, gla_b_gk, gla_norm_g,
              mla_q_norm_g, mla_w_uq, mla_kv_norm_g, mla_w_ukv,
              gdn_conv_w, gdn_a_log, gdn_dt_bias, gdn_norm_g,
              ffn_w_gate, ffn_w_up, ffn_conv_w, ffn_w_down):
    s = x.shape[1]
    cos, sin = rope_tables_2(s)
    lower_bounds = hgrn_lower_bounds(hgrn_lb_logits)
    for l in range(DEPTH):
        h = rms_norm(x, pre_mix_g[l])
        z = h @ w_in[l]
        (a_q, a_f, a_i, a_g,
         b_q, b_k, b_v, b_code, b_g,
         c_q, c_kv, c_kr,
         d_q, d_k, d_v, d_beta, d_a, d_z) = split_columns(z)
        o_a = hgrn2_mixer(a_q, a_f, a_i, a_g, lower_bounds[l], hgrn_norm_g[l])
        o_b = gla_mixer(b_q, b_k, b_v, b_code, b_g, gla_w_gk2[l], gla_b_gk[l], gla_norm_g[l])
        o_c = mla_mixer(c_q, c_kv, c_kr, mla_q_norm_g[l], mla_w_uq[l], mla_kv_norm_g[l], mla_w_ukv[l], cos, sin)
        o_d = gdn_mixer(d_q, d_k, d_v, d_beta, d_a, d_z, gdn_conv_w[l], gdn_a_log[l], gdn_dt_bias[l], gdn_norm_g[l])
        mix = jnp.concatenate([o_a, o_b, o_c, o_d], axis=-1).astype(h.dtype) @ w_out[l]
        x = x + rms_norm(mix, post_mix_g[l])
        h = rms_norm(x, pre_ffn_g[l])
        y = conv_glu_ffn(h, ffn_w_gate[l], ffn_w_up[l], ffn_conv_w[l], ffn_w_down[l])
        x = x + rms_norm(y, post_ffn_g[l])
    return x


def setup_inputs(seed=0):
    out = dict(first_inputs(seed))
    for name, value in second_inputs(seed + 1).items():
        if name != "x":
            out[name + "_2"] = value
    return out


def reference(
    x, ffa_norm, ffa_gate, ffa_up, ffa_down, mix_norm, ffb_norm, ffb_gate, ffb_up, ffb_down,
    ab_w_in, ab_w_out, diff_lam, diff_subln, rwkv_mu, rwkv_w0, rwkv_w2, rwkv_a0, rwkv_a2,
    rwkv_g2, rwkv_kk, rwkv_ka, rwkv_rk, rwkv_lnw, rwkv_lnb, cd_w_in, cd_w_out, nsa_pe_k,
    nsa_w1_k, nsa_w2_k, nsa_pe_v, nsa_w1_v, nsa_w2_v, mlstm_conv_w, mlstm_conv_b, mlstm_ig_b,
    mlstm_fg_b, mlstm_norm, final_norm, w_in_2, w_out_2, pre_mix_g_2, post_mix_g_2, pre_ffn_g_2,
    post_ffn_g_2, hgrn_lb_logits_2, hgrn_norm_g_2, gla_w_gk2_2, gla_b_gk_2, gla_norm_g_2,
    mla_q_norm_g_2, mla_w_uq_2, mla_kv_norm_g_2, mla_w_ukv_2, gdn_conv_w_2, gdn_a_log_2,
    gdn_dt_bias_2, gdn_norm_g_2, ffn_w_gate_2, ffn_w_up_2, ffn_conv_w_2, ffn_w_down_2,
):
    x = first_block(
        x, ffa_norm, ffa_gate, ffa_up, ffa_down, mix_norm, ffb_norm, ffb_gate, ffb_up, ffb_down,
        ab_w_in, ab_w_out, diff_lam, diff_subln, rwkv_mu, rwkv_w0, rwkv_w2, rwkv_a0, rwkv_a2,
        rwkv_g2, rwkv_kk, rwkv_ka, rwkv_rk, rwkv_lnw, rwkv_lnb, cd_w_in, cd_w_out, nsa_pe_k,
        nsa_w1_k, nsa_w2_k, nsa_pe_v, nsa_w1_v, nsa_w2_v, mlstm_conv_w, mlstm_conv_b,
        mlstm_ig_b, mlstm_fg_b, mlstm_norm, final_norm,
    )
    return second_block(
        x, w_in_2, w_out_2, pre_mix_g_2, post_mix_g_2, pre_ffn_g_2, post_ffn_g_2,
        hgrn_lb_logits_2, hgrn_norm_g_2, gla_w_gk2_2, gla_b_gk_2, gla_norm_g_2, mla_q_norm_g_2,
        mla_w_uq_2, mla_kv_norm_g_2, mla_w_ukv_2, gdn_conv_w_2, gdn_a_log_2, gdn_dt_bias_2,
        gdn_norm_g_2, ffn_w_gate_2, ffn_w_up_2, ffn_conv_w_2, ffn_w_down_2,
    )


_drawn_inputs = setup_inputs


def setup_inputs(seed=0):
    import zlib

    import numpy as np

    out = dict(_drawn_inputs(seed))
    spreads = {}
    factors = {'rwkv_lnw': 3.95,
     'nsa_pe_k': 25.54,
     'mlstm_conv_b': 26.28,
     'mlstm_ig_b': 64.0,
     'mlstm_norm': 31.576,
     'mla_q_norm_g_2': 3.056,
     'ffb_norm': 3.367,
     'diff_subln': 3.221,
     'rwkv_lnb': 4.556,
     'mlstm_conv_w': 8.0,
     'mlstm_fg_b': 8.0,
     'nsa_pe_v': 3.671}
    for name, (base, spread) in spreads.items():
        noise = np.random.default_rng([zlib.crc32(name.encode()), seed]).standard_normal(out[name].shape)
        drawn = base * np.exp(spread * noise) if base else spread * noise
        out[name] = jnp.asarray(drawn.astype(out[name].dtype))
    for name, factor in factors.items():
        out[name] = (out[name] * factor).astype(out[name].dtype)
    return out
```

```python
from contextlib import ExitStack, contextmanager

import numpy as np

import concourse.bass as bass
from concourse import mybir

F32 = mybir.dt.float32
I32 = mybir.dt.int32
ALU = mybir.AluOpType
ACT = mybir.ActivationFunctionType
AX = mybir.AxisListType

P = 128
T = 512
D = 1024
KT = D // P
NCH = T // P
D_FF = 2816
FT = D_FF // P
EPS = 1e-6
HEAD = 64


class Core:

    def __init__(self, nc, ctx):
        self.nc = nc
        self.ctx = ctx
        self.n = 0

    def sb(self, ctx, name, shape, dt=F32):
        self.n += 1
        return ctx.enter_context(self.nc.sbuf_tensor(f"{name}_{self.n}", shape, dt))

    @contextmanager
    def stage(self, name, signals):
        nc = self.nc
        self.n += 1
        sems = [nc.alloc_semaphore(f"{s}_{name}_{self.n}") for s in signals.split()]
        with ExitStack() as ctx:
            yield ctx, nc.Block(), sems
        nc.clear_and_free_semaphores(sems)
        nc.all_engine_barrier()


def chain(eng, sem):
    count = [0]

    def link(ins):
        count[0] += 1
        ins.then_inc(sem, 1)
        eng.wait_ge(sem, count[0])
        return ins

    return link


def ffn_stage(C, name, norm, w_gate, w_up, w_down, scale, taps=None, out=None):
    nc, x, h, ps = C.nc, C.x, C.h, C.ps
    W = 256
    PER = W // P
    CH = D_FF // W
    with C.stage(name, "squares_done sum_done rstd_link rstd_done h_ready gate_loaded_0 gate_loaded_1 tile_summed conv_link conv_done silu_done act_done down_loaded_0 down_loaded_1 down_summed x_updated") as (ctx, blk, sems):
        (squares_done, sum_done, rstd_link, rstd_done, h_ready, gate_loaded_0, gate_loaded_1, tile_summed,
         conv_link, conv_done, silu_done, act_done, down_loaded_0, down_loaded_1, down_summed, x_updated) = sems
        gate_loaded = (gate_loaded_0, gate_loaded_1)
        down_loaded = (down_loaded_0, down_loaded_1)
        gate_w = C.sb(ctx, "gate_w", [P, 2, 2, KT, W])
        down_w = C.sb(ctx, "down_w", [P, 2, FT, W])
        acts = C.sb(ctx, "acts", [P, FT, T])
        silu = C.sb(ctx, "silu", [P, 2, T])
        if taps is not None:
            conv = C.sb(ctx, "conv", [P, 2, T])
        rstd = C.sb(ctx, "rstd", [P, T])
        gate_v = w_gate.rearrange("(k p) f -> p k f", p=P)
        up_v = w_up.rearrange("(k p) f -> p k f", p=P)
        down_v = w_down.rearrange("(f p) d -> p f d", p=P)
        GATE, UP, OUT, SUM = (0, 1), (2, 3), (4, 5), 6
        block = ctx.enter_context(blk)

        @block.sync
        def _(sp):

            def load(i, slot):
                p = i * 2 + slot
                sp.wait_ge(tile_summed, (p + 1) * PER)
                sp.dma_start(gate_w[:, slot, 0], gate_v[:, :, bass.ts(p, W)]).then_inc(gate_loaded[slot], 16)
                sp.dma_start(gate_w[:, slot, 1], up_v[:, :, bass.ts(p, W)]).then_inc(gate_loaded[slot], 16)

            with sp.Fori(0, CH // 2) as i:
                load(i, 0)
                load(i, 1)
            load(CH // 2, 0)
            for m in range(D // W):
                if m >= 2:
                    sp.wait_ge(down_summed, (m - 1) * PER)
                sp.dma_start(down_w[:, m % 2], down_v[:, :, m * W:(m + 1) * W]).then_inc(down_loaded[m % 2], 16)

        @block.scalar
        def _(act):
            norm_act(C, act, x, h, rstd, ps[:, SUM], squares_done, sum_done, rstd_link, rstd_done)

            def tiles(p):
                for u in range(PER):
                    act.wait_ge(tile_summed, 2 * PER + p * PER + u + 1)
                    act.wait_ge(act_done, p * PER + u + 1)
                    if taps is None:
                        nc.scalar.activation(silu[:, u], ps[:, GATE[u]], ACT.Silu).then_inc(silu_done, 1)
                    else:
                        act.wait_ge(conv_done, p * PER + u + 1)
                        nc.scalar.activation(silu[:, u], conv[:, u], ACT.Gelu_apprx_tanh).then_inc(silu_done, 1)

            with act.Fori(0, CH) as p:
                tiles(p)

        @block.tensor
        def _(pe):
            pe.sem_inc(tile_summed, 2 * PER)
            norm_pe(C, pe, h, ps[:, SUM], squares_done, sum_done)
            pe.wait_ge(h_ready, 1)

            def tiles(i, slot):
                p = i * 2 + slot
                pe.wait_ge(gate_loaded[slot], (i + 1) * 32)
                for u in range(PER):
                    pe.wait_ge(act_done, p * PER + u + 1)
                    for w, bank in ((0, GATE[u]), (1, UP[u])):
                        for k in range(KT):
                            mm = nc.tensor.matmul(ps[:, bank], gate_w[:, slot, w, k, u * P:(u + 1) * P], h[:, k], start=k == 0, stop=k == KT - 1)
                            if k == KT - 1 and w == 1:
                                mm.then_inc(tile_summed, 1)

            with pe.Fori(0, CH // 2) as i:
                tiles(i, 0)
                tiles(i, 1)
            tiles(CH // 2, 0)
            pe.wait_ge(act_done, FT + 2)
            for m in range(KT):
                pe.wait_ge(down_loaded[m // PER % 2], 16 * (m // PER // 2 + 1))
                if m >= 2:
                    pe.wait_ge(x_updated, m - 1)
                for f in range(FT):
                    mm = nc.tensor.matmul(ps[:, OUT[m % 2]], down_w[:, m // PER % 2, f, m % PER * P:(m % PER + 1) * P], acts[:, f], start=f == 0, stop=f == FT - 1)
                mm.then_inc(down_summed, 1)

        @block.vector
        def _(dve):
            norm_dve(C, dve, x, h, norm, rstd, rstd_done, h_ready)
            dve.sem_inc(act_done, 2)
            with dve.Fori(0, CH) as p:
                for u in range(PER):
                    if taps is not None:
                        tile = p * PER + u
                        y, gate = conv[:, u], ps[:, GATE[u]]
                        dve.wait_ge(tile_summed, 2 * PER + tile + 1)
                        nc.vector.tensor_scalar(y, gate, taps[:, tile, 2:3], None, ALU.mult).then_inc(conv_link, 1)
                        dve.wait_ge(conv_link, tile * 2 + 1)
                        nc.vector.scalar_tensor_tensor(y[:, 1:T], gate[:, 0:T - 1], taps[:, tile, 1:2], y[:, 1:T], ALU.mult, ALU.add).then_inc(conv_link, 1)
                        dve.wait_ge(conv_link, tile * 2 + 2)
                        nc.vector.scalar_tensor_tensor(y[:, 2:T], gate[:, 0:T - 2], taps[:, tile, 0:1], y[:, 2:T], ALU.mult, ALU.add).then_inc(conv_done, 1)
                    dve.wait_ge(silu_done, p * PER + u + 1)
                    nc.vector.tensor_tensor(acts[:, p * PER + u], silu[:, u], ps[:, UP[u]], ALU.mult).then_inc(act_done, 1)
            for m in range(KT):
                dve.wait_ge(down_summed, m + 1)
                if out is None:
                    nc.vector.scalar_tensor_tensor(x[:, m], ps[:, OUT[m % 2]], scale, x[:, m], ALU.mult, ALU.add).then_inc(x_updated, 1)
                else:
                    nc.vector.tensor_copy(out[:, m], ps[:, OUT[m % 2]]).then_inc(x_updated, 1)


def norm_act(C, act, src, sq, rstd, total, squares_done, sum_done, rstd_link, rstd_done):
    for a in range(2):
        C.nc.scalar.activation(sq[:, a * 4:a * 4 + 4], src[:, a * 4:a * 4 + 4], ACT.Square).then_inc(squares_done, 1)
    act.wait_ge(sum_done, 1)
    C.nc.scalar.activation(rstd[:, :], total, ACT.Ln, bias=C.eps, scale=1.0 / D).then_inc(rstd_link, 1)
    act.wait_ge(rstd_link, 1)
    C.nc.scalar.activation(rstd[:, :], rstd[:, :], ACT.Exp, scale=-0.5).then_inc(rstd_done, 1)


def norm_pe(C, pe, sq, total, squares_done, sum_done):
    for k in range(KT):
        pe.wait_ge(squares_done, k // 4 + 1)
        mm = C.nc.tensor.matmul(total, C.ones, sq[:, k], start=k == 0, stop=k == KT - 1)
    mm.then_inc(sum_done, 1)


def norm_dve(C, dve, src, dst, nw, rstd, rstd_done, h_ready):
    dve.wait_ge(rstd_done, 1)
    for k in range(KT):
        last = C.nc.vector.scalar_tensor_tensor(dst[:, k], src[:, k], nw[:, k:k + 1], rstd[:, :], ALU.mult, ALU.mult)
    last.then_inc(h_ready, 1)


CONSTS = {}
ROPE_THETA = 10000.0


def rotation(n, width, first):
    m = np.zeros((n, n), np.float32)
    half = width // 2
    last = n if first == 0 else first + width
    for r in range(first, last):
        if (r - first) % width < half:
            m[r + half, r] = -1.0
        else:
            m[r - half, r] = 1.0
    return m


def level(n):
    b = np.arange(P) >> n
    return ((b[None, :] % 2 == 1) & (b[:, None] == b[None, :] - 1)) * 1.0


def rope(dim, first):
    inv = np.float32(ROPE_THETA) ** (-np.arange(0, dim, 2, dtype=np.float32) / np.float32(dim))
    ang = np.arange(T, dtype=np.float32)[None, :] * inv.astype(np.float32)[:, None]
    cos, sin = np.ones((P, T), np.float32), np.zeros((P, T), np.float32)
    for r in range(first, P if first == 0 else first + dim):
        a = ang[(r - first) % (dim // 2)]
        cos[r], sin[r] = np.cos(a), np.sin(a)
    return cos, sin


def const_arrays():
    i = np.arange(P)
    parts = {"ident": np.eye(P), "ones": np.ones((P, P)),
             "causal": np.where(i[None, :] <= i[:, None], 0.0, -1e30),
             "upper": (i[:, None] <= i[None, :]) * 1.0, "strict": (i[:, None] < i[None, :]) * 1.0,
             "pairs": (i[:, None] // 64 == i[None, :] // 64) * 1.0,
             "rot": rotation(P, 64, 0), "rot_mla": rotation(P, 32, 64),
             "cos": rope(HEAD, 0)[0], "sin": rope(HEAD, 0)[1], "cos_mla": rope(32, 64)[0], "sin_mla": rope(32, 64)[1],
             "levels": np.concatenate([level(n) for n in range(7)], 1),
             "run": np.broadcast_to(np.arange(T) % P != 0, (P, T)) * 1.0,
             "ones_t": np.ones((P, T)), "select": np.concatenate([(i[:, None] == n) * np.ones((P, P)) for n in range(4)], 1),
             "select_pair": np.concatenate([(i[:, None] == 2 * m + i[None, :] // 64) * 1.0 for m in range(2)], 1),
             "cmp_valid": (i[:, None] >= 31) * 1.0,
             "cmp_mask": np.concatenate([np.where(16 * np.arange(31)[None, :] + 31 <= (i + c * P)[:, None], 0.0, -1e30) for c in range(4)], 1),
             "quads": (i[:, None] // 32 == i[None, :] // 32) * 1.0}
    at = 0
    out = []
    for k, v in parts.items():
        v = np.ascontiguousarray(v, dtype=np.float32)
        CONSTS[k] = (at, v.shape[1])
        at += v.shape[1]
        out.append(v)
    for name, value in (("eps", EPS), ("tiny", 1e-12), ("gn_eps", 64e-5), ("one", 1.0)):
        out.append(np.full((P, 1), value, np.float32))
        CONSTS[name] = (at, 1)
        at += 1
    return np.ascontiguousarray(np.concatenate(out, 1))


def setup(C, consts, x_t=None):
    nc = C.nc
    C.ps = C.ctx.enter_context(nc.psum_tensor("ps", [P, 8, T], F32))
    C.x = C.sb(C.ctx, "x", [P, KT, T])
    C.mixed = C.sb(C.ctx, "mixed", [P, KT, T])
    C.h = C.sb(C.ctx, "h", [P, KT, T])
    C.consts = C.sb(C.ctx, "consts", list(consts.shape))

    def const(name):
        a, w = CONSTS[name]
        return C.consts[:, a:a + w]

    C.const = C.table = const
    C.ones, C.ident, C.eps = const("ones"), const("ident"), const("eps")
    a = CONSTS["upper"][0]
    C.mask_pair = C.consts[:, a:a + 2 * P]
    with C.stage("setup", "consts_loaded") as (ctx, blk, (loaded,)):
        block = ctx.enter_context(blk)

        @block.sync
        def _(sp):
            sp.dma_start(C.consts[:, :], consts).then_inc(loaded, 16)
            if x_t is not None:
                sp.dma_start(C.x[:, :, :], x_t).then_inc(loaded, 16)
            sp.wait_ge(loaded, 32 if x_t is not None else 16)


def dump(C, out, src):
    with C.stage("dump", "stored") as (ctx, blk, (stored,)):
        block = ctx.enter_context(blk)

        @block.sync
        def _(sp):
            sp.dma_start(out, src[:]).then_inc(stored, 16)
            sp.wait_ge(stored, 16)


Core.setup = setup
Core.dump = dump


def norm_signals():
    return "squares_done sum_done rstd_link rstd_done h_ready"


def proj_stage(C, name, norm, w, plan):
    nc, x, h, ps = C.nc, C.x, C.h, C.ps
    W, SLOTS, BANKS, SUM = 256, 4, 4, 7
    w_v = w.rearrange("(k p) f -> p k f", p=P)
    sums = []
    last_of = []
    for n, (pieces, outs) in enumerate(plan):
        sums += [(n, *out, *(() if len(out) == 4 else (0,))) for out in outs]
        last_of.append(len(sums))
    total_pieces = [0, 0, 0, 0]
    landed = []
    for n, (pieces, _) in enumerate(plan):
        total_pieces[n % SLOTS] += 16 * len(pieces)
        landed.append(total_pieces[n % SLOTS])
    with C.stage(name, norm_signals() + " w_loaded_0 w_loaded_1 w_loaded_2 w_loaded_3 summed act_copied dve_copied") as (ctx, blk, sems):
        squares_done, sum_done, rstd_link, rstd_done, h_ready, *w_loaded, summed, act_copied, dve_copied = sems
        wt = C.sb(ctx, "w", [P, SLOTS, KT, W])
        rstd = C.sb(ctx, "rstd", [P, T])
        block = ctx.enter_context(blk)

        def source(s):
            dest, first = sums[s][3:]
            return ps[first:first + dest.shape[0], s % BANKS, 0:dest.shape[1]]

        @block.sync
        def _(sp):
            for n, (pieces, _) in enumerate(plan):
                if n >= SLOTS:
                    sp.wait_ge(summed, last_of[n - SLOTS])
                at = 0
                for col, width in pieces:
                    sp.dma_start(wt[:, n % SLOTS, :, at:at + width], w_v[:, :, col:col + width],
                                 allow_slow_non_contiguous=True).then_inc(w_loaded[n % SLOTS], 16)
                    at += width

        @block.tensor
        def _(pe):
            norm_pe(C, pe, h, ps[:, SUM], squares_done, sum_done)
            pe.wait_ge(h_ready, 1)
            for s, (n, columns, c, dest, _) in enumerate(sums):
                pe.wait_ge(w_loaded[n % SLOTS], landed[n])
                if s >= BANKS:
                    pe.wait_ge((act_copied, dve_copied)[s % 2], (s - BANKS) // 2 + 1)
                for k in range(KT):
                    weights = columns(wt[:, n % SLOTS, k])
                    if c is None:
                        mm = nc.tensor.matmul(source(s), weights, h[:, k], start=k == 0, stop=k == KT - 1)
                    else:
                        mm = nc.tensor.matmul(source(s), h[:, k, c * P:(c + 1) * P], weights, start=k == 0, stop=k == KT - 1)
                mm.then_inc(summed, 1)

        @block.scalar
        def _(act):
            norm_act(C, act, x, h, rstd, ps[:, SUM], squares_done, sum_done, rstd_link, rstd_done)
            for s in range(0, len(sums), 2):
                act.wait_ge(summed, s + 1)
                nc.scalar.activation(sums[s][3], source(s), ACT.Copy).then_inc(act_copied, 1)

        @block.vector
        def _(dve):
            norm_dve(C, dve, x, h, norm, rstd, rstd_done, h_ready)
            for s in range(1, len(sums), 2):
                dve.wait_ge(summed, s + 1)
                nc.vector.tensor_copy(sums[s][3], source(s)).then_inc(dve_copied, 1)


def cols(a, b):
    return lambda chunk: chunk[:, a:b]


def t_chunk(first, dests):
    return ([(first, P * len(dests))], [(cols(i * P, (i + 1) * P), None, d) for i, d in enumerate(dests)])


def row_chunk(first, width, dests):
    return ([(first, width)], [(cols(0, width), c, d) for c, d in enumerate(dests)])


def out_stage(C, name, w, mixed, out=None):
    nc, x, ps = C.nc, C.x, C.ps
    W, SLOTS = 256, 2
    PER = W // P
    w_v = w.rearrange("(k p) f -> p k f", p=P)
    with C.stage(name, "w_loaded_0 w_loaded_1 summed x_updated") as (ctx, blk, sems):
        w_loaded, (summed, x_updated) = sems[:2], sems[2:]
        wt = C.sb(ctx, "w", [P, SLOTS, KT, W])
        block = ctx.enter_context(blk)

        @block.sync
        def _(sp):
            for n in range(D // W):
                if n >= SLOTS:
                    sp.wait_ge(summed, (n - SLOTS + 1) * PER)
                sp.dma_start(wt[:, n % SLOTS], w_v[:, :, n * W:(n + 1) * W]).then_inc(w_loaded[n % SLOTS], 16)

        @block.tensor
        def _(pe):
            for m in range(KT):
                n = m // PER
                pe.wait_ge(w_loaded[n % SLOTS], 16 * (n // SLOTS + 1))
                if m >= 4:
                    pe.wait_ge(x_updated, m - 3)
                for k in range(KT):
                    mm = nc.tensor.matmul(ps[:, m % 4], wt[:, n % SLOTS, k, m % PER * P:(m % PER + 1) * P], mixed[:, k], start=k == 0, stop=k == KT - 1)
                mm.then_inc(summed, 1)

        @block.vector
        def _(dve):
            for m in range(KT):
                dve.wait_ge(summed, m + 1)
                if out is None:
                    nc.vector.tensor_tensor(x[:, m], ps[:, m % 4], x[:, m], ALU.add).then_inc(x_updated, 1)
                else:
                    nc.vector.tensor_copy(out[:, m], ps[:, m % 4]).then_inc(x_updated, 1)


def norm_stage(C, name, src, norm, add):
    nc, x, ps = C.nc, C.x, C.ps
    with C.stage(name, norm_signals()) as (ctx, blk, sems):
        squares_done, sum_done, rstd_link, rstd_done, h_ready = sems
        sq = C.sb(ctx, "sq", [P, KT, T])
        rstd = C.sb(ctx, "rstd", [P, T])
        block = ctx.enter_context(blk)

        @block.scalar
        def _(act):
            norm_act(C, act, src, sq, rstd, ps[:, 0], squares_done, sum_done, rstd_link, rstd_done)

        @block.tensor
        def _(pe):
            norm_pe(C, pe, sq, ps[:, 0], squares_done, sum_done)

        @block.vector
        def _(dve):
            norm_dve(C, dve, src, src if add else x, norm, rstd, rstd_done, h_ready)
            if add:
                dve.wait_ge(h_ready, 1)
                for k in range(KT):
                    nc.vector.tensor_tensor(x[:, k], x[:, k], src[:, k], ALU.add)


def rope_stage(C, name, items):
    nc, ps = C.nc, C.ps
    BANKS = 4
    with C.stage(name, "rotated products_done rope_link") as (ctx, blk, (rotated, products_done, rope_link)):
        by_cos = C.sb(ctx, "by_cos", [P, 2, T])
        by_sin = C.sb(ctx, "by_sin", [P, 2, T])
        block = ctx.enter_context(blk)

        @block.tensor
        def _(pe):
            for n, (tile, rot, cos, sin, scale) in enumerate(items):
                rows = tile.shape[0]
                if n >= BANKS:
                    pe.wait_ge(products_done, n - BANKS + 1)
                nc.tensor.matmul(ps[0:rows, n % BANKS], rot[0:rows, 0:rows], tile, start=True, stop=True).then_inc(rotated, 1)

        @block.vector
        def _(dve):
            link = chain(dve, rope_link)
            for n, (tile, rot, cos, sin, scale) in enumerate(items):
                rows = tile.shape[0]
                a, b = by_cos[0:rows, n % 2], by_sin[0:rows, n % 2]
                dve.wait_ge(rotated, n + 1)
                nc.vector.scalar_tensor_tensor(a, tile, scale, cos[0:rows], ALU.mult, ALU.mult)
                link(nc.vector.scalar_tensor_tensor(b, ps[0:rows, n % BANKS], scale, sin[0:rows], ALU.mult, ALU.mult))
                nc.vector.tensor_tensor(tile, a, b, ALU.add).then_inc(products_done, 1)


def attention_stage(C, name, groups):
    nc, ps = C.nc, C.ps
    S_BANKS, T_BANKS, O_BANKS = (0, 1, 2), (3, 4, 5), (6, 7)
    P_RING, T_RING = 4, 3
    LAG_T, LAG_V = 2, 3
    units, joins = [], []
    for g, (sums, rows, dest, ob) in enumerate(groups):
        for i in range(NCH):
            for s, (maps, values) in enumerate(sums):
                for m, (q, k, mask, keys, coef) in enumerate(maps):
                    units.append((q[:, i * P:(i + 1) * P], k[:, 0:keys(i)], mask(i), keys(i), coef and coef(i), m, len(joins)))
                joins.append((g, i, s, len(sums), len(units), keys(i), values))
    with C.stage(name, "scores_done max_link max_done exp_done prob_link prob_done transposed copied values_done out_copied") as (ctx, blk, sems):
        scores_done, max_link, max_done, exp_done, prob_link, prob_done, transposed, copied, values_done, out_copied = sems
        probs = C.sb(ctx, "probs", [P, P_RING, T])
        probs_t = C.sb(ctx, "probs_t", [P, T_RING, T])
        negmax = C.sb(ctx, "negmax", [P, len(units)])
        denom = C.sb(ctx, "denom", [P, len(units)])
        block = ctx.enter_context(blk)

        def bank(u):
            return S_BANKS[u % len(S_BANKS)]

        @block.tensor
        def _(pe):
            def scores(u):
                q, k, mask, keys, coef, m, j = units[u]
                if u >= len(S_BANKS):
                    pe.wait_ge(exp_done, u - len(S_BANKS) + 1)
                nc.tensor.matmul(ps[:, bank(u), 0:keys], q, k, start=True, stop=True).then_inc(scores_done, 1)

            def turn(j):
                g, i, s, n_sums, end, keys, values = joins[j]
                pe.wait_ge(prob_done, j + 1)
                if j >= len(T_BANKS):
                    pe.wait_ge(copied, j - len(T_BANKS) + 1)
                for b in range((keys + P - 1) // P):
                    w = min(P, keys - b * P)
                    mm = nc.tensor.transpose(ps[0:w, T_BANKS[j % len(T_BANKS)], b * P:(b + 1) * P],
                                             probs[:, (end - 1) % P_RING, b * P:b * P + w], C.ident)
                mm.then_inc(transposed, 1)

            def value(j):
                g, i, s, n_sums, end, keys, values = joins[j]
                rows, ob = groups[g][1], O_BANKS[groups[g][3] % 2]
                pe.wait_ge(copied, j + 1)
                if i == 0 and s == 0 and groups[g][3] >= 2:
                    pe.wait_ge(out_copied, groups[g][3] - 1)
                nb = (keys + P - 1) // P
                for b in range(nb):
                    w = min(P, keys - b * P)
                    mm = nc.tensor.matmul(ps[rows, ob, i * P:(i + 1) * P], values(b), probs_t[0:w, j % T_RING, b * P:(b + 1) * P],
                                          start=s == 0 and b == 0, stop=s == n_sums - 1 and b == nb - 1)
                mm.then_inc(values_done, 1)

            sent_t = sent_v = 0
            for u in range(len(units) + 8):
                if u < len(units):
                    scores(u)
                while sent_t < len(joins) and joins[sent_t][4] <= u - 1:
                    turn(sent_t)
                    sent_t += 1
                while sent_v < len(joins) and joins[sent_v][4] <= u - 2 and sent_v < sent_t:
                    value(sent_v)
                    sent_v += 1

        @block.vector
        def _(dve):
            link_max, link = chain(dve, max_link), chain(dve, prob_link)

            def largest(u):
                q, k, mask, keys, coef, m, j = units[u]
                w = mask.shape[1]
                dve.wait_ge(scores_done, u + 1)
                last = ps[:, bank(u), keys - w:keys]
                link_max(nc.vector.tensor_tensor(last, last, mask, ALU.add))
                nc.vector.tensor_reduce(negmax[:, u:u + 1], ps[:, bank(u), 0:keys], AX.X, ALU.max, negate=True).then_inc(max_done, 1)

            def probability(u):
                q, k, mask, keys, coef, m, j = units[u]
                p = probs[:, u % P_RING, 0:keys]
                d = denom[:, u:u + 1]
                dve.wait_ge(exp_done, u + 1)
                link(nc.vector.reciprocal(d, d))
                if coef is not None:
                    link(nc.vector.tensor_tensor(d, d, coef, ALU.mult))
                if m == 0:
                    ins = nc.vector.tensor_scalar(p, p, d, None, ALU.mult)
                else:
                    ins = nc.vector.scalar_tensor_tensor(p, p, d, probs[:, (u - 1) % P_RING, 0:keys], ALU.mult, ALU.add)
                if joins[j][4] == u + 1:
                    ins.then_inc(prob_done, 1)
                else:
                    link(ins)

            def copy(j):
                g, i, s, n_sums, end, keys, values = joins[j]
                w = min(P, keys)
                width = (keys + P - 1) // P * P
                dve.wait_ge(transposed, j + 1)
                if j >= T_RING:
                    dve.wait_ge(values_done, j - T_RING + 1)
                nc.vector.tensor_copy(probs_t[0:w, j % T_RING, 0:width], ps[0:w, T_BANKS[j % len(T_BANKS)], 0:width]).then_inc(copied, 1)

            sent = 0
            for u in range(len(units) + 8):
                if u < len(units):
                    largest(u)
                if 1 <= u <= len(units):
                    probability(u - 1)
                while sent < len(joins) and joins[sent][4] <= u - 1:
                    copy(sent)
                    sent += 1

        @block.scalar
        def _(act):
            def exponent(u):
                q, k, mask, keys, coef, m, j = units[u]
                act.wait_ge(max_done, u + 1)
                if j >= 2:
                    done = max([n + 1 for n, x in enumerate(joins) if x[4] <= u - P_RING + 1] + [0])
                    if done:
                        act.wait_ge(transposed, done)
                nc.scalar.activation(probs[:, u % P_RING, 0:keys], ps[:, bank(u), 0:keys], ACT.Exp, bias=negmax[:, u:u + 1],
                                     accum_out=denom[:, u:u + 1]).then_inc(exp_done, 1)

            copied_banks = 0
            ends = [n + 1 for n, x in enumerate(joins) if x[1] == NCH - 1 and x[2] == x[3] - 1 and groups[x[0]][2] is not None]
            for u in range(len(units) + 12):
                if u < len(units):
                    exponent(u)
                while copied_banks < len(ends) and (joins[ends[copied_banks] - 1][4] <= u - 5 or u >= len(units)):
                    g = joins[ends[copied_banks] - 1][0]
                    act.wait_ge(values_done, ends[copied_banks])
                    dest, ob = groups[g][2], O_BANKS[groups[g][3] % 2]
                    nc.scalar.activation(dest, ps[0:dest.shape[0], ob], ACT.Copy).then_inc(out_copied, 1)
                    copied_banks += 1


def head_norm_stage(C, name, src, dst, mat, count, eps, weights, gates, scale=1.0):
    nc, ps = C.nc, C.ps
    n = src.shape[1]
    with C.stage(name, "squared summed logged rstd_done scaled") as (ctx, blk, (squared, summed, logged, rstd_done, scaled)):
        sq = C.sb(ctx, "sq", [P, n, T])
        block = ctx.enter_context(blk)

        @block.scalar
        def _(act):
            nc.scalar.activation(sq[:, :, :], src, ACT.Square).then_inc(squared, 1)
            act.wait_ge(summed, 1)
            nc.scalar.activation(sq[:, :, :], ps[:, 0:n], ACT.Ln, bias=eps, scale=1.0 / count).then_inc(logged, 1)
            act.wait_ge(logged, 1)
            nc.scalar.activation(sq[:, :, :], sq[:, :, :], ACT.Exp, scale=-0.5).then_inc(rstd_done, 1)

        @block.tensor
        def _(pe):
            pe.wait_ge(squared, 1)
            for m in range(n):
                mm = nc.tensor.matmul(ps[:, m], mat, sq[:, m], start=True, stop=True)
            mm.then_inc(summed, 1)

        @block.vector
        def _(dve):
            dve.wait_ge(rstd_done, 1)
            for m in range(n):
                last = nc.vector.scalar_tensor_tensor(sq[:, m], src[:, m], weights[:, m:m + 1], sq[:, m], ALU.mult, ALU.mult)
            last.then_inc(scaled, 1)
            dve.wait_ge(scaled, 1)
            if gates is not None:
                nc.vector.tensor_tensor(dst, sq[:, :, :], gates, ALU.mult)
            else:
                nc.vector.tensor_scalar(dst, sq[:, :, :], scale, None, ALU.mult)


def lambda_stage(C, lam, lam_init, lam_neg):
    nc = C.nc
    with C.stage("lambda", "multiplied lam_link exped") as (ctx, blk, (multiplied, lam_link, exped)):
        prod = C.sb(ctx, "prod", [P, 2, HEAD])
        s = C.sb(ctx, "s", [P, 2])
        block = ctx.enter_context(blk)

        @block.vector
        def _(dve):
            link = chain(dve, lam_link)
            link(nc.vector.tensor_tensor(prod[:, 0], lam[:, 0], lam[:, 1], ALU.mult))
            link(nc.vector.tensor_tensor(prod[:, 1], lam[:, 2], lam[:, 3], ALU.mult))
            nc.vector.tensor_reduce(s[:, :], prod[:, :, :], AX.X, ALU.add).then_inc(multiplied, 1)
            dve.wait_ge(exped, 1)
            link(nc.vector.tensor_tensor(lam_neg, s[:, 1:2], s[:, 0:1], ALU.subtract))
            link(nc.vector.tensor_scalar(lam_neg, lam_neg, -lam_init, None, ALU.add))

        @block.scalar
        def _(act):
            act.wait_ge(multiplied, 1)
            nc.scalar.activation(s[:, :], s[:, :], ACT.Exp).then_inc(exped, 1)


def diff_attention(C, ctx, qt, kt, v, lam, subln, mixed):
    lam_neg = C.sb(ctx, "lam_neg", [P, 1])
    lambda_stage(C, lam, 0.2, lam_neg[:, :])
    cos, sin, rot = C.const("cos"), C.const("sin"), C.const("rot")
    items = [(qt[:, n], rot, cos, sin, HEAD ** -0.5) for n in range(4)] + [(kt[:, n], rot, cos, sin, 1.0) for n in range(4)]
    rope_stage(C, "diff_rope", items)
    groups = []
    for hd in range(4):
        maps = [(qt[c * 64:c * 64 + 64, hd], kt[c * 64:c * 64 + 64, hd], lambda i: C.const("causal"), lambda i: (i + 1) * P,
                 (lambda i: lam_neg[:, 0:1]) if c else None) for c in range(2)]
        groups.append(([(maps, lambda j, hd=hd: v[:, j, hd * P:(hd + 1) * P])], slice(0, P), mixed[:, hd], hd))
    attention_stage(C, "diff_attn", groups)
    head_norm_stage(C, "diff_norm", mixed[:, 0:4], mixed[:, 0:4], C.ones, P, C.eps, subln, None, 0.8)


def load(C, pairs):
    with C.stage("load", "loaded") as (ctx, blk, (loaded,)):
        block = ctx.enter_context(blk)

        @block.sync
        def _(sp):
            for dst, src in pairs:
                sp.dma_start(dst[:], src).then_inc(loaded, 16)
            sp.wait_ge(loaded, 16 * len(pairs))


Core.load = load


LEVELS = 7


def inverse_signals():
    return "level_masked y_summed y_copied x_summed xt_summed x_updated xt_updated start_turned"


class Inverse:

    def __init__(self, C, heads, sems, xt, x, y, masked):
        self.C, self.H, self.G = C, heads, heads // 4
        (self.level_masked, self.y_summed, self.y_copied, self.x_summed, self.xt_summed, self.x_updated,
         self.xt_updated, self.start_turned) = sems
        self.xts, self.x, self.y, self.masked = xt, x, y, masked

    def xt(self, c):
        return self.xts[c % len(self.xts)]

    def bank(self, which, g):
        a = which * self.G + g
        return self.C.ps[:, a].rearrange("p (h i) -> p h i", h=4)

    def level(self, n):
        return self.C.const("levels")[:, n * P:(n + 1) * P].unsqueeze(1).to_broadcast([P, self.H, P])

    def pool(self, eng, c, mt, ready, ready_value):
        eng.wait_ge(ready, ready_value)
        for n in range(1, LEVELS):
            done = (c * (LEVELS - 1) + n - 2) * self.G
            if done > 0:
                eng.wait_ge(self.y_summed, done)
            self.C.nc.gpsimd.tensor_tensor(self.masked[:, n % 2], mt, self.level(n), ALU.mult).then_inc(self.level_masked, 1)

    def dve_start(self, dve, link, c, mt):
        ident = self.C.ident.unsqueeze(1).to_broadcast([P, self.H, P])
        link(self.C.nc.vector.tensor_tensor(self.xt(c), mt, self.level(0), ALU.mult))
        self.C.nc.vector.tensor_tensor(self.xt(c), ident, self.xt(c), ALU.subtract).then_inc(self.xt_updated, 1)

    def pe(self, pe, c):
        nc = self.C.nc
        L = LEVELS - 1
        upd_xt = c * (L * self.G + 1) + 1
        pe.wait_ge(self.xt_updated, upd_xt)
        for g in range(self.G):
            for q in range(4):
                mm = nc.tensor.transpose(self.bank(1, g)[:, q], self.xt(c)[:, 4 * g + q], self.C.ident)
            mm.then_inc(self.start_turned, 1)
        for n in range(L):
            unit = (c * L + n) * self.G
            pe.wait_ge(self.level_masked, c * L + n + 1)
            for g in range(self.G):
                pe.wait_ge(self.x_updated, c * L * self.G + n * self.G + g + 1)
                for q in range(4):
                    h = 4 * g + q
                    mm = nc.tensor.matmul(self.bank(0, g)[:, q], self.masked[:, (n + 1) % 2, h], self.x[:, h], start=True, stop=True)
                mm.then_inc(self.y_summed, 1)
            for g in range(self.G):
                pe.wait_ge(self.y_copied, unit + g + 1)
                if n > 0:
                    pe.wait_ge(self.xt_updated, upd_xt + (n - 1) * self.G + g + 1)
                if n < L - 1:
                    for q in range(4):
                        h = 4 * g + q
                        mm = nc.tensor.matmul(self.bank(1, g)[:, q], self.xt(c)[:, h], self.y[:, h], start=True, stop=True)
                    mm.then_inc(self.x_summed, 1)
                for q in range(4):
                    h = 4 * g + q
                    mm = nc.tensor.matmul(self.bank(2, g)[:, q], self.y[:, h], self.xt(c)[:, h], start=True, stop=True)
                mm.then_inc(self.xt_summed, 1)

    def act(self, act, c):
        for n in range(LEVELS - 1):
            for g in range(self.G):
                unit = (c * (LEVELS - 1) + n) * self.G + g
                act.wait_ge(self.y_summed, unit + 1)
                self.C.nc.scalar.activation(self.y[:, 4 * g:4 * g + 4], self.bank(0, g), ACT.Copy).then_inc(self.y_copied, 1)

    def dve(self, dve, c):
        nc = self.C.nc
        L = LEVELS - 1
        for g in range(self.G):
            dve.wait_ge(self.start_turned, c * self.G + g + 1)
            nc.vector.tensor_copy(self.x[:, 4 * g:4 * g + 4], self.bank(1, g)).then_inc(self.x_updated, 1)
        for n in range(L):
            for g in range(self.G):
                hs = slice(4 * g, 4 * g + 4)
                if n < L - 1:
                    dve.wait_ge(self.x_summed, (c * (L - 1) + n) * self.G + g + 1)
                    nc.vector.tensor_tensor(self.x[:, hs], self.x[:, hs], self.bank(1, g), ALU.subtract).then_inc(self.x_updated, 1)
                dve.wait_ge(self.xt_summed, (c * L + n) * self.G + g + 1)
                nc.vector.tensor_tensor(self.xt(c)[:, hs], self.xt(c)[:, hs], self.bank(2, g), ALU.subtract).then_inc(self.xt_updated, 1)


DECAY_SCALE = -float(np.exp(-0.5))


def rwkv(C, ctx, pt, vec, w2, a2, g2, mixed):
    nc, ps = C.nc, C.ps
    ones_t = C.const("run")
    sig, a, g, e = (C.sb(ctx, n, [P, 4, T]) for n in ("sig", "a", "g", "e"))
    rq = C.sb(ctx, "rq", [P, 4, 2, T])
    cs = C.sb(ctx, "cs", [P, 4, T])
    oka = C.sb(ctx, "oka", [P, 4])
    eref = C.sb(ctx, "eref", [P, 4, NCH])
    factor = C.sb(ctx, "factor", [P, 4, NCH - 1])
    r_t, k_t, v_t = pt[:, 0:4], pt[:, 4:8], pt[:, 8:12]
    mu, w0, a0, kkw, kaw, rkw, lnw, lnb = (vec[n] for n in ("mu", "w0", "a0", "kk", "ka", "rk", "lnw", "lnb"))

    def col(v, n):
        return v[:, n:n + 1]

    def wide(v):
        return v.unsqueeze(2).to_broadcast([P, 4, T])

    with C.stage("rwkv_mix", "shift_link mixed_in code_done code_summed a_copied g_summed prep_link kk_squared kk_summed kk_logged kk_rstd bonus_in "
                 "bonus_summed d_done exp_done") as (sctx, blk, sems):
        (shift_link, mixed_in, code_done, code_summed, a_copied, g_summed, prep_link, kk_squared, kk_summed, kk_logged, kk_rstd, bonus_in,
         bonus_summed, d_done, exp_done) = sems
        d = C.h
        block = sctx.enter_context(blk)

        @block.vector
        def _(dve):
            link = chain(dve, shift_link)
            for lo, hi in ((12, 14), (0, 8), (8, 12)):
                n = hi - lo
                nc.vector.tensor_tensor(d[:, 0:n, 1:T], pt[:, lo:hi, 0:T - 1], pt[:, lo:hi, 1:T], ALU.subtract)
                link(nc.vector.tensor_scalar(d[:, 0:n, 0:1], pt[:, lo:hi, 0:1], -1.0, None, ALU.mult))
                for m in range(n):
                    ins = nc.vector.scalar_tensor_tensor(pt[:, lo + m], d[:, m], col(mu, lo + m), pt[:, lo + m], ALU.mult, ALU.add)
                if lo == 12:
                    ins.then_inc(mixed_in, 1)
                    dve.wait_ge(mixed_in, 1)
                else:
                    link(ins)
            link2 = chain(dve, prep_link)
            for m in range(4):
                last = nc.vector.tensor_scalar(rq[:, m, 1], k_t[:, m], col(kkw, m), None, ALU.mult)
            link2(last)
            nc.vector.tensor_tensor(e[:, :, :], rq[:, :, 1], rq[:, :, 1], ALU.mult).then_inc(kk_squared, 1)
            link2(nc.vector.tensor_scalar(oka[:, :], kaw, -1.0, 1.0, ALU.mult, ALU.add))
            dve.wait_ge(a_copied, 2)
            for m in range(4):
                last = nc.vector.tensor_scalar(d[:, m], a[:, m], col(kaw, m), col(oka, m), ALU.mult, ALU.add)
            link2(last)
            link2(nc.vector.tensor_tensor(k_t, k_t, d[:, 0:4], ALU.mult))
            for m in range(4):
                last = nc.vector.scalar_tensor_tensor(d[:, 4 + m], r_t[:, m], col(rkw, m), k_t[:, m], ALU.mult, ALU.mult)
            last.then_inc(bonus_in, 1)
            for m in range(4):
                last = nc.vector.tensor_tensor_scan(cs[:, m], ones_t, sig[:, m], 0.0, ALU.mult, ALU.add)
            dve.wait_ge(kk_rstd, 1)
            link2(nc.vector.tensor_tensor(rq[:, :, 1], rq[:, :, 1], e[:, :, :], ALU.mult))
            link2(nc.vector.tensor_tensor(a[:, :, :], a[:, :, :], rq[:, :, 1], ALU.mult))
            for m in range(4):
                csm = cs[:, m].rearrange("p (c t) -> p c t", c=NCH)
                mid = csm[:, :, P // 2 - 1:P // 2].to_broadcast([P, NCH, P])
                last = nc.vector.tensor_tensor(d[:, m].rearrange("p (c t) -> p c t", c=NCH), csm, mid, ALU.subtract)
            link2(last)
            nc.vector.tensor_tensor(sig[:, :, :], d[:, 0:4], sig[:, :, :], ALU.subtract).then_inc(d_done, 1)
            dve.wait_ge(exp_done, 1)
            nc.vector.tensor_tensor(rq[:, :, 0], r_t, e[:, :, :], ALU.mult)
            dve.wait_ge(exp_done, 2)
            nc.vector.tensor_tensor(rq[:, :, 1], rq[:, :, 1], sig[:, :, :], ALU.mult)
            dve.wait_ge(exp_done, 3)
            nc.vector.tensor_tensor(k_t, k_t, d[:, 0:4], ALU.mult)
            nc.vector.tensor_tensor(a[:, :, :], a[:, :, :], d[:, 0:4], ALU.mult)
            dve.wait_ge(exp_done, 4)
            nc.vector.tensor_tensor(factor[:, :, :], eref[:, :, 1:NCH], e[:, :, P - 1:T - P:P], ALU.mult)

        @block.scalar
        def _(act):
            act.wait_ge(mixed_in, 1)
            nc.scalar.activation(pt[0:64, 12], pt[0:64, 12], ACT.Tanh).then_inc(code_done, 1)
            nc.scalar.activation(pt[:, 13], pt[:, 13], ACT.Sigmoid).then_inc(code_done, 1)
            for m in range(4):
                act.wait_ge(code_summed, 2 * m + 1)
                nc.scalar.activation(sig[:, m], ps[:, m], ACT.Sigmoid, bias=col(w0, m))
                act.wait_ge(code_summed, 2 * m + 2)
                last = nc.scalar.activation(a[:, m], ps[:, 4 + m], ACT.Sigmoid, bias=col(a0, m))
                if m == 1 or m == 3:
                    last.then_inc(a_copied, 1)
            act.wait_ge(g_summed, 1)
            nc.scalar.activation(g[:, :, :], ps[:, 0:4], ACT.Copy).then_inc(a_copied, 1)
            act.wait_ge(kk_summed, 1)
            nc.scalar.activation(e[:, :, :], ps[:, 4:8], ACT.Ln, bias=C.const("tiny")).then_inc(kk_logged, 1)
            act.wait_ge(kk_logged, 1)
            nc.scalar.activation(e[:, :, :], e[:, :, :], ACT.Exp, scale=-0.5).then_inc(kk_rstd, 1)
            act.wait_ge(d_done, 1)
            nc.scalar.activation(e[:, :, :], d[:, 0:4], ACT.Exp, scale=DECAY_SCALE).then_inc(exp_done, 1)
            nc.scalar.activation(sig[:, :, :], sig[:, :, :], ACT.Exp, scale=DECAY_SCALE).then_inc(exp_done, 1)
            nc.scalar.activation(d[:, 0:4], d[:, 0:4], ACT.Exp, scale=-DECAY_SCALE).then_inc(exp_done, 1)
            nc.scalar.activation(eref[:, :, :], cs[:, :, P // 2 - 1:T:P], ACT.Exp, scale=DECAY_SCALE).then_inc(exp_done, 1)

        @block.tensor
        def _(pe):
            pe.wait_ge(code_done, 2)
            for m in range(4):
                nc.tensor.matmul(ps[:, m], w2[0:64, m * P:(m + 1) * P], pt[0:64, 12], start=True, stop=True).then_inc(code_summed, 1)
                nc.tensor.matmul(ps[:, 4 + m], a2[64:P, m * P:(m + 1) * P], pt[64:P, 12], start=True, stop=True).then_inc(code_summed, 1)
            pe.wait_ge(a_copied, 2)
            for m in range(4):
                mm = nc.tensor.matmul(ps[:, m], g2[:, m * P:(m + 1) * P], pt[:, 13], start=True, stop=True)
            mm.then_inc(g_summed, 1)
            pe.wait_ge(kk_squared, 1)
            for m in range(4):
                mm = nc.tensor.matmul(ps[:, 4 + m], C.const("pairs"), e[:, m], start=True, stop=True)
            mm.then_inc(kk_summed, 1)
            pe.wait_ge(a_copied, 3)
            pe.wait_ge(bonus_in, 1)
            for m in range(4):
                mm = nc.tensor.matmul(ps[:, m], C.const("pairs"), d[:, 4 + m], start=True, stop=True)
            mm.then_inc(bonus_summed, 1)

    vrow, krow, prow = C.h[:, 0:4], C.h[:, 4:8], e[:, :, :]
    with C.stage("rwkv_turn", "turned turn_copied v_link") as (sctx, blk, (turned, turn_copied, v_link)):
        block = sctx.enter_context(blk)
        jobs = [(src, dst, c) for src, dst in ((v_t, vrow), (k_t, krow), (a, prow)) for c in range(NCH)]

        @block.tensor
        def _(pe):
            for n, (src, dst, c) in enumerate(jobs):
                if n >= 4:
                    pe.wait_ge(turn_copied, n - 3)
                for m in range(4):
                    mm = nc.tensor.transpose(ps[:, 4 + n % 4, m * P:(m + 1) * P], src[:, m, c * P:(c + 1) * P], C.ident)
                mm.then_inc(turned, 1)

        @block.scalar
        def _(act):
            for n, (src, dst, c) in enumerate(jobs):
                act.wait_ge(turned, n + 1)
                nc.scalar.activation(dst[:, c], ps[:, 4 + n % 4], ACT.Copy).then_inc(turn_copied, 1)

        @block.vector
        def _(dve):
            dve.wait_ge(turned, NCH)
            nc.vector.tensor_tensor(v_t, ps[:, 0:4], v_t, ALU.mult).then_inc(v_link, 1)

    y_t = mixed[:, 4:8]
    H = 8
    with C.stage("rwkv_scan", inverse_signals() + " mats_summed mats_ready mats_link rhs_summed rhs_copied u_summed u_copied y_done y_out state_summed state_link state_ready") as (sctx, blk, sems):
        inv_sems, (mats_summed, mats_ready, mats_link, rhs_summed, rhs_copied, u_summed, u_copied, y_done, y_out, state_summed, state_link, state_ready) = sems[:8], sems[8:]
        free = sig[:, :, :].rearrange("p a (h i) -> p (a h) i", i=P)
        inv = Inverse(C, H, inv_sems, [free[:, 0:H]], free[:, H:2 * H], C.sb(sctx, "y", [P, H, P]),
                      cs[:, :, :].rearrange("p (a b) (h i) -> p a (b h) i", a=2, i=P))
        at = C.sb(sctx, "at", [P, H, 4, P])
        rhs = C.sb(sctx, "rhs", [P, 2, H // 2, HEAD])
        un = C.sb(sctx, "un", [P, H, HEAD])
        z = C.sb(sctx, "z", [P, 4, HEAD])
        block = sctx.enter_context(blk)
        RHS, U, Y, S = (6, 7), 2, 0, 1
        both = C.mask_pair.unsqueeze(1).to_broadcast([P, 2, 2 * P])

        def rows(h):
            return slice(64 * (h % 2), 64 * (h % 2) + 64)

        @block.tensor
        def _(pe):
            for c in range(NCH):
                ts = slice(c * P, (c + 1) * P)
                for h in range(H):
                    if c:
                        pe.wait_ge(state_ready, c)
                        pe.wait_ge(y_out, c)
                    nc.tensor.matmul(ps[:, h, 0:2 * P], k_t[rows(h), h // 2, ts], rq[rows(h), h // 2, :, ts], start=True, stop=True)
                    nc.tensor.matmul(ps[:, h, 2 * P:4 * P], a[rows(h), h // 2, ts], rq[rows(h), h // 2, :, ts], start=True, stop=True).then_inc(mats_summed, 1)
                pe.wait_ge(mats_ready, (c + 1) * H)
                inv.pe(pe, c)
                for h in range(H):
                    hs = slice(h * HEAD, (h + 1) * HEAD)
                    out = ps[:, RHS[h % 2], h // 2 * HEAD:(h // 2 + 1) * HEAD]
                    mm = nc.tensor.matmul(out, at[:, h, 1], vrow[:, c, hs], start=True, stop=c == 0)
                    if c:
                        mm = nc.tensor.matmul(out, rq[rows(h), h // 2, 1, ts], z[rows(h), h // 2], start=False, stop=True)
                mm.then_inc(rhs_summed, 1)
                pe.wait_ge(rhs_copied, c + 1)
                pe.wait_ge(inv.xt_updated, (c + 1) * ((LEVELS - 1) * inv.G + 1))
                for h in range(H):
                    mm = nc.tensor.matmul(ps[:, U, h * HEAD:(h + 1) * HEAD], inv.xt(c)[:, h], rhs[:, h % 2, h // 2], start=True, stop=True)
                mm.then_inc(u_summed, 1)
                pe.wait_ge(u_copied, c + 1)
                for h in range(H):
                    hs = slice(h * HEAD, (h + 1) * HEAD)
                    out = ps[rows(h), S, h // 2 * HEAD:(h // 2 + 1) * HEAD]
                    nc.tensor.matmul(out, krow[:, c, hs], vrow[:, c, hs], start=True, stop=False)
                    mm = nc.tensor.matmul(out, prow[:, c, hs], un[:, h], start=False, stop=True)
                mm.then_inc(state_summed, 1)
                for h in range(H):
                    hs = slice(h * HEAD, (h + 1) * HEAD)
                    out = ps[rows(h), Y, h // 2 * P:(h // 2 + 1) * P]
                    nc.tensor.matmul(out, vrow[:, c, hs], at[:, h, 0], start=True, stop=False)
                    if c:
                        nc.tensor.matmul(out, z[rows(h), h // 2], rq[rows(h), h // 2, 0, ts], start=False, stop=False)
                    mm = nc.tensor.matmul(out, un[:, h], at[:, h, 2], start=False, stop=True)
                mm.then_inc(y_done, 1)

        @block.vector
        def _(dve):
            link, link_m = chain(dve, state_link), chain(dve, mats_link)
            for c in range(NCH):
                for h in range(H):
                    dve.wait_ge(mats_summed, c * H + h + 1)
                    nc.vector.tensor_tensor(at[:, h].rearrange("p (a b) i -> p a (b i)", a=2), ps[:, h].rearrange("p (a b) -> p a b", a=2), both, ALU.mult).then_inc(mats_ready, 1)
                dve.wait_ge(mats_ready, (c + 1) * H)
                inv.dve_start(dve, link_m, c, at[:, :, 3])
                inv.dve(dve, c)
                dve.wait_ge(u_summed, c + 1)
                nc.vector.tensor_scalar(un[:, :, :], ps[:, U].rearrange("p (h v) -> p h v", h=H), -1.0, None, ALU.mult).then_inc(u_copied, 1)
                if c == NCH - 1:
                    break
                dve.wait_ge(state_summed, c + 1)
                dve.wait_ge(y_done, c + 1)
                src = ps[:, S, 0:4 * HEAD].rearrange("p (m v) -> p m v", m=4)
                f = factor[:, :, c:c + 1].to_broadcast([P, 4, HEAD])
                if c == 0:
                    nc.vector.tensor_tensor(z[:, :, :], src, f, ALU.mult).then_inc(state_ready, 1)
                else:
                    link(nc.vector.tensor_tensor(z[:, :, :], src, z[:, :, :], ALU.add))
                    nc.vector.tensor_tensor(z[:, :, :], z[:, :, :], f, ALU.mult).then_inc(state_ready, 1)

        @block.gpsimd
        def _(pool):
            for c in range(NCH):
                inv.pool(pool, c, at[:, :, 3], mats_ready, (c + 1) * H)

        @block.scalar
        def _(act):
            for c in range(NCH):
                inv.act(act, c)
                act.wait_ge(rhs_summed, c + 1)
                nc.scalar.activation(rhs[:, :, :, :], ps[:, 6:8, 0:H // 2 * HEAD].rearrange("p a (h v) -> p a h v", v=HEAD), ACT.Copy).then_inc(rhs_copied, 1)
                act.wait_ge(y_done, c + 1)
                nc.scalar.activation(y_t[:, :, c * P:(c + 1) * P], ps[:, Y].rearrange("p (m i) -> p m i", m=4), ACT.Copy).then_inc(y_out, 1)

    with C.stage("rwkv_norm", "mean_summed centred squared var_summed logged rstd_done norm_link") as (sctx, blk, sems):
        mean_summed, centred, squared, var_summed, logged, rstd_done, norm_link = sems
        block = sctx.enter_context(blk)

        @block.tensor
        def _(pe):
            for m in range(4):
                mm = nc.tensor.matmul(ps[:, m], C.const("pairs"), y_t[:, m], start=True, stop=True)
            mm.then_inc(mean_summed, 1)
            pe.wait_ge(squared, 1)
            for m in range(4):
                mm = nc.tensor.matmul(ps[:, 4 + m], C.const("pairs"), e[:, m], start=True, stop=True)
            mm.then_inc(var_summed, 1)

        @block.vector
        def _(dve):
            link = chain(dve, norm_link)
            dve.wait_ge(mean_summed, 1)
            for m in range(4):
                last = nc.vector.scalar_tensor_tensor(y_t[:, m], ps[:, m], -1.0 / HEAD, y_t[:, m], ALU.mult, ALU.add)
            last.then_inc(centred, 1)
            dve.wait_ge(rstd_done, 1)
            for m in range(4):
                last = nc.vector.scalar_tensor_tensor(y_t[:, m], y_t[:, m], col(lnw, m), e[:, m], ALU.mult, ALU.mult)
            link(last)
            for m in range(4):
                last = nc.vector.scalar_tensor_tensor(y_t[:, m], y_t[:, m], col(lnb, m), v_t[:, m], ALU.add, ALU.add)
            link(last)
            nc.vector.tensor_tensor(mixed[:, 4:8], y_t[:, :, :], g[:, :, :], ALU.mult)

        @block.scalar
        def _(act):
            act.wait_ge(centred, 1)
            nc.scalar.activation(e[:, :, :], y_t[:, :, :], ACT.Square).then_inc(squared, 1)
            act.wait_ge(var_summed, 1)
            nc.scalar.activation(e[:, :, :], ps[:, 4:8], ACT.Ln, bias=C.const("gn_eps"), scale=1.0 / HEAD).then_inc(logged, 1)
            act.wait_ge(logged, 1)
            nc.scalar.activation(e[:, :, :], e[:, :, :], ACT.Exp, scale=-0.5).then_inc(rstd_done, 1)


def conv_stage(C, name, items, act_func=ACT.Silu):
    nc = C.nc
    with C.stage(name, "conv_link conv_done activated") as (ctx, blk, (conv_link, conv_done, activated)):
        acc = C.sb(ctx, "acc", [P, 2, T])
        block = ctx.enter_context(blk)

        @block.vector
        def _(dve):
            link = chain(dve, conv_link)
            for n, (src, dst, taps, bias) in enumerate(items):
                y = acc[:, n % 2]
                if n >= 2:
                    dve.wait_ge(activated, n - 1)
                if bias is None:
                    link(nc.vector.tensor_scalar(y, src, taps[-1], None, ALU.mult))
                else:
                    link(nc.vector.tensor_scalar(y, src, taps[-1], bias, ALU.mult, ALU.add))
                for d in range(1, len(taps)):
                    ins = nc.vector.scalar_tensor_tensor(y[:, d:T], src[:, 0:T - d], taps[-1 - d], y[:, d:T], ALU.mult, ALU.add)
                    if d < len(taps) - 1:
                        link(ins)
                ins.then_inc(conv_done, 1)

        @block.scalar
        def _(act):
            for n, (src, dst, taps, bias) in enumerate(items):
                act.wait_ge(conv_done, n + 1)
                nc.scalar.activation(dst, acc[:, n % 2], act_func).then_inc(activated, 1)


N_CMP = (T - 32) // 16 + 1


def sparse_attention(C, ctx, qt, kc, vc, ks, vs, kw, vw, gates, weights, mixed):
    nc, ps = C.nc, C.ps
    NB = 2 * N_CMP
    k_cmp = C.sb(ctx, "k_cmp", [P, N_CMP])
    v_cmp = C.sb(ctx, "v_cmp", [P, 2 * HEAD])
    with C.stage("compress", "w1_loaded_k w1_loaded_v w2_loaded stacked_k stacked_v hidden_summed hidden_done cmp_summed cmp_copied gates_done gate_link rotated rope_link") as (sctx, blk, sems):
        w1_loaded_k, w1_loaded_v, w2_loaded, stacked_k, stacked_v, hidden_summed, hidden_done, cmp_summed, cmp_copied, gates_done, gate_link, rotated, rope_link = sems
        w1 = C.sb(sctx, "w1", [P, 2, 16, 256])
        w2 = C.sb(sctx, "w2", [P, 2, 2, HEAD])
        stack = C.sb(sctx, "stack", [P, 2, 16, 2, N_CMP])
        hidden = C.sb(sctx, "hidden", [P, 2, 2, NB])
        turn = C.sb(sctx, "turn", [P, 2, N_CMP])
        block = sctx.enter_context(blk)

        @block.sync
        def _(sp):
            for n, loaded in enumerate((w1_loaded_k, w1_loaded_v)):
                sp.dma_start(w1[:, n], weights[n][0].rearrange("(a p) f -> p a f", p=P)).then_inc(loaded, 16)
                sp.dma_start(w2[:, n], weights[n][1].rearrange("(a p) f -> p a f", p=P)).then_inc(w2_loaded, 16)

        @block.vector
        def _(dve):
            for n, (z, done) in enumerate(((kc, stacked_k), (vc, stacked_v))):
                for g in range(2):
                    for odd in range(2):
                        rows = slice(64 * g, 64 * g + 64)
                        for a in range(0, 16, 8):
                            view = z[rows, 2 * a:2 * a + 16 * N_CMP].rearrange("p (n a o) -> p a o n", a=8, o=2)[:, :, odd]
                            steps = weights[n][2][rows, odd, a:a + 8].unsqueeze(2).to_broadcast([64, 8, N_CMP])
                            nc.vector.tensor_tensor(stack[64 * odd:64 * odd + 64, n, a:a + 8, g], view, steps, ALU.add).then_inc(done, 1)
            dve.wait_ge(cmp_copied, 1)
            dve.wait_ge(rotated, 1)
            link = chain(dve, rope_link)
            at = slice(31, T, 16)
            nc.vector.tensor_tensor(turn[:, 0], k_cmp[:, :], C.table("cos")[:, at], ALU.mult)
            link(nc.vector.tensor_tensor(turn[:, 1], ps[:, 5, 0:N_CMP], C.table("sin")[:, at], ALU.mult))
            link(nc.vector.tensor_tensor(k_cmp[:, :], turn[:, 0], turn[:, 1], ALU.add))
            dve.wait_ge(gates_done, 1)
            link(nc.vector.tensor_scalar(gates[:, 0, 0:24:3], gates[:, 0, 0:24:3], C.const("cmp_valid"), None, ALU.mult))

        @block.tensor
        def _(pe):
            for n, (loaded, stacked) in enumerate(((w1_loaded_k, stacked_k), (w1_loaded_v, stacked_v))):
                pe.wait_ge(loaded, 16)
                pe.wait_ge(stacked, 8)
                for t in range(2):
                    for a in range(16):
                        mm = nc.tensor.matmul(ps[:, 2 * n + t, 0:NB], w1[:, n, a, t * P:(t + 1) * P],
                                              stack[:, n, a].rearrange("p g n -> p (g n)"), start=a == 0, stop=a == 15)
                mm.then_inc(hidden_summed, 1)
            pe.wait_ge(w2_loaded, 32)
            pe.wait_ge(hidden_done, 1)
            for g in range(2):
                for t in range(2):
                    mm = nc.tensor.matmul(ps[64 * g:64 * g + 64, 4, 0:N_CMP], w2[:, 0, t], hidden[:, 0, t, g * N_CMP:(g + 1) * N_CMP], start=t == 0, stop=t == 1)
            mm.then_inc(cmp_summed, 1)
            pe.wait_ge(cmp_copied, 1)
            nc.tensor.matmul(ps[:, 5, 0:N_CMP], C.const("rot"), k_cmp[:, :], start=True, stop=True).then_inc(rotated, 1)
            pe.wait_ge(hidden_done, 2)
            for g in range(2):
                for t in range(2):
                    mm = nc.tensor.matmul(ps[0:N_CMP, 6, g * HEAD:(g + 1) * HEAD], hidden[:, 1, t, g * N_CMP:(g + 1) * N_CMP], w2[:, 1, t], start=t == 0, stop=t == 1)
            mm.then_inc(cmp_summed, 1)

        @block.scalar
        def _(act):
            nc.scalar.activation(gates[:, :, :], gates[:, :, :], ACT.Sigmoid).then_inc(gates_done, 1)
            for n in range(2):
                act.wait_ge(hidden_summed, n + 1)
                nc.scalar.activation(hidden[:, n], ps[:, 2 * n:2 * n + 2, 0:NB], ACT.Gelu_apprx_tanh).then_inc(hidden_done, 1)
            act.wait_ge(cmp_summed, 1)
            nc.scalar.activation(k_cmp[:, :], ps[:, 4, 0:N_CMP], ACT.Copy).then_inc(cmp_copied, 1)
            act.wait_ge(cmp_summed, 2)
            nc.scalar.activation(v_cmp[0:N_CMP], ps[0:N_CMP, 6, 0:2 * HEAD], ACT.Copy).then_inc(cmp_copied, 1)

    cos, sin, rot = C.table("cos"), C.table("sin"), C.const("rot")
    rope_stage(C, "nsa_rope", [(qt[:, m], rot, cos, sin, HEAD ** -0.5) for m in range(4)] + [(z, rot, cos, sin, 1.0) for z in (ks, kw)])
    groups = []
    for hd in range(8):
        g, m = hd // 4, hd % 4
        rows = slice(64 * g, 64 * g + 64)

        def coef(b, hd=hd):
            return lambda i: gates[:, i, 3 * hd + b:3 * hd + b + 1]

        def causal(k, v, b):
            return ([(qt[rows, m], k[rows], lambda i: C.const("causal"), lambda i: (i + 1) * P, coef(b))],
                    lambda j, g=g: v[:, j, g * HEAD:(g + 1) * HEAD])

        cmp = ([(qt[rows, m], k_cmp[rows], lambda i: C.const("cmp_mask")[:, i * N_CMP:(i + 1) * N_CMP], lambda i: N_CMP, coef(0))],
               lambda j, g=g: v_cmp[0:N_CMP, g * HEAD:(g + 1) * HEAD])
        half = slice(64 * (hd % 2), 64 * (hd % 2) + 64)
        groups.append(([cmp, causal(ks, vs, 1), causal(kw, vw, 2)], half, mixed[:, hd // 2] if hd % 2 else None, hd // 2))
    attention_stage(C, "nsa_attn", groups)


def mlstm(C, ctx, qk, v, li, lf, og, taps, bias, ig_b, fg_b, norm, mixed):
    nc, ps = C.nc, C.ps
    conv_stage(C, "mlstm_conv", [(qk[:, m], qk[:, m], [taps[:, m, j:j + 1] for j in range(4)], bias[:, m:m + 1]) for m in range(4)])
    rowsb = C.sb(ctx, "gate_rows", [4, 4, T])
    b_r, g_r, m_r, s_r = (rowsb[:, n] for n in range(4))
    g_col = C.sb(ctx, "g_col", [P, NCH, 4])
    with C.stage("mlstm_gates", "gate_link gate_in gate_exp gate_log turned og_done") as (sctx, blk, sems):
        gate_link, gate_in, gate_exp, gate_log, turned, og_done = sems
        tmp = C.sb(sctx, "tmp", [4, 2, T])
        block = sctx.enter_context(blk)

        @block.vector
        def _(dve):
            link = chain(dve, gate_link)
            link(nc.vector.tensor_scalar(lf, lf, fg_b, None, ALU.add))
            link(nc.vector.tensor_scalar(li, li, ig_b, None, ALU.add))
            nc.vector.scalar_tensor_tensor(tmp[:, 0], lf, -1.0, lf, ALU.mult, ALU.max).then_inc(gate_in, 1)
            dve.wait_ge(gate_in, 1)
            link(nc.vector.tensor_scalar(lf, lf, 0.0, None, ALU.min))
            dve.wait_ge(gate_log, 1)
            link(nc.vector.tensor_tensor(lf, lf, tmp[:, 1], ALU.subtract))
            link(nc.vector.tensor_tensor_scan(b_r, C.const("ones_t")[0:4], lf, 0.0, ALU.mult, ALU.add))
            link(nc.vector.tensor_tensor(g_r, li, b_r, ALU.subtract))
            link(nc.vector.tensor_tensor_scan(m_r, C.const("ones_t")[0:4], g_r, 0.0, ALU.mult, ALU.max))
            link(nc.vector.tensor_tensor(s_r, b_r, m_r, ALU.add))
            dve.wait_ge(turned, 1)
            link(nc.vector.tensor_copy(g_col[:, :, :], ps[:, 0, 0:16].rearrange("p (c h) -> p c h", h=4)))

        @block.scalar
        def _(act):
            nc.scalar.activation(og, og, ACT.Sigmoid).then_inc(og_done, 1)
            act.wait_ge(gate_in, 1)
            nc.scalar.activation(tmp[:, 1], tmp[:, 0], ACT.Exp, scale=-1.0).then_inc(gate_exp, 1)
            act.wait_ge(gate_exp, 1)
            nc.scalar.activation(tmp[:, 1], tmp[:, 1], ACT.Ln, bias=C.const("one")[0:4]).then_inc(gate_log, 1)

        @block.tensor
        def _(pe):
            pe.wait_ge(gate_link, 6)
            for c in range(NCH):
                mm = nc.tensor.transpose(ps[:, 0, 4 * c:4 * c + 4], g_r[:, c * P:(c + 1) * P], C.ident[0:4, 0:4])
            mm.then_inc(turned, 1)

    with C.stage("mlstm_scan", "rows_spread scores_done clamped exp_done weighed mask_link num_done guard_exp den_link head_done") as (sctx, blk, sems):
        rows_spread, scores_done, clamped, exp_done, weighed, mask_link, num_done, guard_exp, den_link, head_done = sems
        wts = C.sb(sctx, "wts", [P, 3, T])
        guard = C.sb(sctx, "guard", [P, 2, T])
        block = sctx.enter_context(blk)
        M_BANK, G_BANK, S_BANKS, NUM, DEN = 0, 1, (2, 3), (4, 5), (6, 7)
        units = [(h, j) for h in range(4) for j in range(NCH)]

        def head_rows(h):
            return slice(64 * (h % 2), 64 * (h % 2) + 64)

        @block.tensor
        def _(pe):
            def spread(h):
                if h:
                    pe.wait_ge(clamped, 4 * h)
                    pe.wait_ge(guard_exp, h)
                sel = C.const("select")[0:4, h * P:(h + 1) * P]
                nc.tensor.matmul(ps[:, M_BANK], sel, m_r, start=True, stop=True)
                nc.tensor.matmul(ps[:, G_BANK], sel, s_r, start=True, stop=True).then_inc(rows_spread, 1)

            def scores(u):
                h, j = units[u]
                if u >= 2:
                    pe.wait_ge(weighed, u - 1)
                nc.tensor.matmul(ps[:, S_BANKS[u % 2], 0:T - j * P], qk[head_rows(h), 2 + h // 2, j * P:(j + 1) * P],
                                 qk[head_rows(h), h // 2, j * P:T], start=True, stop=True).then_inc(scores_done, 1)

            def sums(u):
                h, j = units[u]
                if j == 0 and h >= 2:
                    pe.wait_ge(head_done, h - 1)
                pe.wait_ge(weighed, u + 1)
                w = wts[:, u % 3, 0:T - j * P]
                nc.tensor.matmul(ps[:, NUM[h % 2], j * P:T], v[:, j, h * P:(h + 1) * P], w, start=j == 0, stop=j == NCH - 1)
                nc.tensor.matmul(ps[:, DEN[h % 2], j * P:T], C.ones, w, start=j == 0, stop=j == NCH - 1).then_inc(num_done, 1)

            for u, (h, j) in enumerate(units):
                if j == 0:
                    spread(h)
                scores(u)
                if u:
                    sums(u - 1)
            sums(len(units) - 1)

        @block.vector
        def _(dve):
            link, link_d = chain(dve, mask_link), chain(dve, den_link)

            def finish(h):
                out = mixed[:, 4 + h]
                gd = guard[:, h % 2]
                dve.wait_ge(num_done, 4 * h + 4)
                dve.wait_ge(guard_exp, h + 1)
                link_d(nc.vector.scalar_tensor_tensor(gd, ps[:, DEN[h % 2]], -1.0, gd, ALU.mult, ALU.max))
                link_d(nc.vector.tensor_tensor(gd, ps[:, DEN[h % 2]], gd, ALU.max))
                link_d(nc.vector.reciprocal(gd, gd))
                nc.vector.tensor_tensor(out, ps[:, NUM[h % 2]], gd, ALU.mult).then_inc(head_done, 1)

            for u, (h, j) in enumerate(units):
                w = wts[:, u % 3, 0:T - j * P]
                dve.wait_ge(rows_spread, h + 1)
                if u >= 3:
                    dve.wait_ge(num_done, u - 2)
                nc.vector.tensor_scalar(w, ps[:, M_BANK, j * P:T], g_col[:, j, h:h + 1], 0.0, ALU.subtract, ALU.max).then_inc(clamped, 1)
                dve.wait_ge(scores_done, u + 1)
                dve.wait_ge(exp_done, u + 1)
                link(nc.vector.scalar_tensor_tensor(w, ps[:, S_BANKS[u % 2], 0:T - j * P], HEAD ** -0.5, w, ALU.mult, ALU.mult))
                nc.vector.tensor_tensor(w[:, 0:P], w[:, 0:P], C.const("upper"), ALU.mult).then_inc(weighed, 1)
                if j == 1 and h:
                    finish(h - 1)
            finish(3)

        @block.scalar
        def _(act):
            for u, (h, j) in enumerate(units):
                if j == 0:
                    act.wait_ge(rows_spread, h + 1)
                    if h >= 2:
                        act.wait_ge(head_done, h - 1)
                    nc.scalar.activation(guard[:, h % 2], ps[:, G_BANK], ACT.Exp, scale=-1.0).then_inc(guard_exp, 1)
                act.wait_ge(clamped, u + 1)
                w = wts[:, u % 3, 0:T - j * P]
                nc.scalar.activation(w, w, ACT.Exp, scale=-1.0).then_inc(exp_done, 1)

    head_norm_stage(C, "mlstm_norm", mixed[:, 4:8], mixed[:, 4:8], C.ones, P, C.eps, norm, og)


def log_sigmoid_terms(C, dve, link, z, tmp, made):
    link(C.nc.vector.scalar_tensor_tensor(tmp, z, -1.0, z, ALU.mult, ALU.max))
    C.nc.vector.tensor_scalar(z, z, 0.0, None, ALU.min).then_inc(made, 1)


def gla_stage(C, name, dk, q, k, lf, v, out):
    nc, ps = C.nc, C.ps
    n = q.shape[1]
    with C.stage(name, "scan_link summed_up at_cleared dist_done exp_done level_ready level_summed level_taken in_decayed in_ready out_dist "
                 "out_decayed out_ready turned turn_copied inc_summed state_link states_ready o_summed") as (ctx, blk, sems):
        (scan_link, summed_up, at_cleared, dist_done, exp_done, level_ready, level_summed, level_taken, in_decayed, in_ready, out_dist,
         out_decayed, out_ready, turned, turn_copied, inc_summed, state_link, states_ready, o_summed) = sems
        b = C.sb(ctx, "b", [P, n, T])
        dist = C.sb(ctx, "dist", [P, 2, n, T])
        pair = C.sb(ctx, "pair", [P, 2, n, T])
        q_in = C.sb(ctx, "q_in", [P, n, T])
        k_out = C.sb(ctx, "k_out", [P, n, T])
        k_row = C.sb(ctx, "k_row", [P, NCH, n * P])
        at = C.sb(ctx, "at", [P, 4, NCH, P])
        states = C.sb(ctx, "states", [P, NCH, n, HEAD])
        block = ctx.enter_context(blk)
        STEPS = LEVELS + 1
        TURN, INC, O = (0, 1, 2, 3), 4, (6, 7)

        def rows(h):
            return slice(dk * (h % (P // dk)), dk * (h % (P // dk)) + dk)

        def tile(h):
            return h // (P // dk)

        def blocks(t, w):
            return t.rearrange("p n (m o w) -> p (n m) o w", o=2, w=w)

        @block.gpsimd
        def _(pool):
            nc.gpsimd.memset(at[:, :, :, :], 0.0).then_inc(at_cleared, 1)

        @block.vector
        def _(dve):
            link = chain(dve, scan_link)
            for m in range(n):
                last = nc.vector.tensor_tensor_scan(b[:, m], C.const("run"), lf[:, m], 0.0, ALU.mult, ALU.add)
            last.then_inc(summed_up, 1)
            dve.wait_ge(summed_up, 1)
            for m in range(n):
                bm = b[:, m].rearrange("p (c t) -> p c t", c=NCH)
                end = bm[:, :, P - 1:P].to_broadcast([P, NCH, P])
                last = nc.vector.tensor_tensor(k_out[:, m].rearrange("p (c t) -> p c t", c=NCH), end, bm, ALU.subtract)
            last.then_inc(out_dist, 1)

            def distance(s):
                w = 1 << s
                if s >= 2:
                    dve.wait_ge(level_ready, s - 1)
                v2 = b[:, :, :].rearrange("p n (m w) -> p (n m) w", w=2 * w)
                ref = v2[:, :, w - 1:w].to_broadcast(list(v2.shape))
                nc.vector.tensor_tensor(dist[:, s % 2].rearrange("p n (m w) -> p (n m) w", w=2 * w), v2, ref, ALU.subtract).then_inc(dist_done, 1)

            def operands(s):
                w = 1 << s
                dve.wait_ge(exp_done, s + 1)
                if s >= 2:
                    dve.wait_ge(level_summed, s)
                for o, src in ((1, q), (0, k)):
                    ins = nc.vector.tensor_tensor(blocks(pair[:, s % 2], w)[:, :, o], blocks(src, w)[:, :, o], blocks(dist[:, s % 2], w)[:, :, o], ALU.mult)
                ins.then_inc(level_ready, 1)
                dve.wait_ge(level_ready, s + 1)

            def take(step):
                dve.wait_ge(level_summed, step + 1)
                dve.wait_ge(at_cleared, 1)
                mask = C.ident if step == 0 else C.const("levels")[:, (step - 1) * P:step * P]
                first = 4 * (step % 2)
                data = ps[:, first:first + 4].rearrange("p h (c i) -> p (h c) i", c=NCH)
                nc.vector.copy_predicated(at[:, :, :, :].rearrange("p h c i -> p (h c) i"), mask.bitcast(I32).unsqueeze(1).to_broadcast([P, 4 * NCH, P]), data).then_inc(level_taken, 1)

            distance(0)
            distance(1)
            dve.wait_ge(in_decayed, 1)
            link(nc.vector.tensor_tensor(q_in[:, :, :], q, q_in[:, :, :], ALU.mult))
            dve.wait_ge(out_decayed, 1)
            nc.vector.tensor_tensor(k_out[:, :, :], k, k_out[:, :, :], ALU.mult).then_inc(out_ready, 1)
            for s in range(LEVELS):
                operands(s)
                if s + 2 < LEVELS:
                    distance(s + 2)
                if s:
                    dve.wait_ge(level_taken, s)
                take(s)
            dve.wait_ge(level_taken, LEVELS)
            take(LEVELS)
            dve.wait_ge(inc_summed, 1)
            slink = chain(dve, state_link)
            inc = ps[:, INC, 0:(NCH - 1) * n * HEAD].rearrange("p (c m v) -> p c m v", c=NCH - 1, m=n)
            dve.wait_ge(in_decayed, 2)
            slink(nc.vector.tensor_copy(states[:, 1], inc[:, 0]))
            for c in range(1, NCH - 1):
                for m in range(n):
                    last = nc.vector.scalar_tensor_tensor(states[:, c + 1, m], states[:, c, m], states[:, 0, m, c:c + 1], inc[:, c, m], ALU.mult, ALU.add)
                slink(last)
            dve.sem_inc(states_ready, 1)

        @block.scalar
        def _(act):
            act.wait_ge(summed_up, 1)
            nc.scalar.activation(q_in[:, :, :], b[:, :, :], ACT.Exp).then_inc(in_decayed, 1)
            act.wait_ge(out_dist, 1)
            nc.scalar.activation(k_out[:, :, :], k_out[:, :, :], ACT.Exp).then_inc(out_decayed, 1)
            nc.scalar.activation(states[:, 0, :, 0:NCH], b[:, :, P - 1:T:P], ACT.Exp).then_inc(in_decayed, 1)
            for s in range(LEVELS):
                w = 1 << s
                act.wait_ge(dist_done, s + 1)
                d = blocks(dist[:, s % 2], w)
                nc.scalar.activation(d[:, :, 1], d[:, :, 1], ACT.Exp)
                nc.scalar.activation(d[:, :, 0], d[:, :, 0], ACT.Exp, scale=-1.0).then_inc(exp_done, 1)
            for c in range(NCH):
                act.wait_ge(turned, c + 1)
                nc.scalar.activation(k_row[:, c], ps[:, TURN[c], 0:n * P], ACT.Copy).then_inc(turn_copied, 1)
            act.wait_ge(o_summed, 1)
            nc.scalar.activation(out, ps[:, O[0]:O[1] + 1], ACT.Copy)

        @block.tensor
        def _(pe):
            for step in range(STEPS):
                if step:
                    pe.wait_ge(level_ready, step)
                if step >= 2:
                    pe.wait_ge(level_taken, step - 1)
                for h in range(4):
                    for c in range(NCH):
                        ts = slice(c * P, (c + 1) * P)
                        if step:
                            left = right = pair[rows(h), (step - 1) % 2, tile(h), ts]
                        else:
                            left, right = k[rows(h), tile(h), ts], q[rows(h), tile(h), ts]
                        mm = nc.tensor.matmul(ps[:, 4 * (step % 2) + h, c * P:(c + 1) * P], left, right, start=True, stop=True)
                mm.then_inc(level_summed, 1)
            pe.wait_ge(out_ready, 1)
            pe.wait_ge(level_taken, STEPS)
            for c in range(NCH):
                for m in range(n):
                    mm = nc.tensor.transpose(ps[:, TURN[c], m * P:(m + 1) * P], k_out[:, m, c * P:(c + 1) * P], C.ident)
                mm.then_inc(turned, 1)
            for c in range(NCH - 1):
                pe.wait_ge(turn_copied, c + 1)
                for h in range(4):
                    at_col = (c * n + tile(h)) * HEAD
                    mm = nc.tensor.matmul(ps[rows(h), INC, at_col:at_col + HEAD], k_row[:, c, h * dk:(h + 1) * dk], v[:, c, h * HEAD:(h + 1) * HEAD], start=True, stop=True)
            mm.then_inc(inc_summed, 1)
            pe.wait_ge(states_ready, 1)
            for h in range(4):
                for c in range(NCH):
                    o = ps[64 * (h % 2):64 * (h % 2) + 64, O[h // 2], c * P:(c + 1) * P]
                    mm = nc.tensor.matmul(o, v[:, c, h * HEAD:(h + 1) * HEAD], at[:, h, c], start=True, stop=c == 0)
                    if c:
                        mm = nc.tensor.matmul(o, states[rows(h), c, tile(h)], q_in[rows(h), tile(h), c * P:(c + 1) * P], start=False, stop=True)
            mm.then_inc(o_summed, 1)


def lower_bound_stage(C, name, logits, lb):
    nc = C.nc
    with C.stage(name, "lb_link shifted exped") as (ctx, blk, (lb_link, shifted, exped)):
        t = C.sb(ctx, "t", [P, 2, 2])
        m = C.sb(ctx, "m", [P, 2])
        block = ctx.enter_context(blk)

        @block.vector
        def _(dve):
            link = chain(dve, lb_link)
            link(nc.vector.tensor_tensor(m[:, :], logits[:, 0], logits[:, 1], ALU.max))
            nc.vector.tensor_tensor(t[:, :, :], logits, m[:, :].unsqueeze(1).to_broadcast([P, 2, 2]), ALU.subtract).then_inc(shifted, 1)
            dve.wait_ge(exped, 1)
            link(nc.vector.tensor_tensor(m[:, :], t[:, 0], t[:, 1], ALU.add))
            link(nc.vector.reciprocal(m[:, :], m[:, :]))
            link(nc.vector.tensor_tensor(lb, t[:, 1], m[:, :], ALU.mult))

        @block.scalar
        def _(act):
            act.wait_ge(shifted, 1)
            nc.scalar.activation(t[:, :, :], t[:, :, :], ACT.Exp).then_inc(exped, 1)


def hgrn(C, ctx, name, q, f, v, g, lb, norm, out):
    nc = C.nc
    k = C.sb(ctx, "hk", [P, 2, T])
    LN_SHIFT = 50
    with C.stage(name + "_in", "silu_done gates_done k_done q_scaled f_link f_ready log_done") as (sctx, blk, sems):
        silu_done, gates_done, k_done, q_scaled, f_link, f_ready, log_done = sems
        tiny = C.sb(sctx, "tiny", [P, 2, T])
        low = C.sb(sctx, "low", [P, 2, T])
        olb = C.sb(sctx, "olb", [P, 2])
        block = sctx.enter_context(blk)

        @block.scalar
        def _(act):
            nc.scalar.activation(k[:, :, :], f, ACT.Sigmoid, scale=-1.0).then_inc(k_done, 1)
            act.wait_ge(k_done, 1)
            nc.scalar.activation(f, f, ACT.Sigmoid).then_inc(gates_done, 1)
            nc.scalar.activation(g, g, ACT.Sigmoid)
            nc.scalar.activation(q, q, ACT.Silu).then_inc(silu_done, 1)
            act.wait_ge(f_ready, 1)
            nc.scalar.activation(low[:, :, :], f, ACT.Ln, scale=float(2 ** LN_SHIFT)).then_inc(log_done, 1)
            act.wait_ge(log_done, 1)
            nc.scalar.activation(f, tiny[:, :, :], ACT.Ln).then_inc(log_done, 1)

        @block.vector
        def _(dve):
            link = chain(dve, f_link)
            dve.wait_ge(gates_done, 1)
            if lb is not None:
                link(nc.vector.tensor_scalar(olb[:, :], lb, -1.0, 1.0, ALU.mult, ALU.add))
                for m in range(2):
                    nc.vector.tensor_scalar(k[:, m], k[:, m], olb[:, m:m + 1], None, ALU.mult)
                    last = nc.vector.tensor_scalar(f[:, m], f[:, m], olb[:, m:m + 1], lb[:, m:m + 1], ALU.mult, ALU.add)
                link(last)
            link(nc.vector.tensor_scalar(f, f, 1e-30, None, ALU.max))
            nc.vector.tensor_scalar(tiny[:, :, :], f, 1e-19, None, ALU.max).then_inc(f_ready, 1)
            dve.wait_ge(silu_done, 1)
            link(nc.vector.tensor_scalar(q, q, HEAD ** -0.5, None, ALU.mult))
            dve.wait_ge(log_done, 2)
            link(nc.vector.tensor_scalar(tiny[:, :, :], tiny[:, :, :], 1e-19, None, ALU.is_le))
            link(nc.vector.tensor_scalar(low[:, :, :], low[:, :, :], -LN_SHIFT * float(np.log(2.0)), None, ALU.add))
            link(nc.vector.copy_predicated(f, tiny[:, :, :].bitcast(I32), low[:, :, :]))

    gla_stage(C, name, HEAD, q, k[:, :, :], f, v, out)
    head_norm_stage(C, name + "_norm", out, out, C.const("pairs"), HEAD, C.eps, norm, g)


def gla(C, ctx, name, q, k, v, code, g, w_gk2, b_gk, norm, out):
    nc, ps = C.nc, C.ps
    lf = C.sb(ctx, "lf", [P, 1, T])
    with C.stage(name + "_in", "gate_summed gate_link terms_made exp_done log_done") as (sctx, blk, sems):
        gate_summed, gate_link, terms_made, exp_done, log_done = sems
        size = C.sb(sctx, "size", [P, T])
        block = sctx.enter_context(blk)

        @block.tensor
        def _(pe):
            nc.tensor.matmul(ps[:, 0], w_gk2, code, start=True, stop=True).then_inc(gate_summed, 1)

        @block.vector
        def _(dve):
            link = chain(dve, gate_link)
            dve.wait_ge(gate_summed, 1)
            link(nc.vector.tensor_scalar(lf[:, 0], ps[:, 0], b_gk, None, ALU.add))
            log_sigmoid_terms(C, dve, link, lf[:, 0], size[:, :], terms_made)
            link(nc.vector.tensor_scalar(q, q, (HEAD // 2) ** -0.5, None, ALU.mult))
            dve.wait_ge(log_done, 1)
            link(nc.vector.tensor_tensor(lf[:, 0], lf[:, 0], size[:, :], ALU.subtract))
            link(nc.vector.tensor_scalar(lf[:, 0], lf[:, 0], 1.0 / 16.0, None, ALU.mult))

        @block.scalar
        def _(act):
            nc.scalar.activation(g, g, ACT.Silu)
            act.wait_ge(terms_made, 1)
            nc.scalar.activation(size[:, :], size[:, :], ACT.Exp, scale=-1.0).then_inc(exp_done, 1)
            act.wait_ge(exp_done, 1)
            nc.scalar.activation(size[:, :], size[:, :], ACT.Ln, bias=C.const("one")).then_inc(log_done, 1)

    gla_stage(C, name, HEAD // 2, q, k, lf[:, :, :], v, out)
    head_norm_stage(C, name + "_norm", out, out, C.const("pairs"), HEAD, C.eps, norm, g)


MLA_QK = 96


def mla(C, ctx, name, cq, ckv, kr, q_norm, kv_norm, w_uq, w_ukv, out):
    nc, ps = C.nc, C.ps
    qh = C.sb(ctx, "qh", [P, 4, T])
    kh = C.sb(ctx, "kh", [P, 4, T])
    v = C.sb(ctx, "v_mla", [P, NCH, 4 * HEAD])
    with C.stage(name + "_in", "squared summed logged rstd_done normed up_summed up_copied kr_copied") as (sctx, blk, sems):
        squared, summed, logged, rstd_done, normed, up_summed, up_copied, kr_copied = sems
        sq = C.sb(sctx, "sq", [P, 3, T])
        block = sctx.enter_context(blk)

        @block.scalar
        def _(act):
            nc.scalar.activation(sq[:, 0:2], cq, ACT.Square).then_inc(squared, 1)
            nc.scalar.activation(sq[:, 2:3], ckv, ACT.Square).then_inc(squared, 1)
            act.wait_ge(summed, 1)
            nc.scalar.activation(sq[:, 0], ps[:, 0], ACT.Ln, bias=C.eps, scale=1.0 / 256)
            nc.scalar.activation(sq[:, 1], ps[:, 1], ACT.Ln, bias=C.eps, scale=1.0 / P).then_inc(logged, 1)
            act.wait_ge(logged, 1)
            nc.scalar.activation(sq[:, 0:2], sq[:, 0:2], ACT.Exp, scale=-0.5).then_inc(rstd_done, 1)
            for u in range(12):
                act.wait_ge(up_summed, u + 1)
                if u < 4:
                    nc.scalar.activation(qh[0:MLA_QK, u], ps[0:MLA_QK, 2 + u % 6], ACT.Copy).then_inc(up_copied, 1)
                elif u < 8:
                    nc.scalar.activation(kh[0:HEAD, u - 4], ps[0:HEAD, 2 + u % 6], ACT.Copy).then_inc(up_copied, 1)
                else:
                    nc.scalar.activation(v[:, u - 8], ps[:, 2 + u % 6, 0:4 * HEAD], ACT.Copy).then_inc(up_copied, 1)

        @block.tensor
        def _(pe):
            pe.wait_ge(squared, 2)
            nc.tensor.matmul(ps[:, 0], C.ones, sq[:, 0], start=True, stop=False)
            nc.tensor.matmul(ps[:, 0], C.ones, sq[:, 1], start=False, stop=True)
            nc.tensor.matmul(ps[:, 1], C.ones, sq[:, 2], start=True, stop=True).then_inc(summed, 1)
            pe.wait_ge(normed, 1)
            for u in range(12):
                if u >= 6:
                    pe.wait_ge(up_copied, u - 5)
                bank = 2 + u % 6
                if u < 4:
                    nc.tensor.matmul(ps[0:MLA_QK, bank], w_uq[:, 0, u * MLA_QK:(u + 1) * MLA_QK], cq[:, 0], start=True, stop=False)
                    mm = nc.tensor.matmul(ps[0:MLA_QK, bank], w_uq[:, 1, u * MLA_QK:(u + 1) * MLA_QK], cq[:, 1], start=False, stop=True)
                elif u < 8:
                    mm = nc.tensor.matmul(ps[0:HEAD, bank], w_ukv[:, (u - 4) * P:(u - 4) * P + HEAD], ckv[:, 0], start=True, stop=True)
                else:
                    c = u - 8
                    values = w_ukv.rearrange("p (h o d) -> p h o d", h=4, o=2)[:, :, 1]
                    mm = nc.tensor.matmul(ps[:, bank, 0:4 * HEAD], ckv[:, 0, c * P:(c + 1) * P], values, start=True, stop=True)
                mm.then_inc(up_summed, 1)

        @block.vector
        def _(dve):
            dve.wait_ge(rstd_done, 1)
            for m in range(2):
                nc.vector.scalar_tensor_tensor(cq[:, m], cq[:, m], q_norm[:, m:m + 1], sq[:, 0], ALU.mult, ALU.mult)
            nc.vector.scalar_tensor_tensor(ckv[:, 0], ckv[:, 0], kv_norm, sq[:, 1], ALU.mult, ALU.mult).then_inc(normed, 1)
            for h in range(4):
                nc.vector.tensor_copy(kh[HEAD:MLA_QK, h], kr[HEAD:MLA_QK])

    cos, sin, rot = C.table("cos_mla"), C.table("sin_mla"), C.const("rot_mla")
    rope_stage(C, name + "_rope", [(qh[0:MLA_QK, h], rot, cos, sin, MLA_QK ** -0.5) for h in range(4)] + [(kh[0:MLA_QK, h], rot, cos, sin, 1.0) for h in range(4)])
    groups = []
    for h in range(4):
        maps = [(qh[0:MLA_QK, h], kh[0:MLA_QK, h], lambda i: C.const("causal"), lambda i: (i + 1) * P, None)]
        groups.append(([(maps, lambda j, h=h: v[:, j, h * HEAD:(h + 1) * HEAD])], slice(64 * (h % 2), 64 * (h % 2) + 64), out[:, h // 2] if h % 2 else None, h // 2))
    attention_stage(C, name, groups)


def gated_delta(C, ctx, name, qkv, z, beta, alpha, taps, a_log, dt_bias, norm, out):
    nc, ps = C.nc, C.ps
    conv_stage(C, name + "_conv", [(qkv[:, m], qkv[:, m], [taps[:, m, j:j + 1] for j in range(4)], None) for m in range(6)])
    q, k, v = qkv[:, 0:2], qkv[:, 2:4], qkv[:, 4:6]
    qb = C.sb(ctx, "qb", [P, 2, 2, T])
    k_in, k_out = C.sb(ctx, "k_in", [P, 2, T]), C.sb(ctx, "k_out", [P, 2, T])
    q_in = C.sb(ctx, "q_in", [P, 2, T])
    decay = C.sb(ctx, "decay", [P, 4, NCH, 2, P])
    b_col = C.sb(ctx, "b_col", [P, NCH, 4])
    last_exp = C.sb(ctx, "last_exp", [P, 2, NCH])
    with C.stage(name + "_in", "gate_link terms_made beta_done exp_done log_done b_ready a_done turned b_copied spread_b spread_beta apart apart_exp "
                 "squared norm_summed logged rstd_done vec_link in_exp dist_done out_exp beta_used") as (sctx, blk, sems):
        (gate_link, terms_made, beta_done, exp_done, log_done, b_ready, a_done, turned, b_copied, spread_b, spread_beta, apart, apart_exp,
         squared, norm_summed, logged, rstd_done, vec_link, in_exp, dist_done, out_exp, beta_used) = sems
        sq = C.sb(sctx, "sq", [P, 4, T])
        size = C.sb(sctx, "size", [4, T])
        soft = C.sb(sctx, "soft", [4, T])
        a_neg = C.sb(sctx, "a_neg", [4, 1])
        block = sctx.enter_context(blk)

        @block.vector
        def _(dve):
            link = chain(dve, gate_link)
            link(nc.vector.tensor_scalar(alpha, alpha, dt_bias, None, ALU.add))
            nc.vector.scalar_tensor_tensor(size[:, :], alpha, -1.0, alpha, ALU.mult, ALU.max).then_inc(terms_made, 1)
            dve.wait_ge(terms_made, 1)
            link(nc.vector.tensor_scalar(alpha, alpha, 0.0, None, ALU.max))
            dve.wait_ge(log_done, 1)
            link(nc.vector.tensor_tensor(alpha, alpha, soft[:, :], ALU.add))
            dve.wait_ge(a_done, 1)
            link(nc.vector.tensor_scalar(alpha, alpha, a_neg[:, :], -1.0, ALU.mult, ALU.mult))
            link(nc.vector.tensor_tensor_scan(size[:, :], C.const("run")[0:4], alpha, 0.0, ALU.mult, ALU.add))
            dve.sem_inc(b_ready, 1)
            vlink = chain(dve, vec_link)
            dve.wait_ge(turned, 1)
            vlink(nc.vector.tensor_copy(b_col[:, :, :], ps[:, 4, 0:4 * NCH].rearrange("p (c h) -> p c h", h=4)))
            dve.wait_ge(spread_b, 1)
            for h in range(4):
                for c in range(NCH):
                    ins = nc.vector.tensor_scalar(decay[:, h, c, 0], ps[:, h, c * P:(c + 1) * P], b_col[:, c, h:h + 1], 0.0, ALU.subtract, ALU.min)
            ins.then_inc(apart, 1)
            dve.wait_ge(rstd_done, 1)
            nc.vector.scalar_tensor_tensor(qb[:, :, 0], q, HEAD ** -0.5, sq[:, 0:2], ALU.mult, ALU.mult)
            vlink(nc.vector.tensor_tensor(k, k, sq[:, 2:4], ALU.mult))
            dve.wait_ge(spread_beta, 1)
            vlink(nc.vector.tensor_tensor(qb[:, :, 1], k, ps[:, 4:6], ALU.mult))
            vlink(nc.vector.tensor_tensor(v, v, ps[:, 4:6], ALU.mult))
            for m in range(2):
                bm = sq[:, m].rearrange("p (c t) -> p c t", c=NCH)
                end = bm[:, :, P - 1:P].to_broadcast([P, NCH, P])
                dve.wait_ge(in_exp, 1)
                ins = nc.vector.tensor_tensor(sq[:, 2 + m].rearrange("p (c t) -> p c t", c=NCH), end, bm, ALU.subtract)
            ins.then_inc(dist_done, 1)
            dve.wait_ge(in_exp, 2)
            nc.vector.tensor_tensor(k_in[:, :, :], qb[:, :, 1], q_in[:, :, :], ALU.mult)
            vlink(nc.vector.tensor_copy(last_exp[:, :, :], q_in[:, :, P - 1:T:P]))
            vlink(nc.vector.tensor_tensor(q_in[:, :, :], qb[:, :, 0], q_in[:, :, :], ALU.mult))
            dve.wait_ge(out_exp, 1)
            nc.vector.tensor_tensor(k_out[:, :, :], k, sq[:, 2:4], ALU.mult)

        @block.scalar
        def _(act):
            nc.scalar.activation(z, z, ACT.Silu)
            nc.scalar.activation(beta, beta, ACT.Sigmoid).then_inc(beta_done, 1)
            nc.scalar.activation(sq[:, :, :], qkv[:, 0:4], ACT.Square).then_inc(squared, 1)
            nc.scalar.activation(a_neg[:, :], a_log, ACT.Exp).then_inc(a_done, 1)
            act.wait_ge(terms_made, 1)
            nc.scalar.activation(soft[:, :], size[:, :], ACT.Exp, scale=-1.0).then_inc(exp_done, 1)
            act.wait_ge(exp_done, 1)
            nc.scalar.activation(soft[:, :], soft[:, :], ACT.Ln, bias=C.const("one")[0:4]).then_inc(log_done, 1)
            act.wait_ge(norm_summed, 1)
            nc.scalar.activation(sq[:, :, :], ps[:, 0:4], ACT.Ln, bias=C.eps).then_inc(logged, 1)
            act.wait_ge(logged, 1)
            nc.scalar.activation(sq[:, :, :], sq[:, :, :], ACT.Exp, scale=-0.5).then_inc(rstd_done, 1)
            act.wait_ge(apart, 1)
            nc.scalar.activation(decay[:, :, :, 0], decay[:, :, :, 0], ACT.Exp).then_inc(apart_exp, 1)
            act.wait_ge(spread_beta, 1)
            act.wait_ge(vec_link, 3)
            nc.scalar.activation(sq[:, 0:2], ps[:, 6:8], ACT.Copy).then_inc(in_exp, 1)
            nc.scalar.activation(q_in[:, :, :], ps[:, 6:8], ACT.Exp).then_inc(in_exp, 1)
            act.wait_ge(dist_done, 1)
            nc.scalar.activation(sq[:, 2:4], sq[:, 2:4], ACT.Exp).then_inc(out_exp, 1)

        @block.gpsimd
        def _(pool):
            pool.wait_ge(apart_exp, 1)
            both = decay[:, :, :, :, :].rearrange("p h c o i -> p (h c) o i")
            for o, mask in ((1, "strict"), (0, "upper")):
                if o == 0:
                    pool.wait_ge(beta_used, 1)
                nc.gpsimd.tensor_tensor(both[:, :, o], both[:, :, 0], C.const(mask).unsqueeze(1).to_broadcast([P, 4 * NCH, P]), ALU.mult).then_inc(beta_used, 1)

        @block.tensor
        def _(pe):
            pe.wait_ge(squared, 1)
            for m in range(4):
                mm = nc.tensor.matmul(ps[:, m], C.const("pairs"), sq[:, m], start=True, stop=True)
            mm.then_inc(norm_summed, 1)
            pe.wait_ge(b_ready, 1)
            for c in range(NCH):
                mm = nc.tensor.transpose(ps[:, 4, 4 * c:4 * c + 4], size[:, c * P:(c + 1) * P], C.ident[0:4, 0:4])
            mm.then_inc(turned, 1)
            pe.wait_ge(logged, 1)
            for h in range(4):
                mm = nc.tensor.matmul(ps[:, h], C.const("select")[0:4, h * P:(h + 1) * P], size[:, :], start=True, stop=True)
            mm.then_inc(spread_b, 1)
            pe.wait_ge(beta_done, 1)
            pe.wait_ge(vec_link, 1)
            for m in range(2):
                nc.tensor.matmul(ps[:, 4 + m], C.const("select_pair")[0:4, m * P:(m + 1) * P], beta, start=True, stop=True)
                mm = nc.tensor.matmul(ps[:, 6 + m], C.const("select_pair")[0:4, m * P:(m + 1) * P], size[:, :], start=True, stop=True)
            mm.then_inc(spread_beta, 1)

    with C.stage(name, inverse_signals() + " mats_summed mats_ready mats_link turned turn_copied zv_summed rhs_ready d_summed d_copied state_summed state_ready y_done y_out") as (sctx, blk, sems):
        inv_sems, (mats_summed, mats_ready, mats_link, turned, turn_copied, zv_summed, rhs_ready, d_summed, d_copied, state_summed, state_ready, y_done, y_out) = sems[:8], sems[8:]
        at = C.sb(sctx, "at", [P, NCH // 2, 2, 4, 2, P])
        k_row, v_row = C.sb(sctx, "k_row", [P, NCH, 2 * P]), C.sb(sctx, "v_row", [P, NCH, 2 * P])
        xts = C.sb(sctx, "xts", [P, 2, 8, P])
        inv = Inverse(C, 8, inv_sems, [xts[:, 0], xts[:, 1]], C.sb(sctx, "x", [P, 8, P]), C.sb(sctx, "y", [P, 8, P]), C.sb(sctx, "masked", [P, 2, 8, P]))
        rhs = C.sb(sctx, "rhs", [P, 2, 2, HEAD])
        delta = C.sb(sctx, "delta", [P, 4, HEAD])
        state = C.sb(sctx, "state", [P, 2, HEAD])
        block = sctx.enter_context(blk)
        ZV, DEL, S, Y = (6, 7), 2, 1, 0

        def rows(h):
            return slice(64 * (h % 2), 64 * (h % 2) + 64)

        def mt(b):
            return at[:, b].rearrange("p c h o i -> p (c h) o i")[:, :, 1]

        @block.tensor
        def _(pe):
            for c in range(NCH):
                for m in range(2):
                    nc.tensor.transpose(ps[:, 4 + c, m * P:(m + 1) * P], k_out[:, m, c * P:(c + 1) * P], C.ident)
                    mm = nc.tensor.transpose(ps[:, 4 + c, (2 + m) * P:(3 + m) * P], v[:, m, c * P:(c + 1) * P], C.ident)
                mm.then_inc(turned, 1)
            for b in range(NCH // 2):
                for h in range(4):
                    if b:
                        pe.wait_ge(mats_ready, 4 * b)
                        pe.wait_ge(inv.xt_updated, b * ((LEVELS - 1) * inv.G + 1))
                        pe.wait_ge(inv.x_updated, b * (LEVELS - 1) * inv.G)
                        pe.wait_ge(inv.y_copied, b * (LEVELS - 1) * inv.G)
                    for o in range(2):
                        ts = slice((2 * b + o) * P, (2 * b + o + 1) * P)
                        mm = nc.tensor.matmul(ps[:, h, 2 * o * P:2 * (o + 1) * P], k[rows(h), h // 2, ts], qb[rows(h), h // 2, :, ts], start=True, stop=True)
                    mm.then_inc(mats_summed, 1)
                pe.wait_ge(mats_ready, 4 * (b + 1))
                pe.wait_ge(turn_copied, NCH)
                inv.pe(pe, b)
            for b in range(1, 3):
                pe.wait_ge(inv.xt_updated, b * ((LEVELS - 1) * inv.G + 1))
            for c in range(NCH):
                ts = slice(c * P, (c + 1) * P)
                if c:
                    pe.wait_ge(state_ready, c)
                    for h in range(4):
                        mm = nc.tensor.matmul(ps[:, ZV[h % 2], h // 2 * HEAD:(h // 2 + 1) * HEAD], k_in[rows(h), h // 2, ts], state[rows(h), h // 2], start=True, stop=True)
                    mm.then_inc(zv_summed, 1)
                pe.wait_ge(rhs_ready, c + 1)
                for h in range(4):
                    mm = nc.tensor.matmul(ps[:, DEL, h * HEAD:(h + 1) * HEAD], xts[:, c // 2, 4 * (c % 2) + h], rhs[:, h % 2, h // 2], start=True, stop=True)
                mm.then_inc(d_summed, 1)
                pe.wait_ge(d_copied, c + 1)
                for h in range(4):
                    mm = nc.tensor.matmul(ps[rows(h), S, h // 2 * HEAD:(h // 2 + 1) * HEAD], k_row[:, c, h * HEAD:(h + 1) * HEAD], delta[:, h], start=True, stop=True)
                mm.then_inc(state_summed, 1)
                if c:
                    pe.wait_ge(y_out, c)
                for h in range(4):
                    o = ps[rows(h), Y, h // 2 * P:(h // 2 + 1) * P]
                    mm = nc.tensor.matmul(o, delta[:, h], at[:, c // 2, c % 2, h, 0], start=True, stop=c == 0)
                    if c:
                        mm = nc.tensor.matmul(o, state[rows(h), h // 2], q_in[rows(h), h // 2, ts], start=False, stop=True)
                mm.then_inc(y_done, 1)

        @block.vector
        def _(dve):
            link = chain(dve, mats_link)
            for b in range(NCH // 2):
                for h in range(4):
                    dve.wait_ge(mats_summed, 4 * b + h + 1)
                    nc.vector.tensor_tensor(at[:, b, :, h], ps[:, h].rearrange("p (c o i) -> p c o i", c=2, o=2), decay[:, h, 2 * b:2 * b + 2], ALU.mult).then_inc(mats_ready, 1)
                dve.wait_ge(mats_ready, 4 * (b + 1))
                inv.dve_start(dve, link, b, mt(b))
                inv.dve(dve, b)
            for c in range(NCH):
                values = v_row[:, c].rearrange("p (m o v) -> p o m v", m=2, o=2)
                if c == 0:
                    dve.wait_ge(turn_copied, NCH)
                    nc.vector.tensor_copy(rhs[:, :, :, :], values).then_inc(rhs_ready, 1)
                else:
                    dve.wait_ge(zv_summed, c)
                    nc.vector.tensor_tensor(rhs[:, :, :, :], values, ps[:, ZV[0]:ZV[1] + 1, 0:2 * HEAD].rearrange("p o (m v) -> p o m v", m=2), ALU.subtract).then_inc(rhs_ready, 1)
                dve.wait_ge(d_summed, c + 1)
                nc.vector.tensor_copy(delta[:, :, :], ps[:, DEL, 0:4 * HEAD].rearrange("p (h v) -> p h v", h=4)).then_inc(d_copied, 1)
                dve.wait_ge(state_summed, c + 1)
                dve.wait_ge(y_done, c + 1)
                if c == 0:
                    nc.vector.tensor_copy(state[:, :, :], ps[:, S, 0:2 * HEAD].rearrange("p (m v) -> p m v", m=2)).then_inc(state_ready, 1)
                elif c < NCH - 1:
                    for m in range(2):
                        ins = nc.vector.scalar_tensor_tensor(state[:, m], state[:, m], last_exp[:, m, c:c + 1], ps[:, S, m * HEAD:(m + 1) * HEAD], ALU.mult, ALU.add)
                    ins.then_inc(state_ready, 1)

        @block.gpsimd
        def _(pool):
            for b in range(NCH // 2):
                inv.pool(pool, b, mt(b), mats_ready, 4 * (b + 1))

        @block.scalar
        def _(act):
            for c in range(NCH):
                act.wait_ge(turned, c + 1)
                nc.scalar.activation(k_row[:, c], ps[:, 4 + c, 0:2 * P], ACT.Copy)
                nc.scalar.activation(v_row[:, c], ps[:, 4 + c, 2 * P:4 * P], ACT.Copy).then_inc(turn_copied, 1)
            for b in range(NCH // 2):
                inv.act(act, b)
            for c in range(NCH):
                act.wait_ge(y_done, c + 1)
                nc.scalar.activation(out[:, :, c * P:(c + 1) * P], ps[:, Y, 0:2 * P].rearrange("p (m i) -> p m i", m=2), ACT.Copy).then_inc(y_out, 1)
    head_norm_stage(C, name + "_norm", out, out, C.const("pairs"), HEAD, C.eps, norm, z)


class Vectors:

    def __init__(self):
        self.at, self.width, self.shapes = {}, 0, {}

    def add(self, name, shape):
        self.at[name], self.shapes[name] = self.width, tuple(shape)
        self.width += int(np.prod(shape))

    def view(self, buffer, name):
        shape = self.shapes[name]
        v = buffer[:, self.at[name]:self.at[name] + int(np.prod(shape))]
        if len(shape) == 2:
            return v.rearrange("p (a b) -> p a b", b=shape[1])
        return v


def columns(a):
    return np.asarray(a).reshape(-1, P).T


def on_rows(a, rows=P):
    out = np.zeros((P, 1), np.float32)
    out[:len(a), 0] = a
    return out


def vector_arrays(inputs):
    v = {}
    for name in ("ffa_norm", "mix_norm", "ffb_norm"):
        for layer in range(2):
            v[f"{name}{layer}"] = ((8,), columns(inputs[name][layer]))
    v["final_norm"] = ((8,), columns(inputs["final_norm"]))
    for name, n in (("mu", 14), ("w0", 4), ("a0", 4), ("kk", 4), ("ka", 4), ("rk", 4), ("lnw", 4), ("lnb", 4)):
        v[name] = ((n,), columns(inputs["rwkv_" + name][0]))
    v["lam"] = ((4, HEAD), np.broadcast_to(np.asarray(inputs["diff_lam"][0]).reshape(1, -1), (P, 4 * HEAD)))
    v["subln"] = ((4,), np.repeat(columns(inputs["diff_subln"][0]), 4, 1))
    for kind in "kv":
        z = np.asarray(inputs["nsa_pe_" + kind][0]).reshape(16, 2, HEAD).transpose(2, 1, 0).reshape(HEAD, 32)
        v["pe_" + kind] = ((2, 16), np.concatenate([z, z], 0))
    v["mlstm_taps"] = ((4, 4), np.asarray(inputs["mlstm_conv_w"][0]).T.reshape(4, P, 4).transpose(1, 0, 2).reshape(P, 16))
    v["mlstm_bias"] = ((4,), columns(inputs["mlstm_conv_b"][0]))
    v["ig_b"] = ((1,), on_rows(inputs["mlstm_ig_b"][0]))
    v["fg_b"] = ((1,), on_rows(inputs["mlstm_fg_b"][0]))
    v["mlstm_norm"] = ((4,), columns(inputs["mlstm_norm"][0]))
    v["lb_logits"] = ((2, 2), columns(inputs["hgrn_lb_logits_2"]))
    for layer in range(2):
        for name in ("pre_mix_g", "post_mix_g", "pre_ffn_g", "post_ffn_g"):
            v[f"{name}{layer}"] = ((8,), columns(inputs[name + "_2"][layer]))
        for name in ("hgrn_norm_g", "gla_norm_g", "gdn_norm_g"):
            v[f"{name}{layer}"] = ((2,), columns(np.tile(np.asarray(inputs[name + "_2"][layer]), 4)))
        v[f"gla_b{layer}"] = ((1,), columns(inputs["gla_b_gk_2"][layer]))
        v[f"mla_q_norm{layer}"] = ((2,), columns(inputs["mla_q_norm_g_2"][layer]))
        v[f"mla_kv_norm{layer}"] = ((1,), columns(inputs["mla_kv_norm_g_2"][layer]))
        v[f"gdn_taps{layer}"] = ((6, 4), np.asarray(inputs["gdn_conv_w_2"][layer]).T.reshape(6, P, 4).transpose(1, 0, 2).reshape(P, 24))
        v[f"gdn_a_log{layer}"] = ((1,), on_rows(inputs["gdn_a_log_2"][layer]))
        v[f"gdn_dt{layer}"] = ((1,), on_rows(inputs["gdn_dt_bias_2"][layer]))
        v[f"ffn_taps{layer}"] = ((FT, 3), np.asarray(inputs["ffn_conv_w_2"][layer]).T.reshape(FT, P, 3).transpose(1, 0, 2).reshape(P, FT * 3))
    return v


def starts(sizes):
    out, at = [], 0
    for s in sizes:
        out.append(at)
        at += s
    return out


def first_mixers_even(C, V, io):
    with ExitStack() as ctx:
        pt = C.sb(ctx, "pt", [P, 14, T])
        w2a2, g2 = C.sb(ctx, "w2a2", [P, 512]), C.sb(ctx, "g2", [P, 512])
        with ExitStack() as qkv:
            qt, kt, v = (C.sb(qkv, n, [P, 4, T]) for n in ("qt", "kt", "v"))
            plan = []
            for first, dst in ((0, qt), (512, kt)):
                plan += [t_chunk(first + 256 * n, [dst[:, 2 * n], dst[:, 2 * n + 1]]) for n in range(2)]
            plan += [row_chunk(1024 + 256 * n, 256, [v[:, c, 256 * n:256 * n + 256] for c in range(NCH)]) for n in range(2)]
            plan += [t_chunk(1536 + 256 * n, [pt[:, 2 * n], pt[:, 2 * n + 1]]) for n in range(7)]
            proj_stage(C, "ab", V("mix_norm0"), io["ab_w_in"], plan)
            diff_attention(C, qkv, qt, kt, v, V("lam"), V("subln"), C.mixed)
        C.load([(w2a2[0:64], io["rwkv_w2"]), (w2a2[64:P], io["rwkv_a2"]), (g2, io["rwkv_g2"])])
        vec = {n: V(n) for n in ("mu", "w0", "a0", "kk", "ka", "rk", "lnw", "lnb")}
        rwkv(C, ctx, pt, vec, w2a2, w2a2, g2, C.mixed)
    out_stage(C, "ab_out", io["ab_w_out"], C.mixed)


def first_mixers_odd(C, V, io):
    with ExitStack() as ctx:
        qk, og, vm = C.sb(ctx, "qk", [P, 4, T]), C.sb(ctx, "og", [P, 4, T]), C.sb(ctx, "vm", [P, NCH, 512])
        li, lf = C.sb(ctx, "li", [4, T]), C.sb(ctx, "lf", [4, T])
        qt, kc, vc, ks, kw = (C.sb(ctx, n, [P, k, T]) for n, k in (("qt", 4), ("kc", 1), ("vc", 1), ("ks", 1), ("kw", 1)))
        vs, vw = C.sb(ctx, "vs", [P, NCH, P]), C.sb(ctx, "vw", [P, NCH, P])
        gates = C.sb(ctx, "gates", [P, NCH, 24])
        c_q, c_kc, c_vc, c_ks, c_vs, c_kw, c_vw, c_g, d_q, d_k, d_v, d_i, d_f, d_o = starts((512, 128, 128, 128, 128, 128, 128, 24, 256, 256, 512, 4, 4, 512))

        plan = [([(c_q + 256 * o + 64 * (2 * n + m), 64) for m in range(2) for o in range(2)], [(cols(m * P, m * P + P), None, qt[:, 2 * n + m]) for m in range(2)]) for n in range(2)]
        plan += [t_chunk(c_kc, [kc[:, 0], vc[:, 0]])]
        plan += [([(c_ks, 128), (c_kw, 128)], [(cols(0, P), None, ks[:, 0]), (cols(P, 2 * P), None, kw[:, 0])])]
        plan += [([(c_vs, 128), (c_vw, 128)], [(cols(o * P, o * P + P), c, z[:, c]) for o, z in ((0, vs), (1, vw)) for c in range(NCH)])]
        plan += [row_chunk(c_g, 24, [gates[:, c] for c in range(NCH)])]
        plan += [t_chunk(d_q, [qk[:, 0], qk[:, 1]]), t_chunk(d_k, [qk[:, 2], qk[:, 3]])]
        plan += [row_chunk(d_v + 256 * n, 256, [vm[:, c, 256 * n:256 * n + 256] for c in range(NCH)]) for n in range(2)]
        plan += [([(d_i, 8)], [(cols(0, 4), None, li[:, :]), (cols(4, 8), None, lf[:, :])])]
        plan += [t_chunk(d_o + 256 * n, [og[:, 2 * n], og[:, 2 * n + 1]]) for n in range(2)]
        proj_stage(C, "cd", V("mix_norm1"), io["cd_w_in"], plan)
        weights = [(io["nsa_w1_" + kind], io["nsa_w2_" + kind], V("pe_" + kind)) for kind in "kv"]
        sparse_attention(C, ctx, qt, kc[:, 0], vc[:, 0], ks[:, 0], vs, kw[:, 0], vw, gates, weights, C.mixed)
        mlstm(C, ctx, qk, vm, li[:, :], lf[:, :], og[:, :, :], V("mlstm_taps"), V("mlstm_bias"), V("ig_b")[0:4], V("fg_b")[0:4], V("mlstm_norm"), C.mixed)
    out_stage(C, "cd_out", io["cd_w_out"], C.mixed)


def second_mixers(C, V, io, layer, lb):
    L = str(layer)
    with ExitStack() as ctx:
        qkv, z = C.sb(ctx, "qkv", [P, 6, T]), C.sb(ctx, "z", [P, 2, T])
        beta, alpha = C.sb(ctx, "beta", [4, T]), C.sb(ctx, "alpha", [4, T])
        with ExitStack() as inner:
            aq, af, ag, bg, cq = (C.sb(inner, n, [P, 2, T]) for n in ("aq", "af", "ag", "bg", "cq"))
            bq, bk, ckv = (C.sb(inner, n, [P, 1, T]) for n in ("bq", "bk", "ckv"))
            kr, code = C.sb(inner, "kr", [P, T]), C.sb(inner, "code", [16, T])
            av, bv = C.sb(inner, "av", [P, NCH, 256]), C.sb(inner, "bv", [P, NCH, 256])
            w_gk2, w_uq, w_ukv = C.sb(inner, "w_gk2", [16, P]), C.sb(inner, "w_uq", [P, 2, 384]), C.sb(inner, "w_ukv", [P, 512])
            s = starts((256, 256, 256, 256, 128, 128, 256, 16, 256, 256, 128, 32, 256, 256, 256, 4, 4, 256))
            plan = [t_chunk(s[n], [d[:, 0], d[:, 1]]) for n, d in ((0, aq), (1, af), (3, ag))]
            plan += [row_chunk(s[2], 256, [av[:, c] for c in range(NCH)]), t_chunk(s[4], [bq[:, 0], bk[:, 0]]), row_chunk(s[6], 256, [bv[:, c] for c in range(NCH)])]
            plan += [([(s[7], 16)], [(cols(0, 16), None, code[:, :])]), t_chunk(s[8], [bg[:, 0], bg[:, 1]]), t_chunk(s[9], [cq[:, 0], cq[:, 1]])]
            plan += [([(s[10], 160)], [(cols(0, P), None, ckv[:, 0]), (cols(P, P + 32), None, kr[64:96], 64)])]
            plan += [t_chunk(s[12 + n], [qkv[:, 2 * n], qkv[:, 2 * n + 1]]) for n in range(3)]
            plan += [([(s[15], 8)], [(cols(0, 4), None, beta[:, :]), (cols(4, 8), None, alpha[:, :])]), t_chunk(s[17], [z[:, 0], z[:, 1]])]
            proj_stage(C, "in" + L, V("pre_mix_g" + L), io["w_in_2"][layer], plan)
            C.load([(w_gk2, io["gla_w_gk2_2"][layer]), (w_ukv, io["mla_w_ukv_2"][layer]), (w_uq, io["mla_w_uq_2"][layer].rearrange("(a p) f -> p a f", p=P))])
            with ExitStack() as one:
                hgrn(C, one, "hgrn" + L, aq[:, :, :], af[:, :, :], av, ag[:, :, :], lb, V("hgrn_norm_g" + L), C.mixed[:, 0:2])
            with ExitStack() as one:
                gla(C, one, "gla" + L, bq[:, :, :], bk[:, :, :], bv, code[:, :], bg[:, :, :], w_gk2[:, :], V("gla_b" + L), V("gla_norm_g" + L), C.mixed[:, 2:4])
            with ExitStack() as one:
                mla(C, one, "mla" + L, cq[:, :, :], ckv[:, :, :], kr[:, :], V("mla_q_norm" + L), V("mla_kv_norm" + L), w_uq, w_ukv[:, :], C.mixed[:, 4:6])
        gated_delta(C, ctx, "gdn" + L, qkv, z[:, :, :], beta[:, :], alpha[:, :], V("gdn_taps" + L), V("gdn_a_log" + L)[0:4], V("gdn_dt" + L)[0:4], V("gdn_norm_g" + L), C.mixed[:, 6:8])
    out_stage(C, "mix_out" + L, io["w_out_2"][layer], C.mixed, C.h)
    norm_stage(C, "mix_post" + L, C.h, V("post_mix_g" + L), True)


def build_program(nc, io, vectors, upto=99):
    with ExitStack() as ctx:
        C = Core(nc, ctx)
        vecs = C.sb(ctx, "vecs", [P, vectors.width])
        lb = C.sb(ctx, "lb", [P, 2])
        C.setup(io["consts"], io["x_t"])
        C.load([(vecs, io["vecs"])])

        def V(name):
            return vectors.view(vecs, name)

        for layer in range(2):
            if upto <= layer * 3:
                break
            ffn_stage(C, f"ffa{layer}", V(f"ffa_norm{layer}"), io["ffa_gate"][layer], io["ffa_up"][layer], io["ffa_down"][layer], 0.5)
            if upto <= layer * 3 + 1:
                break
            (first_mixers_even, first_mixers_odd)[layer](C, V, io)
            if upto <= layer * 3 + 2:
                break
            ffn_stage(C, f"ffb{layer}", V(f"ffb_norm{layer}"), io["ffb_gate"][layer], io["ffb_up"][layer], io["ffb_down"][layer], 0.5)
        if upto > 6:
            norm_stage(C, "final", C.x, V("final_norm"), False)
            lower_bound_stage(C, "bounds", V("lb_logits"), lb[:, :])
            for layer in range(2):
                second_mixers(C, V, io, layer, lb[:, :] if layer else None)
                ffn_stage(C, f"ffn{layer}", V(f"pre_ffn_g{layer}"), io["ffn_w_gate_2"][layer], io["ffn_w_up_2"][layer], io["ffn_w_down_2"][layer], 1.0,
                          taps=V(f"ffn_taps{layer}"), out=C.mixed)
                norm_stage(C, f"ffn_post{layer}", C.mixed, V(f"post_ffn_g{layer}"), True)
                if upto <= 7 + layer:
                    break
        C.dump(io["out"], C.x)


WEIGHTS = ("ffa_gate", "ffa_up", "ffa_down", "ffb_gate", "ffb_up", "ffb_down", "w_in_2", "w_out_2", "ffn_w_gate_2", "ffn_w_up_2", "ffn_w_down_2",
           "gla_w_gk2_2", "mla_w_ukv_2", "mla_w_uq_2")
ONE_LAYER = ("ab_w_in", "ab_w_out", "rwkv_w2", "rwkv_a2", "rwkv_g2", "cd_w_in", "cd_w_out", "nsa_w1_k", "nsa_w2_k", "nsa_w1_v", "nsa_w2_v")


def launch_arrays(inputs):
    arrays = {n: np.ascontiguousarray(inputs[n]) for n in WEIGHTS}
    arrays.update({n: np.ascontiguousarray(inputs[n][0]) for n in ONE_LAYER})
    arrays["x_t"] = np.ascontiguousarray(np.asarray(inputs["x"])[0].T.reshape(KT, P, T).transpose(1, 0, 2))
    arrays["consts"] = const_arrays()
    vectors = Vectors()
    parts = vector_arrays(inputs)
    for name, (shape, a) in parts.items():
        vectors.add(name, shape)
    arrays["vecs"] = np.ascontiguousarray(np.concatenate([a for _, a in parts.values()], 1))
    return arrays, vectors


def kernel(**inputs):
    import concourse.bacc as bacc
    from concourse.bass_utils import run_bass_kernel_spmd

    nc = bacc.Bacc("TRN2", target_bir_lowering=False, num_devices=1)
    arrays, vectors = launch_arrays(inputs)
    io = {n: nc.dram_tensor("in_" + n, a.shape, F32, kind="ExternalInput").ap() for n, a in arrays.items()}
    io["out"] = nc.dram_tensor("out_0", (P, KT, T), F32, kind="ExternalOutput").ap()
    build_program(nc, io, vectors)
    r = run_bass_kernel_spmd(nc, [{"in_" + n: a for n, a in arrays.items()}], core_ids=[0])
    got = r.results[0]["out_0"]
    return np.ascontiguousarray(got.transpose(2, 1, 0).reshape(1, T, D))
```

```python
from contextlib import ExitStack, contextmanager

import numpy as np

import concourse.bass as bass
from concourse import mybir

F32 = mybir.dt.float32
I32 = mybir.dt.int32
F32R = mybir.dt.float32r
ALU = mybir.AluOpType
ACT = mybir.ActivationFunctionType
AX = mybir.AxisListType

P = 128
T = 512
D = 1024
KT = D // P
NCH = T // P
D_FF = 2816
FT = D_FF // P
EPS = 1e-6
HEAD = 64
CHUNK = 2048


class Core:

    def __init__(self, nc, ctx):
        self.nc = nc
        self.ctx = ctx
        self.n = 0
        self.streams = []
        self.loads = [0, 0]

    def sb(self, ctx, name, shape, dt=F32):
        self.n += 1
        return ctx.enter_context(self.nc.sbuf_tensor(f"{name}_{self.n}", shape, dt))

    @contextmanager
    def stage(self, name, signals):
        nc = self.nc
        self.n += 1
        sems = [nc.alloc_semaphore(f"{s}_{name}_{self.n}") for s in signals.split()]
        with ExitStack() as ctx:
            yield ctx, nc.Block(), sems
        nc.clear_and_free_semaphores(sems)
        nc.all_engine_barrier()


def chain(eng, sem):
    count = [0]

    def link(ins):
        count[0] += 1
        ins.then_inc(sem, 1)
        eng.wait_ge(sem, count[0])
        return ins

    return link


def three_products(nc, out, lhs, rhs, start, stop):
    (lhs_hi, lhs_lo), (rhs_hi, rhs_lo) = [[a.bitcast(F32R) for a in side] for side in (lhs, rhs)]
    nc.tensor.matmul(out, lhs_hi, rhs_hi, start=start, stop=False)
    nc.tensor.matmul(out, lhs_hi, rhs_lo, start=False, stop=False)
    return nc.tensor.matmul(out, lhs_lo, rhs_hi, start=False, stop=stop)


def high_part(nc, hi, a):
    return nc.vector.tensor_copy(hi.bitcast(F32R), a)


def low_part(nc, lo, a, hi):
    return nc.vector.tensor_tensor(lo.bitcast(F32R), a, hi, ALU.subtract)


class WeightChunks:
    signals = "high_done split_done weights_used"

    def __init__(self, C, ctx, sems, count):
        self.C, self.count = C, count
        self.high_done, self.split_done, self.weights_used = sems
        self.parts = C.sb(ctx, "weights", [P, 2, 2, CHUNK])
        self.before = list(C.loads)
        for u in range(2):
            C.loads[u] += (count - u + 1) // 2

    def load(self, sp, pair, u, src, first=False):
        if not first:
            sp.wait_ge(self.split_done, pair * 2 + u - 1)
        sp.dma_start(self.C.raw[:, u, 0:src.shape[1]], src).then_inc(self.C.raw_loaded[u], 16)

    def load_next(self, sp):
        sp.wait_ge(self.C.late, self.C.late_count)
        if self.C.streams:
            for u, src in enumerate(self.C.streams.pop(0)):
                sp.wait_ge(self.split_done, self.count - (self.count - 1 - u) % 2)
                sp.dma_start(self.C.raw[:, u, 0:src.shape[1]], src).then_inc(self.C.raw_loaded[u], 16)

    def high(self, act, pair, u, size, first=False):
        act.wait_ge(self.C.raw_loaded[u], pair * 16 + (self.before[u] + 1) * 16)
        if not first:
            act.wait_ge(self.weights_used, pair * 2 + u - 1)
        self.C.nc.scalar.activation(self.parts[:, u, 0, 0:size].bitcast(F32R), self.C.raw[:, u, 0:size], ACT.Copy).then_inc(self.high_done, 1)

    def low(self, dve, pair, u, size):
        dve.wait_ge(self.high_done, pair * 2 + u + 1)
        low_part(self.C.nc, self.parts[:, u, 1, 0:size], self.C.raw[:, u, 0:size], self.parts[:, u, 0, 0:size]).then_inc(self.split_done, 1)

    def wait(self, pe, pair, u):
        pe.wait_ge(self.split_done, pair * 2 + u + 1)

    def piece(self, u, a, b):
        return self.parts[:, u, 0, a:b], self.parts[:, u, 1, a:b]


class SquareSums:
    signals = "squared added"

    def __init__(self, C, sems, src, ready):
        self.C, self.src, self.ready = C, src, ready
        self.squared, self.added = sems

    def square(self, act, m):
        act.wait_ge(self.ready, m + 1)
        if m >= 3:
            act.wait_ge(self.added, m - 2)
        slot = 1 + (m + 1) % 2 if m else 0
        self.C.nc.scalar.activation(self.C.squares[:, slot], self.src[:, m], ACT.Square).then_inc(self.squared, 1)

    def pool(self, pool):
        s = self.C.squares
        for m in range(1, KT - 1):
            pool.wait_ge(self.squared, m + 1)
            if m >= 2:
                pool.wait_ge(self.added, m - 1)
            self.C.nc.gpsimd.tensor_tensor(s[:, 0], s[:, 0], s[:, 1 + (m + 1) % 2], ALU.add).then_inc(self.added, 1)


class Rstd:
    signals = "parts_added total_summed ln_done rstd_done"

    def __init__(self, C, ctx, sems, sums=None, bank=6):
        self.C, self.sums, self.bank = C, sums, bank
        self.parts_added, self.total_summed, self.ln_done, self.rstd_done = sems
        self.rstd = C.sb(ctx, "rstd", [P, T])
        self.early = C.sb(ctx, "early", [P, 1])

    def pe(self, pe):
        ones, squares, total = self.C.ones, self.C.squares, self.C.ps[:, self.bank]
        if self.sums:
            pe.wait_ge(self.sums.added, KT - 2)
            self.C.nc.tensor.matmul(total, ones, squares[:, 0], start=True, stop=False)
            pe.wait_ge(self.sums.squared, KT)
            self.C.nc.tensor.matmul(total, ones, squares[:, 1], start=False, stop=True).then_inc(self.total_summed, 1)
        else:
            pe.wait_ge(self.parts_added, 1)
            self.C.nc.tensor.matmul(total, ones, squares[:, 0], start=True, stop=True).then_inc(self.total_summed, 1)

    def dve(self, dve):
        squares = self.C.squares
        self.C.nc.vector.tensor_tensor(squares[:, 0], squares[:, 0], squares[:, 1], ALU.add).then_inc(self.parts_added, 1)

    def act(self, act):
        self.C.nc.scalar.activation(self.early[:, :], self.C.eps, ACT.Ln)
        act.wait_ge(self.total_summed, 1)
        self.C.nc.scalar.activation(self.rstd[:, :], self.C.ps[:, self.bank], ACT.Ln, bias=self.C.eps, scale=1.0 / D).then_inc(self.ln_done, 1)
        act.wait_ge(self.ln_done, 1)
        self.C.nc.scalar.activation(self.rstd[:, :], self.rstd[:, :], ACT.Exp, scale=-0.5).then_inc(self.rstd_done, 1)


class Activations:
    signals = "raw_done high_done_h h_done"

    def __init__(self, C, ctx, sems):
        self.C = C
        self.raw_done, self.high_done, self.done = sems
        self.hi, self.lo = C.sb(ctx, "act_high", [P, KT, T]), C.sb(ctx, "act_low", [P, KT, T])

    def dve(self, dve, raw_of, make=None):

        def low(k):
            dve.wait_ge(self.high_done, k + 1)
            low_part(self.C.nc, self.lo[:, k], raw_of(k), self.hi[:, k]).then_inc(self.done, 1)

        for k in range(KT):
            if make:
                if k >= 2:
                    dve.wait_ge(self.done, k - 1)
                make(k).then_inc(self.raw_done, 1)
                if k:
                    low(k - 1)
                dve.wait_ge(self.raw_done, k + 1)
                high_part(self.C.nc, self.hi[:, k], raw_of(k)).then_inc(self.high_done, 1)
            else:
                high_part(self.C.nc, self.hi[:, k], raw_of(k)).then_inc(self.high_done, 1)
                if k:
                    low(k - 1)
        low(KT - 1)

    def dve_norm(self, dve, norm, rstd):
        C = self.C

        def raw_of(k):
            return C.squares[:, 2 * (k % 2)]

        dve.wait_ge(rstd.rstd_done, 1)
        self.dve(dve, raw_of, lambda k: C.nc.vector.scalar_tensor_tensor(raw_of(k), C.x[:, k], norm[:, k:k + 1], rstd.rstd[:, :], ALU.mult, ALU.mult))

    def tile(self, k, columns=slice(0, T)):
        return self.hi[:, k, columns], self.lo[:, k, columns]


class Finish:
    signals = "updated post_link renormed squared added post_parts_added post_total_summed post_ln_done post_rstd_done squared_x added_x"

    def __init__(self, C, ctx, sems, post, scale):
        self.C, self.post, self.scale = C, post, scale
        self.updated, self.post_link, self.renormed = sems[0:3]
        self.y = post[2] if post and post[0] == "add" else C.x
        self.sums = SquareSums(C, sems[3:5], self.y, self.updated)
        self.last = self.sums
        if post:
            self.rstd = Rstd(C, ctx, sems[5:9], self.sums)
            self.last = SquareSums(C, sems[9:11], C.x, self.renormed)

    def update(self, m, bank, first):
        nc, y = self.C.nc, self.y[:, m]
        if self.y is not self.C.x and first:
            return nc.vector.tensor_copy(y, bank)
        return nc.vector.scalar_tensor_tensor(y, bank, self.scale, y, ALU.mult, ALU.add)

    def dve(self, dve):
        if not self.post:
            return
        nc, x, y, w, rstd = self.C.nc, self.C.x, self.y, self.post[1], self.rstd.rstd[:, :]
        dve.wait_ge(self.rstd.rstd_done, 1)
        add = self.post[0] == "add"
        for m in range(KT):
            ins = nc.vector.scalar_tensor_tensor(y[:, m], y[:, m], w[:, m:m + 1], rstd, ALU.mult, ALU.mult)
            ins.then_inc(self.post_link if add else self.renormed, 1)
            if add:
                dve.wait_ge(self.post_link, m + 1)
                nc.vector.tensor_tensor(x[:, m], x[:, m], y[:, m], ALU.add).then_inc(self.renormed, 1)

    def square(self, act, m):
        self.sums.square(act, m)

    def act(self, act):
        if self.post:
            self.rstd.act(act)
            for m in range(KT):
                self.last.square(act, m)

    def pe(self, pe):
        if self.post:
            self.rstd.pe(pe)

    def pool(self, pool):
        self.sums.pool(pool)
        if self.post:
            pool.wait_ge(self.rstd.rstd_done, 1)
            self.last.pool(pool)


FFN_HALVES = (12, FT - 12)


def ffn_arrays(name, gate, up, down):
    g, u = (a.reshape(KT, P, FT, P).transpose(2, 1, 0, 3) for a in (gate, up))
    arrays = {name + "_gates": np.stack([g, u], 2).reshape(FT, P, CHUNK)}
    first = 0
    for half, tiles in enumerate(FFN_HALVES):
        d = down[first * P:(first + tiles) * P].reshape(tiles, P, KT, P).transpose(2, 1, 0, 3)
        arrays[f"{name}_down{half}"] = d.reshape(KT, P, tiles * P)
        first += tiles
    return arrays


def ffn_stage(C, name, norm, io, scale, taps=None, post=None):
    nc, x, ps = C.nc, C.x, C.ps
    gates = io[name + "_gates"]
    downs = [io[f"{name}_down{half}"] for half in range(2)]
    signals = " ".join((WeightChunks.signals, Rstd.signals, Activations.signals, "conv_link conv_done silu_done product_done high_part_done act_done half_updated", Finish.signals))
    with C.stage(name, signals) as (ctx, blk, sems):
        conv_link, conv_done, silu_done, product_done, high_part_done, act_done, half_updated = sems[10:17]
        chunks = WeightChunks(C, ctx, sems[0:3], FT + 2 * KT)
        rstd = Rstd(C, ctx, sems[3:7])
        h = Activations(C, ctx, sems[7:10])
        hidden = C.sb(ctx, "hidden", [P, 2, FFN_HALVES[0], T])
        silu = C.sb(ctx, "silu", [P, 2, T])
        if taps is not None:
            conv = C.sb(ctx, "conv", [P, 2, T])
        if post and post[0] == "add":
            post = (*post, C.sb(ctx, "y", [P, KT, T]))
        finish = Finish(C, ctx, sems[17:], post, scale)
        GATE, UP, OUT = (0, 1), (2, 3), (4, 5)
        block = ctx.enter_context(blk)
        halves = ((0, 0, FFN_HALVES[0]), (FFN_HALVES[0] // 2 + KT // 2, FFN_HALVES[0], FFN_HALVES[1]))
        down_pair = [pair + tiles // 2 for pair, _, tiles in halves]

        @block.sync
        def _(sp):
            for half, (pair, tile, tiles) in enumerate(halves):
                with sp.Fori(0 if half else 1, tiles // 2) as i:
                    for u in range(2):
                        chunks.load(sp, i + pair, u, gates[i * 2 + (tile + u)])
                with sp.Fori(0, KT // 2) as i:
                    for u in range(2):
                        chunks.load(sp, i + down_pair[half], u, downs[half][i * 2 + u])
            chunks.load_next(sp)

        @block.scalar
        def _(act):
            chunks.high(act, 0, 0, CHUNK, first=True)
            rstd.act(act)

            def silu_tile(pair, t, u, first=False):
                act.wait_ge(chunks.weights_used if taps is None else conv_done, (pair * 2 + u + 1) if taps is None else t + 1)
                if not first:
                    act.wait_ge(act_done, t - 1)
                if taps is None:
                    nc.scalar.activation(silu[:, u], ps[:, GATE[u]], ACT.Silu).then_inc(silu_done, 1)
                else:
                    nc.scalar.activation(silu[:, u], conv[:, u], ACT.Gelu_apprx_tanh).then_inc(silu_done, 1)

            def steps(pair, size, next_size, work, first=False):
                for u in range(2):
                    if u == 0:
                        chunks.high(act, pair, 1, size, first)
                    elif next_size:
                        chunks.high(act, pair + 1, 0, next_size)
                    work(u)

            for half, (pair, tile, tiles) in enumerate(halves):
                def gate_steps(i, next_size, first=False):
                    steps(i + pair, CHUNK, next_size, lambda u: silu_tile(i + pair, i * 2 + (tile + u), u, first), first)

                if half == 0:
                    gate_steps(0, CHUNK, first=True)
                with act.Fori(1 - half, tiles // 2 - 1) as i:
                    gate_steps(i, CHUNK)
                gate_steps(tiles // 2 - 1, tiles * P)
                if half == 0:
                    with act.Fori(0, KT // 2 - 1) as i:
                        steps(i + down_pair[0], tiles * P, tiles * P, lambda u: None)
                    steps(down_pair[0] + KT // 2 - 1, tiles * P, CHUNK, lambda u: None)
            for n in range(KT // 2):
                steps(down_pair[1] + n, FFN_HALVES[1] * P, FFN_HALVES[1] * P if n < KT // 2 - 1 else 0, lambda u: finish.square(act, n * 2 + u))
            finish.act(act)

        @block.tensor
        def _(pe):
            rstd.pe(pe)

            def gate_tile(pair, t, u, first=False):
                chunks.wait(pe, pair, u)
                if not first:
                    pe.wait_ge(product_done, t - 1)
                for k in range(KT):
                    if first and u == 0:
                        pe.wait_ge(h.done, k + 1)
                    for w, bank in ((0, GATE[u]), (1, UP[u])):
                        at = (w * KT + k) * P
                        mm = three_products(nc, ps[:, bank], chunks.piece(u, at, at + P), h.tile(k), k == 0, k == KT - 1)
                mm.then_inc(chunks.weights_used, 1)

            def down_tile(half, pair, m, u, first=False):
                tiles = FFN_HALVES[half]
                chunks.wait(pe, pair, u)
                if not first:
                    pe.wait_ge((half_updated, finish.updated)[half], m - 1)
                elif half == 1:
                    pe.wait_ge(half_updated, KT - 1 + u)
                for f in range(tiles):
                    if first and u == 0:
                        pe.wait_ge(act_done, halves[half][1] + f + 1)
                    mm = three_products(nc, ps[:, OUT[u]], chunks.piece(u, f * P, f * P + P), (hidden[:, 0, f], hidden[:, 1, f]), f == 0, f == tiles - 1)
                mm.then_inc(chunks.weights_used, 1)

            for half, (pair, tile, tiles) in enumerate(halves):
                if half == 0:
                    for u in range(2):
                        gate_tile(0, u, u, first=True)
                with pe.Fori(1 - half, tiles // 2) as i:
                    for u in range(2):
                        gate_tile(i + pair, i * 2 + (tile + u), u)
                for u in range(2):
                    down_tile(half, down_pair[half], u, u, first=True)
                with pe.Fori(1, KT // 2) as i:
                    for u in range(2):
                        down_tile(half, i + down_pair[half], i * 2 + u, u)
            finish.pe(pe)

        @block.vector
        def _(dve):
            rstd.dve(dve)
            chunks.low(dve, 0, 0, CHUNK)
            h.dve_norm(dve, norm, rstd)

            def hidden_tile(pair, t, f, u):
                product, hi = silu[:, u], hidden[:, 0, f]
                if taps is not None:
                    y, gate = conv[:, u], ps[:, GATE[u]]
                    dve.wait_ge(chunks.weights_used, pair * 2 + u + 1)
                    nc.vector.tensor_scalar(y, gate, taps[:, t, 2:3], None, ALU.mult).then_inc(conv_link, 1)
                    dve.wait_ge(conv_link, t * 2 + 1)
                    nc.vector.scalar_tensor_tensor(y[:, 1:T], gate[:, 0:T - 1], taps[:, t, 1:2], y[:, 1:T], ALU.mult, ALU.add).then_inc(conv_link, 1)
                    dve.wait_ge(conv_link, t * 2 + 2)
                    nc.vector.scalar_tensor_tensor(y[:, 2:T], gate[:, 0:T - 2], taps[:, t, 0:1], y[:, 2:T], ALU.mult, ALU.add).then_inc(conv_done, 1)
                dve.wait_ge(silu_done, t + 1)
                nc.vector.tensor_tensor(product, product, ps[:, UP[u]], ALU.mult).then_inc(product_done, 1)
                dve.wait_ge(product_done, t + 1)
                high_part(nc, hi, product).then_inc(high_part_done, 1)
                dve.wait_ge(high_part_done, t + 1)
                low_part(nc, hidden[:, 1, f], product, hi).then_inc(act_done, 1)

            def down_tile(half, pair, m, u):
                dve.wait_ge(chunks.weights_used, pair * 2 + u + 1)
                finish.update(m, ps[:, OUT[u]], half == 0).then_inc((half_updated, finish.updated)[half], 1)

            def steps(pair, size, next_size, work):
                for u in range(2):
                    if u == 0:
                        chunks.low(dve, pair, 1, size)
                    elif next_size:
                        chunks.low(dve, pair + 1, 0, next_size)
                    work(u)

            for half, (pair, tile, tiles) in enumerate(halves):
                def gate_steps(i, next_size):
                    steps(i + pair, CHUNK, next_size, lambda u: hidden_tile(i + pair, i * 2 + (tile + u), i * 2 + u, u))

                def down_steps(i, next_size):
                    steps(i + down_pair[half], tiles * P, next_size, lambda u: down_tile(half, i + down_pair[half], i * 2 + u, u))

                with dve.Fori(0, tiles // 2 - 1) as i:
                    gate_steps(i, CHUNK)
                gate_steps(tiles // 2 - 1, tiles * P)
                with dve.Fori(0, KT // 2 - 1) as i:
                    down_steps(i, tiles * P)
                down_steps(KT // 2 - 1, 0 if half else CHUNK)
            finish.dve(dve)

        @block.gpsimd
        def _(pool):
            finish.pool(pool)


def proj_arrays(name, w, pieces_of):
    w = w.reshape(KT, P, -1).transpose(1, 0, 2)
    return {name: np.concatenate([np.concatenate([w[:, :, a:a + n] for a, n in pieces], 2).ravel() for pieces in pieces_of])}


def proj_chunks(flat, pieces_of):
    views, at = [], 0
    for pieces in pieces_of:
        size = KT * sum(n for _, n in pieces)
        views.append(flat[at:at + P * size].rearrange("(p n) -> p n", p=P))
        at += P * size
    return views


def proj_stage(C, name, norm, flat, plan, beside=()):
    nc, x, ps = C.nc, C.x, C.ps
    BANKS = 6
    views = proj_chunks(flat, [pieces for pieces, _ in plan])
    sums = []
    last_of = []
    for n, (pieces, outs) in enumerate(plan):
        sums += [(n, *out, *(() if len(out) == 4 else (0,))) for out in outs]
        last_of.append(len(sums) - 1)
    with C.stage(name, " ".join((WeightChunks.signals, Rstd.signals, Activations.signals, "summed copied beside_loaded"))) as (ctx, blk, sems):
        summed, copied, beside_loaded = sems[10:]
        chunks = WeightChunks(C, ctx, sems[0:3], len(plan))
        rstd = Rstd(C, ctx, sems[3:7])
        h = Activations(C, ctx, sems[7:10])
        block = ctx.enter_context(blk)

        def source(s):
            dest, first = sums[s][3:]
            return ps[first:first + dest.shape[0], s % BANKS, 0:dest.shape[1]]

        @block.sync
        def _(sp):
            for dst, src in beside:
                sp.dma_start(dst[:], src).then_inc(beside_loaded, 16)
            for n in range(2, len(plan)):
                chunks.load(sp, n // 2, n % 2, views[n])
            chunks.load_next(sp)
            if beside:
                sp.wait_ge(beside_loaded, 16 * len(beside))

        @block.tensor
        def _(pe):
            rstd.pe(pe)
            for s, (n, (a, b), c, dest, first) in enumerate(sums):
                chunks.wait(pe, n // 2, n % 2)
                if s >= BANKS:
                    pe.wait_ge(copied, s - BANKS + 1)
                width = views[n].shape[1] // KT
                for k in range(KT):
                    if s == 0:
                        pe.wait_ge(h.done, k + 1)
                    weights = chunks.piece(n % 2, k * width + a, k * width + b)
                    tile = h.tile(k) if c is None else h.tile(k, slice(c * P, (c + 1) * P))
                    lhs, rhs = (weights, tile) if c is None else (tile, weights)
                    mm = three_products(nc, ps[0:first + dest.shape[0], s % BANKS, 0:dest.shape[1]], lhs, rhs, k == 0, k == KT - 1)
                mm.then_inc(summed, 1)

        @block.scalar
        def _(act):
            chunks.high(act, 0, 0, views[0].shape[1], first=True)
            rstd.act(act)
            for n in range(len(plan)):
                if n + 1 < len(plan):
                    if n >= 1:
                        act.wait_ge(summed, last_of[n - 1] + 1)
                    chunks.high(act, (n + 1) // 2, (n + 1) % 2, views[n + 1].shape[1], first=True)
                for s in range(last_of[n] - len(plan[n][1]) + 1, last_of[n] + 1):
                    act.wait_ge(summed, s + 1)
                    nc.scalar.activation(sums[s][3], source(s), ACT.Copy).then_inc(copied, 1)

        @block.vector
        def _(dve):
            rstd.dve(dve)
            chunks.low(dve, 0, 0, views[0].shape[1])
            h.dve_norm(dve, norm, rstd)
            for n in range(1, len(plan)):
                chunks.low(dve, n // 2, n % 2, views[n].shape[1])


def t_outs(dests):
    return [((i * P, (i + 1) * P), None, d) for i, d in enumerate(dests)]


def row_outs(width, dests):
    return [((0, width), c, d) for c, d in enumerate(dests)]


def out_arrays(name, w):
    return {name: w.reshape(KT, P, 4, 2, P).transpose(2, 1, 3, 0, 4).reshape(4, P, CHUNK)}


def out_stage(C, name, w, mixed, post=False):
    nc, ps = C.nc, C.ps
    with C.stage(name, " ".join((WeightChunks.signals, Activations.signals, Finish.signals))) as (ctx, blk, sems):
        chunks = WeightChunks(C, ctx, sems[0:3], KT // 2)
        if post:
            post = ("add", post, C.sb(ctx, "y", [P, KT, T]))
        finish = Finish(C, ctx, sems[6:], post or None, 1.0)
        acts = Activations(C, ctx, sems[3:6])
        BANKS = 4
        block = ctx.enter_context(blk)

        @block.sync
        def _(sp):
            for n in range(2, KT // 2):
                chunks.load(sp, n // 2, n % 2, w[n])
            chunks.load_next(sp)

        @block.tensor
        def _(pe):
            for n in range(KT // 2):
                chunks.wait(pe, n // 2, n % 2)
                if n >= 2:
                    pe.wait_ge(finish.updated, n * 2 - 2)
                for k in range(KT):
                    if n == 0:
                        pe.wait_ge(acts.done, k + 1)
                    for o in range(2):
                        at = (o * KT + k) * P
                        mm = three_products(nc, ps[:, (n * 2 + o) % BANKS], chunks.piece(n % 2, at, at + P), acts.tile(k), k == 0, k == KT - 1)
                mm.then_inc(chunks.weights_used, 1)
            finish.pe(pe)

        @block.scalar
        def _(act):
            chunks.high(act, 0, 0, CHUNK, first=True)
            for n in range(KT // 2):
                if n + 1 < KT // 2:
                    chunks.high(act, (n + 1) // 2, (n + 1) % 2, CHUNK, first=n == 0)
                for o in range(2):
                    finish.square(act, n * 2 + o)
            finish.act(act)

        @block.vector
        def _(dve):
            chunks.low(dve, 0, 0, CHUNK)
            acts.dve(dve, lambda k: mixed[:, k])
            for n in range(KT // 2):
                if n + 1 < KT // 2:
                    chunks.low(dve, (n + 1) // 2, (n + 1) % 2, CHUNK)
                dve.wait_ge(chunks.weights_used, n + 1)
                for o in range(2):
                    m = n * 2 + o
                    finish.update(m, ps[:, m % BANKS], True).then_inc(finish.updated, 1)
            finish.dve(dve)

        @block.gpsimd
        def _(pool):
            finish.pool(pool)


CONSTS = {}
ROPE_THETA = 10000.0


def rotation(n, width, first):
    m = np.zeros((n, n), np.float32)
    half = width // 2
    last = n if first == 0 else first + width
    for r in range(first, last):
        if (r - first) % width < half:
            m[r + half, r] = -1.0
        else:
            m[r - half, r] = 1.0
    return m


def level(n):
    b = np.arange(P) >> n
    return ((b[None, :] % 2 == 1) & (b[:, None] == b[None, :] - 1)) * 1.0


def rope(dim, first):
    inv = np.float32(ROPE_THETA) ** (-np.arange(0, dim, 2, dtype=np.float32) / np.float32(dim))
    ang = np.arange(T, dtype=np.float32)[None, :] * inv.astype(np.float32)[:, None]
    cos, sin = np.ones((P, T), np.float32), np.zeros((P, T), np.float32)
    for r in range(first, P if first == 0 else first + dim):
        a = ang[(r - first) % (dim // 2)]
        cos[r], sin[r] = np.cos(a), np.sin(a)
    return cos, sin


def const_arrays():
    i = np.arange(P)
    parts = {"ones": np.ones((P, P)), "eps": np.full((P, 1), EPS), "tiny": np.full((P, 1), 1e-12), "gn_eps": np.full((P, 1), 64e-5),
             "one": np.ones((P, 1)), "ident": np.eye(P),
             "causal": np.where(i[None, :] <= i[:, None], 0.0, -1e30),
             "upper": (i[:, None] <= i[None, :]) * 1.0, "strict": (i[:, None] < i[None, :]) * 1.0,
             "pairs": (i[:, None] // 64 == i[None, :] // 64) * 1.0,
             "rot": rotation(P, 64, 0), "rot_mla": rotation(P, 32, 64),
             "cos": rope(HEAD, 0)[0], "sin": rope(HEAD, 0)[1], "cos_mla": rope(32, 64)[0], "sin_mla": rope(32, 64)[1],
             "levels": np.concatenate([level(n) for n in range(7)], 1),
             "run": np.broadcast_to(np.arange(T) % P != 0, (P, T)) * 1.0,
             "ones_t": np.ones((P, T)), "select": np.concatenate([(i[:, None] == n) * np.ones((P, P)) for n in range(4)], 1),
             "select_pair": np.concatenate([(i[:, None] == 2 * m + i[None, :] // 64) * 1.0 for m in range(2)], 1),
             "cmp_valid": (i[:, None] >= 31) * 1.0,
             "cmp_mask": np.concatenate([np.where(16 * np.arange(31)[None, :] + 31 <= (i + c * P)[:, None], 0.0, -1e30) for c in range(4)], 1),
             "quads": (i[:, None] // 32 == i[None, :] // 32) * 1.0}
    at = 0
    out = []
    for k, v in parts.items():
        v = np.ascontiguousarray(v, dtype=np.float32)
        CONSTS[k] = (at, v.shape[1])
        at += v.shape[1]
        out.append(v)
    return np.ascontiguousarray(np.concatenate(out, 1))


def setup(C, consts, x_t, vecs, vecs_in):
    nc = C.nc
    C.ps = C.ctx.enter_context(nc.psum_tensor("ps", [P, 8, T], F32))
    C.x = C.sb(C.ctx, "x", [P, KT, T])
    C.consts = C.sb(C.ctx, "consts", list(consts.shape))
    C.squares = C.sb(C.ctx, "squares", [P, 3, T])
    C.raw = C.sb(C.ctx, "raw", [P, 2, CHUNK])
    C.raw_loaded = [nc.alloc_semaphore(f"raw_loaded_{u}") for u in range(2)]

    def const(name):
        a, w = CONSTS[name]
        return C.consts[:, a:a + w]

    C.const = const
    C.ones, C.ident, C.eps = const("ones"), const("ident"), const("eps")
    a = CONSTS["upper"][0]
    C.mask_pair = C.consts[:, a:a + 2 * P]
    C.late = nc.alloc_semaphore("tables_loaded")
    C.late_count = 16
    head = CONSTS["ident"][0]
    with C.stage("setup", "small_loaded x_loaded_0 x_loaded_1 x_loaded_2 x_loaded_3 x_ready squared added") as (ctx, blk, sems):
        small_loaded, *x_loaded = sems[0:5]
        x_ready = sems[5]
        sums = SquareSums(C, sems[6:8], C.x, x_ready)
        block = ctx.enter_context(blk)

        @block.sync
        def _(sp):
            for n, loaded in enumerate(x_loaded):
                sp.dma_start(C.x[:, 2 * n:2 * n + 2], x_t[:, 2 * n:2 * n + 2]).then_inc(loaded, 16)
            sp.dma_start(C.consts[:, 0:head], consts[:, 0:head]).then_inc(small_loaded, 16)
            sp.dma_start(vecs, vecs_in).then_inc(small_loaded, 16)
            for u, src in enumerate(C.streams.pop(0)):
                sp.dma_start(C.raw[:, u, 0:src.shape[1]], src).then_inc(C.raw_loaded[u], 16)
            sp.dma_start(C.consts[:, head:], consts[:, head:]).then_inc(C.late, 16)
            sp.wait_ge(small_loaded, 32)

        @block.scalar
        def _(act):
            for m in range(KT):
                act.wait_ge(x_loaded[m // 2], 16)
                act.sem_inc(x_ready, 1)
                sums.square(act, m)

        @block.gpsimd
        def _(pool):
            sums.pool(pool)


def store(C, out, src):
    with C.stage("store", "stored") as (ctx, blk, (stored,)):
        block = ctx.enter_context(blk)

        @block.sync
        def _(sp):
            sp.dma_start(out, src[:]).then_inc(stored, 16)
            sp.wait_ge(stored, 16)


Core.setup = setup
Core.store = store


def rope_stage(C, name, items):
    nc, ps = C.nc, C.ps
    BANKS = 4
    with C.stage(name, "rotated cos_done products_done rope_link") as (ctx, blk, (rotated, cos_done, products_done, rope_link)):
        by_cos = C.sb(ctx, "by_cos", [P, 2, T])
        by_sin = C.sb(ctx, "by_sin", [P, 2, T])
        block = ctx.enter_context(blk)

        @block.tensor
        def _(pe):
            for n, (tile, rot, cos, sin, scale) in enumerate(items):
                rows = tile.shape[0]
                if n >= BANKS:
                    pe.wait_ge(products_done, n - BANKS + 1)
                nc.tensor.matmul(ps[0:rows, n % BANKS], rot[0:rows, 0:rows], tile, start=True, stop=True).then_inc(rotated, 1)

        @block.vector
        def _(dve):
            link = chain(dve, rope_link)
            for n, (tile, rot, cos, sin, scale) in enumerate(items):
                rows = tile.shape[0]
                a, b = by_cos[0:rows, n % 2], by_sin[0:rows, n % 2]
                dve.wait_ge(rotated, n + 1)
                link(nc.vector.scalar_tensor_tensor(b, ps[0:rows, n % BANKS], scale, sin[0:rows], ALU.mult, ALU.mult))
                dve.wait_ge(cos_done, n + 1)
                nc.vector.scalar_tensor_tensor(tile, a, scale, b, ALU.mult, ALU.add).then_inc(products_done, 1)

        @block.gpsimd
        def _(pool):
            for n, (tile, rot, cos, sin, scale) in enumerate(items):
                rows = tile.shape[0]
                if n >= 2:
                    pool.wait_ge(products_done, n - 1)
                nc.gpsimd.tensor_tensor(by_cos[0:rows, n % 2], tile, cos[0:rows], ALU.mult).then_inc(cos_done, 1)


class Convolution:
    signals = "conv_link conv_done"

    def __init__(self, C, ctx, sems, items):
        self.C, self.items = C, items
        self.conv_link, self.conv_done = sems
        if items:
            self.acc = C.sb(ctx, "conv_acc", [P, len(items), T])
            self.product = C.sb(ctx, "conv_product", [P, T])

    def pool(self, pool):
        eng = self.C.nc.gpsimd
        link = chain(pool, self.conv_link)
        for n, (src, dst, taps, bias) in enumerate(self.items):
            y = self.acc[:, n]
            for d in range(len(taps)):
                to = self.product[:, d:T] if d else y
                link(eng.tensor_tensor(to, src[:, 0:T - d], taps[-1 - d].to_broadcast([P, T - d]), ALU.mult))
                if d:
                    ins = eng.tensor_tensor(y[:, d:T], y[:, d:T], to, ALU.add)
                    if d < len(taps) - 1:
                        link(ins)
                    else:
                        ins.then_inc(self.conv_done, 1)
                        pool.wait_ge(self.conv_done, n + 1)

    def act(self, act):
        for n, (src, dst, taps, bias) in enumerate(self.items):
            act.wait_ge(self.conv_done, n + 1)
            if bias is None:
                self.C.nc.scalar.activation(dst, self.acc[:, n], ACT.Silu)
            else:
                self.C.nc.scalar.activation(dst, self.acc[:, n], ACT.Silu, bias=bias)


def attention_stage(C, name, groups, conv=()):
    nc, ps = C.nc, C.ps
    S_BANKS, T_BANKS, O_BANKS = (0, 1, 2), (3, 4, 5), (6, 7)
    P_RING, T_RING = 4, 3
    units, joins = [], []
    for g, (sums, rows, dest, ob) in enumerate(groups):
        for i in range(NCH):
            for s, (maps, values) in enumerate(sums):
                for m, (q, k, mask, keys, coef) in enumerate(maps):
                    units.append((q[:, i * P:(i + 1) * P], k[:, 0:keys(i)], mask(i), keys(i), coef and coef(i), m, len(joins)))
                joins.append((g, i, s, len(sums), len(units), keys(i), values))
    with C.stage(name, "scores_done max_link max_done exp_done prob_link prob_done transposed copied values_done out_copied " + Convolution.signals) as (ctx, blk, sems):
        scores_done, max_link, max_done, exp_done, prob_link, prob_done, transposed, copied, values_done, out_copied = sems[:10]
        conv = Convolution(C, ctx, sems[10:], conv)
        probs = C.sb(ctx, "probs", [P, P_RING, T])
        probs_t = C.sb(ctx, "probs_t", [P, T_RING, T])
        negmax = C.sb(ctx, "negmax", [P, len(units)])
        denom = C.sb(ctx, "denom", [P, len(units)])
        block = ctx.enter_context(blk)

        def bank(u):
            return S_BANKS[u % len(S_BANKS)]

        @block.tensor
        def _(pe):
            def scores(u):
                q, k, mask, keys, coef, m, j = units[u]
                if u >= len(S_BANKS):
                    pe.wait_ge(exp_done, u - len(S_BANKS) + 1)
                nc.tensor.matmul(ps[:, bank(u), 0:keys], q, k, start=True, stop=True).then_inc(scores_done, 1)

            def turn(j):
                g, i, s, n_sums, end, keys, values = joins[j]
                pe.wait_ge(prob_done, j + 1)
                if j >= len(T_BANKS):
                    pe.wait_ge(copied, j - len(T_BANKS) + 1)
                for b in range((keys + P - 1) // P):
                    w = min(P, keys - b * P)
                    mm = nc.tensor.transpose(ps[0:w, T_BANKS[j % len(T_BANKS)], b * P:(b + 1) * P],
                                             probs[:, (end - 1) % P_RING, b * P:b * P + w], C.ident)
                mm.then_inc(transposed, 1)

            def value(j):
                g, i, s, n_sums, end, keys, values = joins[j]
                rows, ob = groups[g][1], O_BANKS[groups[g][3] % 2]
                pe.wait_ge(copied, j + 1)
                if i == 0 and s == 0 and groups[g][3] >= 2:
                    pe.wait_ge(out_copied, groups[g][3] - 1)
                nb = (keys + P - 1) // P
                for b in range(nb):
                    w = min(P, keys - b * P)
                    mm = nc.tensor.matmul(ps[rows, ob, i * P:(i + 1) * P], values(b), probs_t[0:w, j % T_RING, b * P:(b + 1) * P],
                                          start=s == 0 and b == 0, stop=s == n_sums - 1 and b == nb - 1)
                mm.then_inc(values_done, 1)

            sent_t = sent_v = 0
            for u in range(len(units) + 8):
                if u < len(units):
                    scores(u)
                while sent_t < len(joins) and joins[sent_t][4] <= u - 1:
                    turn(sent_t)
                    sent_t += 1
                while sent_v < len(joins) and joins[sent_v][4] <= u - 2 and sent_v < sent_t:
                    value(sent_v)
                    sent_v += 1

        @block.vector
        def _(dve):
            link_max, link = chain(dve, max_link), chain(dve, prob_link)

            def largest(u):
                q, k, mask, keys, coef, m, j = units[u]
                w = mask.shape[1]
                dve.wait_ge(scores_done, u + 1)
                last = ps[:, bank(u), keys - w:keys]
                link_max(nc.vector.tensor_tensor(last, last, mask, ALU.add))
                nc.vector.tensor_reduce(negmax[:, u:u + 1], ps[:, bank(u), 0:keys], AX.X, ALU.max, negate=True).then_inc(max_done, 1)

            def probability(u):
                q, k, mask, keys, coef, m, j = units[u]
                p = probs[:, u % P_RING, 0:keys]
                d = denom[:, u:u + 1]
                dve.wait_ge(exp_done, u + 1)
                link(nc.vector.reciprocal(d, d))
                if coef is not None:
                    link(nc.vector.tensor_tensor(d, d, coef, ALU.mult))
                if m == 0:
                    ins = nc.vector.tensor_scalar(p, p, d, None, ALU.mult)
                else:
                    ins = nc.vector.scalar_tensor_tensor(p, p, d, probs[:, (u - 1) % P_RING, 0:keys], ALU.mult, ALU.add)
                if joins[j][4] == u + 1:
                    ins.then_inc(prob_done, 1)
                else:
                    link(ins)

            for u in range(len(units) + 8):
                if u < len(units):
                    largest(u)
                if 1 <= u <= len(units):
                    probability(u - 1)

        @block.scalar
        def _(act):
            def exponent(u):
                q, k, mask, keys, coef, m, j = units[u]
                act.wait_ge(max_done, u + 1)
                if j >= 2:
                    done = max([n + 1 for n, x in enumerate(joins) if x[4] <= u - P_RING + 1] + [0])
                    if done:
                        act.wait_ge(transposed, done)
                nc.scalar.activation(probs[:, u % P_RING, 0:keys], ps[:, bank(u), 0:keys], ACT.Exp, bias=negmax[:, u:u + 1],
                                     accum_out=denom[:, u:u + 1]).then_inc(exp_done, 1)

            def copy(j):
                g, i, s, n_sums, end, keys, values = joins[j]
                w = min(P, keys)
                width = (keys + P - 1) // P * P
                act.wait_ge(transposed, j + 1)
                if j >= T_RING:
                    act.wait_ge(values_done, j - T_RING + 1)
                nc.scalar.activation(probs_t[0:w, j % T_RING, 0:width], ps[0:w, T_BANKS[j % len(T_BANKS)], 0:width], ACT.Copy).then_inc(copied, 1)

            sent = 0
            copied_banks = 0
            ends = [n + 1 for n, x in enumerate(joins) if x[1] == NCH - 1 and x[2] == x[3] - 1 and groups[x[0]][2] is not None]
            for u in range(len(units) + 12):
                if u < len(units):
                    exponent(u)
                while sent < len(joins) and joins[sent][4] <= u - 1:
                    copy(sent)
                    sent += 1
                while copied_banks < len(ends) and ends[copied_banks] <= sent and (joins[ends[copied_banks] - 1][4] <= u - 5 or u >= len(units)):
                    g = joins[ends[copied_banks] - 1][0]
                    act.wait_ge(values_done, ends[copied_banks])
                    dest, ob = groups[g][2], O_BANKS[groups[g][3] % 2]
                    nc.scalar.activation(dest, ps[0:dest.shape[0], ob], ACT.Copy).then_inc(out_copied, 1)
                    copied_banks += 1
            conv.act(act)

        @block.gpsimd
        def _(pool):
            conv.pool(pool)


def head_norm_stage(C, name, src, dst, mat, count, eps, weights, gates, scale=1.0):
    nc, ps = C.nc, C.ps
    n = src.shape[1]
    with C.stage(name, "squared summed logged rstd_done scaled") as (ctx, blk, (squared, summed, logged, rstd_done, scaled)):
        sq = C.sb(ctx, "sq", [P, n, T])
        block = ctx.enter_context(blk)

        @block.scalar
        def _(act):
            for m in range(n):
                nc.scalar.activation(sq[:, m], src[:, m], ACT.Square).then_inc(squared, 1)
            for m in range(n):
                act.wait_ge(summed, m + 1)
                nc.scalar.activation(sq[:, m], ps[:, m], ACT.Ln, bias=eps, scale=1.0 / count).then_inc(logged, 1)
            for m in range(n):
                act.wait_ge(logged, m + 1)
                nc.scalar.activation(sq[:, m], sq[:, m], ACT.Exp, scale=-0.5).then_inc(rstd_done, 1)

        @block.tensor
        def _(pe):
            for m in range(n):
                pe.wait_ge(squared, m + 1)
                nc.tensor.matmul(ps[:, m], mat, sq[:, m], start=True, stop=True).then_inc(summed, 1)

        @block.vector
        def _(dve):
            for m in range(n + 1):
                if m < n:
                    dve.wait_ge(rstd_done, m + 1)
                    nc.vector.scalar_tensor_tensor(sq[:, m], src[:, m], weights[:, m:m + 1], sq[:, m], ALU.mult, ALU.mult).then_inc(scaled, 1)
                if m:
                    dve.wait_ge(scaled, m)
                    if gates is not None:
                        nc.vector.tensor_tensor(dst[:, m - 1], sq[:, m - 1], gates[:, m - 1], ALU.mult)
                    else:
                        nc.vector.tensor_scalar(dst[:, m - 1], sq[:, m - 1], scale, None, ALU.mult)


def lambda_stage(C, lam, lam_init, lam_neg):
    nc = C.nc
    with C.stage("lambda", "multiplied lam_link exped") as (ctx, blk, (multiplied, lam_link, exped)):
        prod = C.sb(ctx, "prod", [P, 2, HEAD])
        s = C.sb(ctx, "s", [P, 2])
        block = ctx.enter_context(blk)

        @block.vector
        def _(dve):
            link = chain(dve, lam_link)
            link(nc.vector.tensor_tensor(prod[:, 0], lam[:, 0], lam[:, 1], ALU.mult))
            link(nc.vector.tensor_tensor(prod[:, 1], lam[:, 2], lam[:, 3], ALU.mult))
            nc.vector.tensor_reduce(s[:, :], prod[:, :, :], AX.X, ALU.add).then_inc(multiplied, 1)
            dve.wait_ge(exped, 1)
            link(nc.vector.tensor_tensor(lam_neg, s[:, 1:2], s[:, 0:1], ALU.subtract))
            link(nc.vector.tensor_scalar(lam_neg, lam_neg, -lam_init, None, ALU.add))

        @block.scalar
        def _(act):
            act.wait_ge(multiplied, 1)
            nc.scalar.activation(s[:, :], s[:, :], ACT.Exp).then_inc(exped, 1)


def diff_attention(C, ctx, qt, kt, v, lam, subln, mixed):
    lam_neg = C.sb(ctx, "lam_neg", [P, 1])
    lambda_stage(C, lam, 0.2, lam_neg[:, :])
    cos, sin, rot = C.const("cos"), C.const("sin"), C.const("rot")
    items = [(qt[:, n], rot, cos, sin, HEAD ** -0.5) for n in range(4)] + [(kt[:, n], rot, cos, sin, 1.0) for n in range(4)]
    rope_stage(C, "diff_rope", items)
    groups = []
    for hd in range(4):
        maps = [(qt[c * 64:c * 64 + 64, hd], kt[c * 64:c * 64 + 64, hd], lambda i: C.const("causal"), lambda i: (i + 1) * P,
                 (lambda i: lam_neg[:, 0:1]) if c else None) for c in range(2)]
        groups.append(([(maps, lambda j, hd=hd: v[:, j, hd * P:(hd + 1) * P])], slice(0, P), mixed[:, hd], hd))
    attention_stage(C, "diff_attn", groups)
    head_norm_stage(C, "diff_norm", mixed[:, 0:4], mixed[:, 0:4], C.ones, P, C.eps, subln, None, 0.8)


LEVELS = 7


def inverse_signals():
    return "level_masked y_summed y_copied x_summed xt_summed x_updated xt_updated start_turned"


class Inverse:

    def __init__(self, C, heads, sems, xt, x, y, masked):
        self.C, self.H, self.G = C, heads, heads // 4
        (self.level_masked, self.y_summed, self.y_copied, self.x_summed, self.xt_summed, self.x_updated,
         self.xt_updated, self.start_turned) = sems
        self.xts, self.x, self.y, self.masked = xt, x, y, masked

    def xt(self, c):
        return self.xts[c % len(self.xts)]

    def bank(self, which, g):
        a = which * self.G + g
        return self.C.ps[:, a].rearrange("p (h i) -> p h i", h=4)

    def level(self, n):
        return self.C.const("levels")[:, n * P:(n + 1) * P].unsqueeze(1).to_broadcast([P, self.H, P])

    def pool(self, eng, c, mt, ready, ready_value):
        eng.wait_ge(ready, ready_value)
        for n in range(1, LEVELS):
            done = (c * (LEVELS - 1) + n - 2) * self.G
            if done > 0:
                eng.wait_ge(self.y_summed, done)
            self.C.nc.gpsimd.tensor_tensor(self.masked[:, n % 2], mt, self.level(n), ALU.mult).then_inc(self.level_masked, 1)

    def dve_start(self, dve, link, c, mt):
        ident = self.C.ident.unsqueeze(1).to_broadcast([P, self.H, P])
        link(self.C.nc.vector.tensor_tensor(self.xt(c), mt, self.level(0), ALU.mult))
        self.C.nc.vector.tensor_tensor(self.xt(c), ident, self.xt(c), ALU.subtract).then_inc(self.xt_updated, 1)

    def pe(self, pe, c):
        nc = self.C.nc
        L = LEVELS - 1
        upd_xt = c * (L * self.G + 1) + 1
        pe.wait_ge(self.xt_updated, upd_xt)
        for g in range(self.G):
            for q in range(4):
                mm = nc.tensor.transpose(self.bank(1, g)[:, q], self.xt(c)[:, 4 * g + q], self.C.ident)
            mm.then_inc(self.start_turned, 1)
        for n in range(L):
            unit = (c * L + n) * self.G
            pe.wait_ge(self.level_masked, c * L + n + 1)
            for g in range(self.G):
                pe.wait_ge(self.x_updated, c * L * self.G + n * self.G + g + 1)
                for q in range(4):
                    h = 4 * g + q
                    mm = nc.tensor.matmul(self.bank(0, g)[:, q], self.masked[:, (n + 1) % 2, h], self.x[:, h], start=True, stop=True)
                mm.then_inc(self.y_summed, 1)
            for g in range(self.G):
                pe.wait_ge(self.y_copied, unit + g + 1)
                if n > 0:
                    pe.wait_ge(self.xt_updated, upd_xt + (n - 1) * self.G + g + 1)
                if n < L - 1:
                    for q in range(4):
                        h = 4 * g + q
                        mm = nc.tensor.matmul(self.bank(1, g)[:, q], self.xt(c)[:, h], self.y[:, h], start=True, stop=True)
                    mm.then_inc(self.x_summed, 1)
                for q in range(4):
                    h = 4 * g + q
                    mm = nc.tensor.matmul(self.bank(2, g)[:, q], self.y[:, h], self.xt(c)[:, h], start=True, stop=True)
                mm.then_inc(self.xt_summed, 1)

    def act(self, act, c):
        for n in range(LEVELS - 1):
            for g in range(self.G):
                unit = (c * (LEVELS - 1) + n) * self.G + g
                act.wait_ge(self.y_summed, unit + 1)
                self.C.nc.scalar.activation(self.y[:, 4 * g:4 * g + 4], self.bank(0, g), ACT.Copy).then_inc(self.y_copied, 1)

    def dve(self, dve, c):
        nc = self.C.nc
        L = LEVELS - 1
        for g in range(self.G):
            dve.wait_ge(self.start_turned, c * self.G + g + 1)
            nc.vector.tensor_copy(self.x[:, 4 * g:4 * g + 4], self.bank(1, g)).then_inc(self.x_updated, 1)
        for n in range(L):
            for g in range(self.G):
                hs = slice(4 * g, 4 * g + 4)
                if n < L - 1:
                    dve.wait_ge(self.x_summed, (c * (L - 1) + n) * self.G + g + 1)
                    nc.vector.tensor_tensor(self.x[:, hs], self.x[:, hs], self.bank(1, g), ALU.subtract).then_inc(self.x_updated, 1)
                dve.wait_ge(self.xt_summed, (c * L + n) * self.G + g + 1)
                nc.vector.tensor_tensor(self.xt(c)[:, hs], self.xt(c)[:, hs], self.bank(2, g), ALU.subtract).then_inc(self.xt_updated, 1)


DECAY_SCALE = -float(np.exp(-0.5))


def rwkv(C, ctx, pt, vec, w2, a2, g2, mixed):
    nc, ps = C.nc, C.ps
    ones_t = C.const("run")
    both_halves = C.sb(ctx, "both_halves", [P, 8, T])
    sig, a, g, e = (C.sb(ctx, n, [P, 4, T]) for n in ("sig", "a", "g", "e"))
    rq = C.sb(ctx, "rq", [P, 4, 2, T])
    cs = C.sb(ctx, "cs", [P, 4, T])
    oka = C.sb(ctx, "oka", [P, 4])
    eref = C.sb(ctx, "eref", [P, 4, NCH])
    factor = C.sb(ctx, "factor", [P, 4, NCH - 1])
    r_t, k_t, v_t = pt[:, 0:4], pt[:, 4:8], pt[:, 8:12]
    mu, w0, a0, kkw, kaw, rkw, lnw, lnb = (vec[n] for n in ("mu", "w0", "a0", "kk", "ka", "rk", "lnw", "lnb"))

    def col(v, n):
        return v[:, n:n + 1]

    def wide(v):
        return v.unsqueeze(2).to_broadcast([P, 4, T])

    with C.stage("rwkv_mix", "shift_link mixed_in code_done code_summed a_copied g_summed prep_link kk_squared kk_summed kk_logged kk_rstd bonus_in "
                 "bonus_summed d_done exp_done") as (sctx, blk, sems):
        (shift_link, mixed_in, code_done, code_summed, a_copied, g_summed, prep_link, kk_squared, kk_summed, kk_logged, kk_rstd, bonus_in,
         bonus_summed, d_done, exp_done) = sems
        d = both_halves
        block = sctx.enter_context(blk)

        @block.vector
        def _(dve):
            link = chain(dve, shift_link)
            for lo, hi in ((12, 14), (0, 8), (8, 12)):
                n = hi - lo
                nc.vector.tensor_tensor(d[:, 0:n, 1:T], pt[:, lo:hi, 0:T - 1], pt[:, lo:hi, 1:T], ALU.subtract)
                link(nc.vector.tensor_scalar(d[:, 0:n, 0:1], pt[:, lo:hi, 0:1], -1.0, None, ALU.mult))
                for m in range(n):
                    ins = nc.vector.scalar_tensor_tensor(pt[:, lo + m], d[:, m], col(mu, lo + m), pt[:, lo + m], ALU.mult, ALU.add)
                if lo == 12:
                    ins.then_inc(mixed_in, 1)
                    dve.wait_ge(mixed_in, 1)
                else:
                    link(ins)
            link2 = chain(dve, prep_link)
            for m in range(4):
                last = nc.vector.tensor_scalar(rq[:, m, 1], k_t[:, m], col(kkw, m), None, ALU.mult)
            link2(last)
            nc.vector.tensor_tensor(e[:, :, :], rq[:, :, 1], rq[:, :, 1], ALU.mult).then_inc(kk_squared, 1)
            link2(nc.vector.tensor_scalar(oka[:, :], kaw, -1.0, 1.0, ALU.mult, ALU.add))
            dve.wait_ge(a_copied, 2)
            for m in range(4):
                last = nc.vector.tensor_scalar(d[:, m], a[:, m], col(kaw, m), col(oka, m), ALU.mult, ALU.add)
            link2(last)
            link2(nc.vector.tensor_tensor(k_t, k_t, d[:, 0:4], ALU.mult))
            for m in range(4):
                last = nc.vector.scalar_tensor_tensor(d[:, 4 + m], r_t[:, m], col(rkw, m), k_t[:, m], ALU.mult, ALU.mult)
            last.then_inc(bonus_in, 1)
            for m in range(4):
                last = nc.vector.tensor_tensor_scan(cs[:, m], ones_t, sig[:, m], 0.0, ALU.mult, ALU.add)
            dve.wait_ge(kk_rstd, 1)
            link2(nc.vector.tensor_tensor(rq[:, :, 1], rq[:, :, 1], e[:, :, :], ALU.mult))
            link2(nc.vector.tensor_tensor(a[:, :, :], a[:, :, :], rq[:, :, 1], ALU.mult))
            for m in range(4):
                csm = cs[:, m].rearrange("p (c t) -> p c t", c=NCH)
                mid = csm[:, :, P // 2 - 1:P // 2].to_broadcast([P, NCH, P])
                last = nc.vector.tensor_tensor(d[:, m].rearrange("p (c t) -> p c t", c=NCH), csm, mid, ALU.subtract)
            link2(last)
            nc.vector.tensor_tensor(sig[:, :, :], d[:, 0:4], sig[:, :, :], ALU.subtract).then_inc(d_done, 1)
            dve.wait_ge(exp_done, 1)
            nc.vector.tensor_tensor(rq[:, :, 0], r_t, e[:, :, :], ALU.mult)
            dve.wait_ge(exp_done, 2)
            nc.vector.tensor_tensor(rq[:, :, 1], rq[:, :, 1], sig[:, :, :], ALU.mult)
            dve.wait_ge(exp_done, 3)
            nc.vector.tensor_tensor(k_t, k_t, d[:, 0:4], ALU.mult)
            nc.vector.tensor_tensor(a[:, :, :], a[:, :, :], d[:, 0:4], ALU.mult)
            dve.wait_ge(exp_done, 4)
            nc.vector.tensor_tensor(factor[:, :, :], eref[:, :, 1:NCH], e[:, :, P - 1:T - P:P], ALU.mult)

        @block.scalar
        def _(act):
            act.wait_ge(mixed_in, 1)
            nc.scalar.activation(pt[0:64, 12], pt[0:64, 12], ACT.Tanh).then_inc(code_done, 1)
            nc.scalar.activation(pt[:, 13], pt[:, 13], ACT.Sigmoid).then_inc(code_done, 1)
            for m in range(4):
                act.wait_ge(code_summed, 2 * m + 1)
                nc.scalar.activation(sig[:, m], ps[:, m], ACT.Sigmoid, bias=col(w0, m))
                act.wait_ge(code_summed, 2 * m + 2)
                last = nc.scalar.activation(a[:, m], ps[:, 4 + m], ACT.Sigmoid, bias=col(a0, m))
                if m == 1 or m == 3:
                    last.then_inc(a_copied, 1)
            act.wait_ge(g_summed, 1)
            nc.scalar.activation(g[:, :, :], ps[:, 0:4], ACT.Copy).then_inc(a_copied, 1)
            act.wait_ge(kk_summed, 1)
            nc.scalar.activation(e[:, :, :], ps[:, 4:8], ACT.Ln, bias=C.const("tiny")).then_inc(kk_logged, 1)
            act.wait_ge(kk_logged, 1)
            nc.scalar.activation(e[:, :, :], e[:, :, :], ACT.Exp, scale=-0.5).then_inc(kk_rstd, 1)
            act.wait_ge(d_done, 1)
            nc.scalar.activation(e[:, :, :], d[:, 0:4], ACT.Exp, scale=DECAY_SCALE).then_inc(exp_done, 1)
            nc.scalar.activation(sig[:, :, :], sig[:, :, :], ACT.Exp, scale=DECAY_SCALE).then_inc(exp_done, 1)
            nc.scalar.activation(d[:, 0:4], d[:, 0:4], ACT.Exp, scale=-DECAY_SCALE).then_inc(exp_done, 1)
            nc.scalar.activation(eref[:, :, :], cs[:, :, P // 2 - 1:T:P], ACT.Exp, scale=DECAY_SCALE).then_inc(exp_done, 1)

        @block.tensor
        def _(pe):
            pe.wait_ge(code_done, 2)
            for m in range(4):
                nc.tensor.matmul(ps[:, m], w2[0:64, m * P:(m + 1) * P], pt[0:64, 12], start=True, stop=True).then_inc(code_summed, 1)
                nc.tensor.matmul(ps[:, 4 + m], a2[64:P, m * P:(m + 1) * P], pt[64:P, 12], start=True, stop=True).then_inc(code_summed, 1)
            pe.wait_ge(a_copied, 2)
            for m in range(4):
                mm = nc.tensor.matmul(ps[:, m], g2[:, m * P:(m + 1) * P], pt[:, 13], start=True, stop=True)
            mm.then_inc(g_summed, 1)
            pe.wait_ge(kk_squared, 1)
            for m in range(4):
                mm = nc.tensor.matmul(ps[:, 4 + m], C.const("pairs"), e[:, m], start=True, stop=True)
            mm.then_inc(kk_summed, 1)
            pe.wait_ge(a_copied, 3)
            pe.wait_ge(bonus_in, 1)
            for m in range(4):
                mm = nc.tensor.matmul(ps[:, m], C.const("pairs"), d[:, 4 + m], start=True, stop=True)
            mm.then_inc(bonus_summed, 1)

    vrow, krow, prow = both_halves[:, 0:4], both_halves[:, 4:8], e[:, :, :]
    with C.stage("rwkv_turn", "turned turn_copied v_link") as (sctx, blk, (turned, turn_copied, v_link)):
        block = sctx.enter_context(blk)
        jobs = [(src, dst, c) for src, dst in ((v_t, vrow), (k_t, krow), (a, prow)) for c in range(NCH)]

        @block.tensor
        def _(pe):
            for n, (src, dst, c) in enumerate(jobs):
                if n >= 4:
                    pe.wait_ge(turn_copied, n - 3)
                for m in range(4):
                    mm = nc.tensor.transpose(ps[:, 4 + n % 4, m * P:(m + 1) * P], src[:, m, c * P:(c + 1) * P], C.ident)
                mm.then_inc(turned, 1)

        @block.scalar
        def _(act):
            for n, (src, dst, c) in enumerate(jobs):
                act.wait_ge(turned, n + 1)
                nc.scalar.activation(dst[:, c], ps[:, 4 + n % 4], ACT.Copy).then_inc(turn_copied, 1)

        @block.vector
        def _(dve):
            dve.wait_ge(turned, NCH)
            nc.vector.tensor_tensor(v_t, ps[:, 0:4], v_t, ALU.mult).then_inc(v_link, 1)

    y_t = mixed[:, 4:8]
    H = 8
    with C.stage("rwkv_scan", inverse_signals() + " mats_summed mats_ready mats_link rhs_summed rhs_copied u_summed u_copied y_done y_out state_summed state_link state_ready") as (sctx, blk, sems):
        inv_sems, (mats_summed, mats_ready, mats_link, rhs_summed, rhs_copied, u_summed, u_copied, y_done, y_out, state_summed, state_link, state_ready) = sems[:8], sems[8:]
        free = sig[:, :, :].rearrange("p a (h i) -> p (a h) i", i=P)
        inv = Inverse(C, H, inv_sems, [free[:, 0:H]], free[:, H:2 * H], C.sb(sctx, "y", [P, H, P]),
                      cs[:, :, :].rearrange("p (a b) (h i) -> p a (b h) i", a=2, i=P))
        at = C.sb(sctx, "at", [P, H, 4, P])
        rhs = C.sb(sctx, "rhs", [P, 2, H // 2, HEAD])
        un = C.squares[:, 0].rearrange("p (h v) -> p h v", h=H)
        z = C.squares[:, 1, 0:4 * HEAD].rearrange("p (h v) -> p h v", h=4)
        block = sctx.enter_context(blk)
        RHS, U, Y, S = (6, 7), 2, 0, 1
        both = C.mask_pair.unsqueeze(1).to_broadcast([P, 2, 2 * P])

        def rows(h):
            return slice(64 * (h % 2), 64 * (h % 2) + 64)

        @block.tensor
        def _(pe):
            for c in range(NCH):
                ts = slice(c * P, (c + 1) * P)
                for h in range(H):
                    if c:
                        pe.wait_ge(state_ready, c)
                        pe.wait_ge(y_out, c)
                    nc.tensor.matmul(ps[:, h, 0:2 * P], k_t[rows(h), h // 2, ts], rq[rows(h), h // 2, :, ts], start=True, stop=True)
                    nc.tensor.matmul(ps[:, h, 2 * P:4 * P], a[rows(h), h // 2, ts], rq[rows(h), h // 2, :, ts], start=True, stop=True).then_inc(mats_summed, 1)
                pe.wait_ge(mats_ready, (c + 1) * H)
                inv.pe(pe, c)
                for h in range(H):
                    hs = slice(h * HEAD, (h + 1) * HEAD)
                    out = ps[:, RHS[h % 2], h // 2 * HEAD:(h // 2 + 1) * HEAD]
                    mm = nc.tensor.matmul(out, at[:, h, 1], vrow[:, c, hs], start=True, stop=c == 0)
                    if c:
                        mm = nc.tensor.matmul(out, rq[rows(h), h // 2, 1, ts], z[rows(h), h // 2], start=False, stop=True)
                mm.then_inc(rhs_summed, 1)
                pe.wait_ge(rhs_copied, c + 1)
                pe.wait_ge(inv.xt_updated, (c + 1) * ((LEVELS - 1) * inv.G + 1))
                for h in range(H):
                    mm = nc.tensor.matmul(ps[:, U, h * HEAD:(h + 1) * HEAD], inv.xt(c)[:, h], rhs[:, h % 2, h // 2], start=True, stop=True)
                mm.then_inc(u_summed, 1)
                pe.wait_ge(u_copied, c + 1)
                for h in range(H):
                    hs = slice(h * HEAD, (h + 1) * HEAD)
                    out = ps[rows(h), S, h // 2 * HEAD:(h // 2 + 1) * HEAD]
                    nc.tensor.matmul(out, krow[:, c, hs], vrow[:, c, hs], start=True, stop=False)
                    mm = nc.tensor.matmul(out, prow[:, c, hs], un[:, h], start=False, stop=True)
                mm.then_inc(state_summed, 1)
                for h in range(H):
                    hs = slice(h * HEAD, (h + 1) * HEAD)
                    out = ps[rows(h), Y, h // 2 * P:(h // 2 + 1) * P]
                    nc.tensor.matmul(out, vrow[:, c, hs], at[:, h, 0], start=True, stop=False)
                    if c:
                        nc.tensor.matmul(out, z[rows(h), h // 2], rq[rows(h), h // 2, 0, ts], start=False, stop=False)
                    mm = nc.tensor.matmul(out, un[:, h], at[:, h, 2], start=False, stop=True)
                mm.then_inc(y_done, 1)

        @block.vector
        def _(dve):
            link, link_m = chain(dve, state_link), chain(dve, mats_link)
            for c in range(NCH):
                for h in range(H):
                    dve.wait_ge(mats_summed, c * H + h + 1)
                    nc.vector.tensor_tensor(at[:, h].rearrange("p (a b) i -> p a (b i)", a=2), ps[:, h].rearrange("p (a b) -> p a b", a=2), both, ALU.mult).then_inc(mats_ready, 1)
                dve.wait_ge(mats_ready, (c + 1) * H)
                inv.dve_start(dve, link_m, c, at[:, :, 3])
                inv.dve(dve, c)
                dve.wait_ge(u_summed, c + 1)
                nc.vector.tensor_scalar(un[:, :, :], ps[:, U].rearrange("p (h v) -> p h v", h=H), -1.0, None, ALU.mult).then_inc(u_copied, 1)
                if c == NCH - 1:
                    break
                dve.wait_ge(state_summed, c + 1)
                dve.wait_ge(y_done, c + 1)
                src = ps[:, S, 0:4 * HEAD].rearrange("p (m v) -> p m v", m=4)
                f = factor[:, :, c:c + 1].to_broadcast([P, 4, HEAD])
                if c == 0:
                    nc.vector.tensor_tensor(z[:, :, :], src, f, ALU.mult).then_inc(state_ready, 1)
                else:
                    link(nc.vector.tensor_tensor(z[:, :, :], src, z[:, :, :], ALU.add))
                    nc.vector.tensor_tensor(z[:, :, :], z[:, :, :], f, ALU.mult).then_inc(state_ready, 1)

        @block.gpsimd
        def _(pool):
            for c in range(NCH):
                inv.pool(pool, c, at[:, :, 3], mats_ready, (c + 1) * H)

        @block.scalar
        def _(act):
            for c in range(NCH):
                inv.act(act, c)
                act.wait_ge(rhs_summed, c + 1)
                nc.scalar.activation(rhs[:, :, :, :], ps[:, 6:8, 0:H // 2 * HEAD].rearrange("p a (h v) -> p a h v", v=HEAD), ACT.Copy).then_inc(rhs_copied, 1)
                act.wait_ge(y_done, c + 1)
                nc.scalar.activation(y_t[:, :, c * P:(c + 1) * P], ps[:, Y].rearrange("p (m i) -> p m i", m=4), ACT.Copy).then_inc(y_out, 1)

    with C.stage("rwkv_norm", "mean_summed centred squared var_summed logged rstd_done norm_link") as (sctx, blk, sems):
        mean_summed, centred, squared, var_summed, logged, rstd_done, norm_link = sems
        block = sctx.enter_context(blk)

        @block.tensor
        def _(pe):
            for m in range(4):
                nc.tensor.matmul(ps[:, m], C.const("pairs"), y_t[:, m], start=True, stop=True).then_inc(mean_summed, 1)
            for m in range(4):
                pe.wait_ge(squared, m + 1)
                nc.tensor.matmul(ps[:, 4 + m], C.const("pairs"), e[:, m], start=True, stop=True).then_inc(var_summed, 1)

        @block.vector
        def _(dve):
            link = chain(dve, norm_link)
            for m in range(4):
                dve.wait_ge(mean_summed, m + 1)
                nc.vector.scalar_tensor_tensor(y_t[:, m], ps[:, m], -1.0 / HEAD, y_t[:, m], ALU.mult, ALU.add).then_inc(centred, 1)
            for m in range(4):
                dve.wait_ge(rstd_done, m + 1)
                link(nc.vector.scalar_tensor_tensor(y_t[:, m], y_t[:, m], col(lnw, m), e[:, m], ALU.mult, ALU.mult))
                link(nc.vector.scalar_tensor_tensor(y_t[:, m], y_t[:, m], col(lnb, m), v_t[:, m], ALU.add, ALU.add))
                nc.vector.tensor_tensor(mixed[:, 4 + m], y_t[:, m], g[:, m], ALU.mult)

        @block.scalar
        def _(act):
            for m in range(4):
                act.wait_ge(centred, m + 1)
                nc.scalar.activation(e[:, m], y_t[:, m], ACT.Square).then_inc(squared, 1)
            for m in range(4):
                act.wait_ge(var_summed, m + 1)
                nc.scalar.activation(e[:, m], ps[:, 4 + m], ACT.Ln, bias=C.const("gn_eps"), scale=1.0 / HEAD).then_inc(logged, 1)
            for m in range(4):
                act.wait_ge(logged, m + 1)
                nc.scalar.activation(e[:, m], e[:, m], ACT.Exp, scale=-0.5).then_inc(rstd_done, 1)


N_CMP = (T - 32) // 16 + 1


def sparse_attention(C, ctx, qt, kc, vc, ks, vs, kw, vw, gates, weights, mixed, conv):
    nc, ps = C.nc, C.ps
    NB = 2 * N_CMP
    k_cmp = C.sb(ctx, "k_cmp", [P, N_CMP])
    v_cmp = C.sb(ctx, "v_cmp", [P, 2 * HEAD])
    with C.stage("compress", "w1_loaded_k w1_loaded_v w2_loaded stacked_k stacked_v hidden_summed hidden_done cmp_summed cmp_copied gates_done gate_link rotated rope_link") as (sctx, blk, sems):
        w1_loaded_k, w1_loaded_v, w2_loaded, stacked_k, stacked_v, hidden_summed, hidden_done, cmp_summed, cmp_copied, gates_done, gate_link, rotated, rope_link = sems
        w1 = C.sb(sctx, "w1", [P, 2, 16, 256])
        w2 = C.sb(sctx, "w2", [P, 2, 2, HEAD])
        stack = C.sb(sctx, "stack", [P, 2, 16, 2, N_CMP])
        hidden = C.sb(sctx, "hidden", [P, 2, 2, NB])
        turn = C.sb(sctx, "turn", [P, 2, N_CMP])
        block = sctx.enter_context(blk)

        @block.sync
        def _(sp):
            for n, loaded in enumerate((w1_loaded_k, w1_loaded_v)):
                sp.dma_start(w1[:, n], weights[n][0].rearrange("(a p) f -> p a f", p=P)).then_inc(loaded, 16)
                sp.dma_start(w2[:, n], weights[n][1].rearrange("(a p) f -> p a f", p=P)).then_inc(w2_loaded, 16)

        @block.vector
        def _(dve):
            for n, (z, done) in enumerate(((kc, stacked_k), (vc, stacked_v))):
                for g in range(2):
                    for odd in range(2):
                        rows = slice(64 * g, 64 * g + 64)
                        for a in range(0, 16, 8):
                            view = z[rows, 2 * a:2 * a + 16 * N_CMP].rearrange("p (n a o) -> p a o n", a=8, o=2)[:, :, odd]
                            steps = weights[n][2][rows, odd, a:a + 8].unsqueeze(2).to_broadcast([64, 8, N_CMP])
                            nc.vector.tensor_tensor(stack[64 * odd:64 * odd + 64, n, a:a + 8, g], view, steps, ALU.add).then_inc(done, 1)
            dve.wait_ge(cmp_copied, 1)
            dve.wait_ge(rotated, 1)
            link = chain(dve, rope_link)
            at = slice(31, T, 16)
            nc.vector.tensor_tensor(turn[:, 0], k_cmp[:, :], C.const("cos")[:, at], ALU.mult)
            link(nc.vector.tensor_tensor(turn[:, 1], ps[:, 5, 0:N_CMP], C.const("sin")[:, at], ALU.mult))
            link(nc.vector.tensor_tensor(k_cmp[:, :], turn[:, 0], turn[:, 1], ALU.add))
            dve.wait_ge(gates_done, 1)
            link(nc.vector.tensor_scalar(gates[:, 0, 0:24:3], gates[:, 0, 0:24:3], C.const("cmp_valid"), None, ALU.mult))

        @block.tensor
        def _(pe):
            for n, (loaded, stacked) in enumerate(((w1_loaded_k, stacked_k), (w1_loaded_v, stacked_v))):
                pe.wait_ge(loaded, 16)
                pe.wait_ge(stacked, 8)
                for t in range(2):
                    for a in range(16):
                        mm = nc.tensor.matmul(ps[:, 2 * n + t, 0:NB], w1[:, n, a, t * P:(t + 1) * P],
                                              stack[:, n, a].rearrange("p g n -> p (g n)"), start=a == 0, stop=a == 15)
                mm.then_inc(hidden_summed, 1)
            pe.wait_ge(w2_loaded, 32)
            pe.wait_ge(hidden_done, 1)
            for g in range(2):
                for t in range(2):
                    mm = nc.tensor.matmul(ps[64 * g:64 * g + 64, 4, 0:N_CMP], w2[:, 0, t], hidden[:, 0, t, g * N_CMP:(g + 1) * N_CMP], start=t == 0, stop=t == 1)
            mm.then_inc(cmp_summed, 1)
            pe.wait_ge(cmp_copied, 1)
            nc.tensor.matmul(ps[:, 5, 0:N_CMP], C.const("rot"), k_cmp[:, :], start=True, stop=True).then_inc(rotated, 1)
            pe.wait_ge(hidden_done, 2)
            for g in range(2):
                for t in range(2):
                    mm = nc.tensor.matmul(ps[0:N_CMP, 6, g * HEAD:(g + 1) * HEAD], hidden[:, 1, t, g * N_CMP:(g + 1) * N_CMP], w2[:, 1, t], start=t == 0, stop=t == 1)
            mm.then_inc(cmp_summed, 1)

        @block.scalar
        def _(act):
            nc.scalar.activation(gates[:, :, :], gates[:, :, :], ACT.Sigmoid).then_inc(gates_done, 1)
            for n in range(2):
                act.wait_ge(hidden_summed, n + 1)
                nc.scalar.activation(hidden[:, n], ps[:, 2 * n:2 * n + 2, 0:NB], ACT.Gelu_apprx_tanh).then_inc(hidden_done, 1)
            act.wait_ge(cmp_summed, 1)
            nc.scalar.activation(k_cmp[:, :], ps[:, 4, 0:N_CMP], ACT.Copy).then_inc(cmp_copied, 1)
            act.wait_ge(cmp_summed, 2)
            nc.scalar.activation(v_cmp[0:N_CMP], ps[0:N_CMP, 6, 0:2 * HEAD], ACT.Copy).then_inc(cmp_copied, 1)

    cos, sin, rot = C.const("cos"), C.const("sin"), C.const("rot")
    rope_stage(C, "nsa_rope", [(qt[:, m], rot, cos, sin, HEAD ** -0.5) for m in range(4)] + [(z, rot, cos, sin, 1.0) for z in (ks, kw)])
    groups = []
    for hd in range(8):
        g, m = hd // 4, hd % 4
        rows = slice(64 * g, 64 * g + 64)

        def coef(b, hd=hd):
            return lambda i: gates[:, i, 3 * hd + b:3 * hd + b + 1]

        def causal(k, v, b):
            return ([(qt[rows, m], k[rows], lambda i: C.const("causal"), lambda i: (i + 1) * P, coef(b))],
                    lambda j, g=g: v[:, j, g * HEAD:(g + 1) * HEAD])

        cmp = ([(qt[rows, m], k_cmp[rows], lambda i: C.const("cmp_mask")[:, i * N_CMP:(i + 1) * N_CMP], lambda i: N_CMP, coef(0))],
               lambda j, g=g: v_cmp[0:N_CMP, g * HEAD:(g + 1) * HEAD])
        half = slice(64 * (hd % 2), 64 * (hd % 2) + 64)
        groups.append(([cmp, causal(ks, vs, 1), causal(kw, vw, 2)], half, mixed[:, hd // 2] if hd % 2 else None, hd // 2))
    attention_stage(C, "nsa_attn", groups, conv)


def mlstm(C, ctx, qk, v, li, lf, og, ig_b, fg_b, norm, mixed):
    nc, ps = C.nc, C.ps
    rowsb = C.sb(ctx, "gate_rows", [4, 4, T])
    b_r, g_r, m_r, s_r = (rowsb[:, n] for n in range(4))
    g_col = C.sb(ctx, "g_col", [P, NCH, 4])
    with C.stage("mlstm_gates", "gate_link gate_in gate_exp gate_log turned og_done") as (sctx, blk, sems):
        gate_link, gate_in, gate_exp, gate_log, turned, og_done = sems
        tmp = C.sb(sctx, "tmp", [4, 2, T])
        block = sctx.enter_context(blk)

        @block.vector
        def _(dve):
            link = chain(dve, gate_link)
            link(nc.vector.tensor_scalar(lf, lf, fg_b, None, ALU.add))
            link(nc.vector.tensor_scalar(li, li, ig_b, None, ALU.add))
            nc.vector.scalar_tensor_tensor(tmp[:, 0], lf, -1.0, lf, ALU.mult, ALU.max).then_inc(gate_in, 1)
            dve.wait_ge(gate_in, 1)
            link(nc.vector.tensor_scalar(lf, lf, 0.0, None, ALU.min))
            dve.wait_ge(gate_log, 1)
            link(nc.vector.tensor_tensor(lf, lf, tmp[:, 1], ALU.subtract))
            link(nc.vector.tensor_tensor_scan(b_r, C.const("ones_t")[0:4], lf, 0.0, ALU.mult, ALU.add))
            link(nc.vector.tensor_tensor(g_r, li, b_r, ALU.subtract))
            link(nc.vector.tensor_tensor_scan(m_r, C.const("ones_t")[0:4], g_r, 0.0, ALU.mult, ALU.max))
            link(nc.vector.tensor_tensor(s_r, b_r, m_r, ALU.add))
            dve.wait_ge(turned, 1)
            link(nc.vector.tensor_copy(g_col[:, :, :], ps[:, 0, 0:16].rearrange("p (c h) -> p c h", h=4)))

        @block.scalar
        def _(act):
            nc.scalar.activation(og, og, ACT.Sigmoid).then_inc(og_done, 1)
            act.wait_ge(gate_in, 1)
            nc.scalar.activation(tmp[:, 1], tmp[:, 0], ACT.Exp, scale=-1.0).then_inc(gate_exp, 1)
            act.wait_ge(gate_exp, 1)
            nc.scalar.activation(tmp[:, 1], tmp[:, 1], ACT.Ln, bias=C.const("one")[0:4]).then_inc(gate_log, 1)

        @block.tensor
        def _(pe):
            pe.wait_ge(gate_link, 6)
            for c in range(NCH):
                mm = nc.tensor.transpose(ps[:, 0, 4 * c:4 * c + 4], g_r[:, c * P:(c + 1) * P], C.ident[0:4, 0:4])
            mm.then_inc(turned, 1)

    with C.stage("mlstm_scan", "rows_spread scores_done clamped exp_done weighed mask_link num_done guard_exp den_link head_done") as (sctx, blk, sems):
        rows_spread, scores_done, clamped, exp_done, weighed, mask_link, num_done, guard_exp, den_link, head_done = sems
        wts = C.sb(sctx, "wts", [P, 3, T])
        guard = C.sb(sctx, "guard", [P, 2, T])
        block = sctx.enter_context(blk)
        M_BANK, G_BANK, S_BANKS, NUM, DEN = 0, 1, (2, 3), (4, 5), (6, 7)
        units = [(h, j) for h in range(4) for j in range(NCH)]

        def head_rows(h):
            return slice(64 * (h % 2), 64 * (h % 2) + 64)

        @block.tensor
        def _(pe):
            def spread(h):
                if h:
                    pe.wait_ge(clamped, 4 * h)
                    pe.wait_ge(guard_exp, h)
                sel = C.const("select")[0:4, h * P:(h + 1) * P]
                nc.tensor.matmul(ps[:, M_BANK], sel, m_r, start=True, stop=True)
                nc.tensor.matmul(ps[:, G_BANK], sel, s_r, start=True, stop=True).then_inc(rows_spread, 1)

            def scores(u):
                h, j = units[u]
                if u >= 2:
                    pe.wait_ge(weighed, u - 1)
                nc.tensor.matmul(ps[:, S_BANKS[u % 2], 0:T - j * P], qk[head_rows(h), 2 + h // 2, j * P:(j + 1) * P],
                                 qk[head_rows(h), h // 2, j * P:T], start=True, stop=True).then_inc(scores_done, 1)

            def sums(u):
                h, j = units[u]
                if j == 0 and h >= 2:
                    pe.wait_ge(head_done, h - 1)
                pe.wait_ge(weighed, u + 1)
                w = wts[:, u % 3, 0:T - j * P]
                nc.tensor.matmul(ps[:, NUM[h % 2], j * P:T], v[:, j, h * P:(h + 1) * P], w, start=j == 0, stop=j == NCH - 1)
                nc.tensor.matmul(ps[:, DEN[h % 2], j * P:T], C.ones, w, start=j == 0, stop=j == NCH - 1).then_inc(num_done, 1)

            for u, (h, j) in enumerate(units):
                if j == 0:
                    spread(h)
                scores(u)
                if u:
                    sums(u - 1)
            sums(len(units) - 1)

        @block.vector
        def _(dve):
            link, link_d = chain(dve, mask_link), chain(dve, den_link)

            def finish(h):
                out = mixed[:, 4 + h]
                gd = guard[:, h % 2]
                dve.wait_ge(num_done, 4 * h + 4)
                dve.wait_ge(guard_exp, h + 1)
                link_d(nc.vector.scalar_tensor_tensor(gd, ps[:, DEN[h % 2]], -1.0, gd, ALU.mult, ALU.max))
                link_d(nc.vector.tensor_tensor(gd, ps[:, DEN[h % 2]], gd, ALU.max))
                link_d(nc.vector.reciprocal(gd, gd))
                nc.vector.tensor_tensor(out, ps[:, NUM[h % 2]], gd, ALU.mult).then_inc(head_done, 1)

            for u, (h, j) in enumerate(units):
                w = wts[:, u % 3, 0:T - j * P]
                dve.wait_ge(rows_spread, h + 1)
                if u >= 3:
                    dve.wait_ge(num_done, u - 2)
                nc.vector.tensor_scalar(w, ps[:, M_BANK, j * P:T], g_col[:, j, h:h + 1], 0.0, ALU.subtract, ALU.max).then_inc(clamped, 1)
                dve.wait_ge(scores_done, u + 1)
                dve.wait_ge(exp_done, u + 1)
                link(nc.vector.scalar_tensor_tensor(w, ps[:, S_BANKS[u % 2], 0:T - j * P], HEAD ** -0.5, w, ALU.mult, ALU.mult))
                nc.vector.tensor_tensor(w[:, 0:P], w[:, 0:P], C.const("upper"), ALU.mult).then_inc(weighed, 1)
                if j == 1 and h:
                    finish(h - 1)
            finish(3)

        @block.scalar
        def _(act):
            for u, (h, j) in enumerate(units):
                if j == 0:
                    act.wait_ge(rows_spread, h + 1)
                    if h >= 2:
                        act.wait_ge(head_done, h - 1)
                    nc.scalar.activation(guard[:, h % 2], ps[:, G_BANK], ACT.Exp, scale=-1.0).then_inc(guard_exp, 1)
                act.wait_ge(clamped, u + 1)
                w = wts[:, u % 3, 0:T - j * P]
                nc.scalar.activation(w, w, ACT.Exp, scale=-1.0).then_inc(exp_done, 1)

    head_norm_stage(C, "mlstm_norm", mixed[:, 4:8], mixed[:, 4:8], C.ones, P, C.eps, norm, og)


def log_sigmoid_terms(C, dve, link, z, tmp, made):
    link(C.nc.vector.scalar_tensor_tensor(tmp, z, -1.0, z, ALU.mult, ALU.max))
    C.nc.vector.tensor_scalar(z, z, 0.0, None, ALU.min).then_inc(made, 1)


def gla_stage(C, name, dk, q, k, lf, v, out, conv=()):
    nc, ps = C.nc, C.ps
    n = q.shape[1]
    with C.stage(name, "scan_link summed_up at_cleared dist_done exp_done level_ready level_summed level_taken in_decayed in_ready out_dist "
                 "out_decayed out_ready turned turn_copied inc_summed state_link states_ready o_summed " + Convolution.signals) as (ctx, blk, sems):
        (scan_link, summed_up, at_cleared, dist_done, exp_done, level_ready, level_summed, level_taken, in_decayed, in_ready, out_dist,
         out_decayed, out_ready, turned, turn_copied, inc_summed, state_link, states_ready, o_summed) = sems[:19]
        conv = Convolution(C, ctx, sems[19:], conv)
        b = C.sb(ctx, "b", [P, n, T])
        dist = C.sb(ctx, "dist", [P, 2, n, T])
        pair = C.sb(ctx, "pair", [P, 2, n, T])
        q_in = C.sb(ctx, "q_in", [P, n, T])
        k_out = C.sb(ctx, "k_out", [P, n, T])
        k_row = C.sb(ctx, "k_row", [P, NCH, n * P])
        at = C.sb(ctx, "at", [P, 4, NCH, P])
        states = C.sb(ctx, "states", [P, NCH, n, HEAD])
        block = ctx.enter_context(blk)
        STEPS = LEVELS + 1
        TURN, INC, O = (0, 1, 2, 3), 4, (6, 7)

        def rows(h):
            return slice(dk * (h % (P // dk)), dk * (h % (P // dk)) + dk)

        def tile(h):
            return h // (P // dk)

        def blocks(t, w):
            return t.rearrange("p n (m o w) -> p (n m) o w", o=2, w=w)

        def odd(t, w):
            return t.rearrange("p (m o w) -> p m o w", o=2, w=w)[:, :, 1]

        @block.gpsimd
        def _(pool):
            nc.gpsimd.memset(at[:, :, :, :], 0.0).then_inc(at_cleared, 1)
            conv.pool(pool)

        @block.vector
        def _(dve):
            link = chain(dve, scan_link)
            for m in range(n):
                last = nc.vector.tensor_tensor_scan(b[:, m], C.const("run"), lf[:, m], 0.0, ALU.mult, ALU.add)
            last.then_inc(summed_up, 1)
            dve.wait_ge(summed_up, 1)
            for m in range(n):
                bm = b[:, m].rearrange("p (c t) -> p c t", c=NCH)
                end = bm[:, :, P - 1:P].to_broadcast([P, NCH, P])
                last = nc.vector.tensor_tensor(k_out[:, m].rearrange("p (c t) -> p c t", c=NCH), end, bm, ALU.subtract)
            last.then_inc(out_dist, 1)

            def distance(s):
                w = 1 << s
                if s >= 2:
                    dve.wait_ge(level_ready, s - 1)
                v2 = b[:, :, :].rearrange("p n (m w) -> p (n m) w", w=2 * w)
                ref = v2[:, :, w - 1:w].to_broadcast(list(v2.shape))
                nc.vector.tensor_tensor(dist[:, s % 2].rearrange("p n (m w) -> p (n m) w", w=2 * w), v2, ref, ALU.subtract).then_inc(dist_done, 1)

            def operands(s):
                w = 1 << s
                dve.wait_ge(exp_done, s + 1)
                if s >= 2:
                    dve.wait_ge(level_summed, s)
                for o, src in ((1, q), (0, k)):
                    ins = nc.vector.tensor_tensor(blocks(pair[:, s % 2], w)[:, :, o], blocks(src, w)[:, :, o], blocks(dist[:, s % 2], w)[:, :, o], ALU.mult)
                ins.then_inc(level_ready, 1)
                dve.wait_ge(level_ready, s + 1)

            def take(step):
                dve.wait_ge(level_summed, step + 1)
                dve.wait_ge(at_cleared, 1)
                mask = C.ident if step == 0 else C.const("levels")[:, (step - 1) * P:step * P]
                first = 4 * (step % 2)
                data = ps[:, first:first + 4].rearrange("p h (c i) -> p (h c) i", c=NCH)
                to, mask = at[:, :, :, :].rearrange("p h c i -> p (h c) i"), mask.bitcast(I32).unsqueeze(1).to_broadcast([P, 4 * NCH, P])
                if step:
                    w = 1 << (step - 1)
                    to, mask, data = (t.rearrange("p h (m o w) -> p h m o w", o=2, w=w)[:, :, :, 1] for t in (to, mask, data))
                nc.vector.copy_predicated(to, mask, data).then_inc(level_taken, 1)

            distance(0)
            distance(1)
            dve.wait_ge(in_decayed, 1)
            link(nc.vector.tensor_tensor(q_in[:, :, :], q, q_in[:, :, :], ALU.mult))
            dve.wait_ge(out_decayed, 1)
            nc.vector.tensor_tensor(k_out[:, :, :], k, k_out[:, :, :], ALU.mult).then_inc(out_ready, 1)
            for s in range(LEVELS):
                operands(s)
                if s + 2 < LEVELS:
                    distance(s + 2)
                if s:
                    dve.wait_ge(level_taken, s)
                take(s)
            dve.wait_ge(level_taken, LEVELS)
            take(LEVELS)
            dve.wait_ge(inc_summed, 1)
            slink = chain(dve, state_link)
            inc = ps[:, INC, 0:(NCH - 1) * n * HEAD].rearrange("p (c m v) -> p c m v", c=NCH - 1, m=n)
            dve.wait_ge(in_decayed, 2)
            slink(nc.vector.tensor_copy(states[:, 1], inc[:, 0]))
            for c in range(1, NCH - 1):
                for m in range(n):
                    last = nc.vector.scalar_tensor_tensor(states[:, c + 1, m], states[:, c, m], states[:, 0, m, c:c + 1], inc[:, c, m], ALU.mult, ALU.add)
                slink(last)
            dve.sem_inc(states_ready, 1)

        @block.scalar
        def _(act):
            act.wait_ge(summed_up, 1)
            nc.scalar.activation(q_in[:, :, :], b[:, :, :], ACT.Exp).then_inc(in_decayed, 1)
            act.wait_ge(out_dist, 1)
            nc.scalar.activation(k_out[:, :, :], k_out[:, :, :], ACT.Exp).then_inc(out_decayed, 1)
            nc.scalar.activation(states[:, 0, :, 0:NCH], b[:, :, P - 1:T:P], ACT.Exp).then_inc(in_decayed, 1)
            for s in range(LEVELS):
                w = 1 << s
                act.wait_ge(dist_done, s + 1)
                d = blocks(dist[:, s % 2], w)
                nc.scalar.activation(d[:, :, 1], d[:, :, 1], ACT.Exp)
                nc.scalar.activation(d[:, :, 0], d[:, :, 0], ACT.Exp, scale=-1.0).then_inc(exp_done, 1)
            for c in range(NCH):
                act.wait_ge(turned, c + 1)
                nc.scalar.activation(k_row[:, c], ps[:, TURN[c], 0:n * P], ACT.Copy).then_inc(turn_copied, 1)
            conv.act(act)
            act.wait_ge(o_summed, 1)
            nc.scalar.activation(out, ps[:, O[0]:O[1] + 1], ACT.Copy)

        @block.tensor
        def _(pe):
            for step in range(STEPS):
                if step:
                    pe.wait_ge(level_ready, step)
                if step >= 2:
                    pe.wait_ge(level_taken, step - 1)
                for c in range(NCH):
                    for h in range(4):
                        ts = slice(c * P, (c + 1) * P)
                        out_sum = ps[:, 4 * (step % 2) + h, c * P:(c + 1) * P]
                        if step:
                            left = pair[rows(h), (step - 1) % 2, tile(h), ts]
                            right = odd(left, 1 << (step - 1))
                            out_sum = odd(out_sum, 1 << (step - 1))
                        else:
                            left, right = k[rows(h), tile(h), ts], q[rows(h), tile(h), ts]
                        mm = nc.tensor.matmul(out_sum, left, right, start=True, stop=True)
                mm.then_inc(level_summed, 1)
            pe.wait_ge(out_ready, 1)
            pe.wait_ge(level_taken, STEPS)
            for c in range(NCH):
                for m in range(n):
                    mm = nc.tensor.transpose(ps[:, TURN[c], m * P:(m + 1) * P], k_out[:, m, c * P:(c + 1) * P], C.ident)
                mm.then_inc(turned, 1)
            for c in range(NCH - 1):
                pe.wait_ge(turn_copied, c + 1)
                for h in range(4):
                    at_col = (c * n + tile(h)) * HEAD
                    mm = nc.tensor.matmul(ps[rows(h), INC, at_col:at_col + HEAD], k_row[:, c, h * dk:(h + 1) * dk], v[:, c, h * HEAD:(h + 1) * HEAD], start=True, stop=True)
            mm.then_inc(inc_summed, 1)
            pe.wait_ge(states_ready, 1)
            for h in range(4):
                for c in range(NCH):
                    o = ps[64 * (h % 2):64 * (h % 2) + 64, O[h // 2], c * P:(c + 1) * P]
                    mm = nc.tensor.matmul(o, v[:, c, h * HEAD:(h + 1) * HEAD], at[:, h, c], start=True, stop=c == 0)
                    if c:
                        mm = nc.tensor.matmul(o, states[rows(h), c, tile(h)], q_in[rows(h), tile(h), c * P:(c + 1) * P], start=False, stop=True)
            mm.then_inc(o_summed, 1)


def lower_bound_stage(C, name, logits, lb):
    nc = C.nc
    with C.stage(name, "lb_link shifted exped") as (ctx, blk, (lb_link, shifted, exped)):
        t = C.sb(ctx, "t", [P, 2, 2])
        m = C.sb(ctx, "m", [P, 2])
        block = ctx.enter_context(blk)

        @block.vector
        def _(dve):
            link = chain(dve, lb_link)
            link(nc.vector.tensor_tensor(m[:, :], logits[:, 0], logits[:, 1], ALU.max))
            nc.vector.tensor_tensor(t[:, :, :], logits, m[:, :].unsqueeze(1).to_broadcast([P, 2, 2]), ALU.subtract).then_inc(shifted, 1)
            dve.wait_ge(exped, 1)
            link(nc.vector.tensor_tensor(m[:, :], t[:, 0], t[:, 1], ALU.add))
            link(nc.vector.reciprocal(m[:, :], m[:, :]))
            link(nc.vector.tensor_tensor(lb, t[:, 1], m[:, :], ALU.mult))

        @block.scalar
        def _(act):
            act.wait_ge(shifted, 1)
            nc.scalar.activation(t[:, :, :], t[:, :, :], ACT.Exp).then_inc(exped, 1)


def hgrn(C, ctx, name, q, f, v, g, lb, out, conv):
    nc = C.nc
    k = C.sb(ctx, "hk", [P, 2, T])
    LN_SHIFT = 50
    with C.stage(name + "_in", "silu_done gates_done k_done q_scaled f_link f_ready log_done") as (sctx, blk, sems):
        silu_done, gates_done, k_done, q_scaled, f_link, f_ready, log_done = sems
        tiny = C.sb(sctx, "tiny", [P, 2, T])
        low = C.sb(sctx, "low", [P, 2, T])
        olb = C.sb(sctx, "olb", [P, 2])
        block = sctx.enter_context(blk)

        @block.scalar
        def _(act):
            nc.scalar.activation(k[:, :, :], f, ACT.Sigmoid, scale=-1.0).then_inc(k_done, 1)
            act.wait_ge(k_done, 1)
            nc.scalar.activation(f, f, ACT.Sigmoid).then_inc(gates_done, 1)
            nc.scalar.activation(g, g, ACT.Sigmoid)
            nc.scalar.activation(q, q, ACT.Silu).then_inc(silu_done, 1)
            act.wait_ge(f_ready, 1)
            nc.scalar.activation(low[:, :, :], f, ACT.Ln, scale=float(2 ** LN_SHIFT)).then_inc(log_done, 1)
            act.wait_ge(log_done, 1)
            nc.scalar.activation(f, tiny[:, :, :], ACT.Ln).then_inc(log_done, 1)

        @block.vector
        def _(dve):
            link = chain(dve, f_link)
            dve.wait_ge(gates_done, 1)
            if lb is not None:
                link(nc.vector.tensor_scalar(olb[:, :], lb, -1.0, 1.0, ALU.mult, ALU.add))
                for m in range(2):
                    nc.vector.tensor_scalar(k[:, m], k[:, m], olb[:, m:m + 1], None, ALU.mult)
                    last = nc.vector.tensor_scalar(f[:, m], f[:, m], olb[:, m:m + 1], lb[:, m:m + 1], ALU.mult, ALU.add)
                link(last)
            link(nc.vector.tensor_scalar(f, f, 1e-30, None, ALU.max))
            nc.vector.tensor_scalar(tiny[:, :, :], f, 1e-19, None, ALU.max).then_inc(f_ready, 1)
            dve.wait_ge(silu_done, 1)
            link(nc.vector.tensor_scalar(q, q, HEAD ** -0.5, None, ALU.mult))
            dve.wait_ge(log_done, 2)
            link(nc.vector.tensor_scalar(tiny[:, :, :], tiny[:, :, :], 1e-19, None, ALU.is_le))
            link(nc.vector.tensor_scalar(low[:, :, :], low[:, :, :], -LN_SHIFT * float(np.log(2.0)), None, ALU.add))
            link(nc.vector.copy_predicated(f, tiny[:, :, :].bitcast(I32), low[:, :, :]))

    gla_stage(C, name, HEAD, q, k[:, :, :], f, v, out, conv)


def gla(C, ctx, name, q, k, v, code, g, w_gk2, b_gk, out, conv):
    nc, ps = C.nc, C.ps
    lf = C.sb(ctx, "lf", [P, 1, T])
    with C.stage(name + "_in", "gate_summed gate_link terms_made exp_done log_done") as (sctx, blk, sems):
        gate_summed, gate_link, terms_made, exp_done, log_done = sems
        size = C.sb(sctx, "size", [P, T])
        block = sctx.enter_context(blk)

        @block.tensor
        def _(pe):
            nc.tensor.matmul(ps[:, 0], w_gk2, code, start=True, stop=True).then_inc(gate_summed, 1)

        @block.vector
        def _(dve):
            link = chain(dve, gate_link)
            dve.wait_ge(gate_summed, 1)
            link(nc.vector.tensor_scalar(lf[:, 0], ps[:, 0], b_gk, None, ALU.add))
            log_sigmoid_terms(C, dve, link, lf[:, 0], size[:, :], terms_made)
            link(nc.vector.tensor_scalar(q, q, (HEAD // 2) ** -0.5, None, ALU.mult))
            dve.wait_ge(log_done, 1)
            link(nc.vector.tensor_tensor(lf[:, 0], lf[:, 0], size[:, :], ALU.subtract))
            link(nc.vector.tensor_scalar(lf[:, 0], lf[:, 0], 1.0 / 16.0, None, ALU.mult))

        @block.scalar
        def _(act):
            nc.scalar.activation(g, g, ACT.Silu)
            act.wait_ge(terms_made, 1)
            nc.scalar.activation(size[:, :], size[:, :], ACT.Exp, scale=-1.0).then_inc(exp_done, 1)
            act.wait_ge(exp_done, 1)
            nc.scalar.activation(size[:, :], size[:, :], ACT.Ln, bias=C.const("one")).then_inc(log_done, 1)

    gla_stage(C, name, HEAD // 2, q, k, lf[:, :, :], v, out, conv)


MLA_QK = 96


def mla(C, ctx, name, cq, ckv, kr, q_norm, kv_norm, w_uq, w_ukv, out):
    nc, ps = C.nc, C.ps
    qh = C.sb(ctx, "qh", [P, 4, T])
    kh = C.sb(ctx, "kh", [P, 4, T])
    v = C.sb(ctx, "v_mla", [P, NCH, 4 * HEAD])
    with C.stage(name + "_in", "squared summed logged rstd_done normed up_summed up_copied kr_copied") as (sctx, blk, sems):
        squared, summed, logged, rstd_done, normed, up_summed, up_copied, kr_copied = sems
        sq = C.sb(sctx, "sq", [P, 3, T])
        block = sctx.enter_context(blk)

        @block.scalar
        def _(act):
            nc.scalar.activation(sq[:, 0:2], cq, ACT.Square).then_inc(squared, 1)
            nc.scalar.activation(sq[:, 2:3], ckv, ACT.Square).then_inc(squared, 1)
            act.wait_ge(summed, 1)
            nc.scalar.activation(sq[:, 0], ps[:, 0], ACT.Ln, bias=C.eps, scale=1.0 / 256)
            nc.scalar.activation(sq[:, 1], ps[:, 1], ACT.Ln, bias=C.eps, scale=1.0 / P).then_inc(logged, 1)
            act.wait_ge(logged, 1)
            nc.scalar.activation(sq[:, 0:2], sq[:, 0:2], ACT.Exp, scale=-0.5).then_inc(rstd_done, 1)
            for u in range(12):
                act.wait_ge(up_summed, u + 1)
                if u < 4:
                    nc.scalar.activation(qh[0:MLA_QK, u], ps[0:MLA_QK, 2 + u % 6], ACT.Copy).then_inc(up_copied, 1)
                elif u < 8:
                    nc.scalar.activation(kh[0:HEAD, u - 4], ps[0:HEAD, 2 + u % 6], ACT.Copy).then_inc(up_copied, 1)
                else:
                    nc.scalar.activation(v[:, u - 8], ps[:, 2 + u % 6, 0:4 * HEAD], ACT.Copy).then_inc(up_copied, 1)

        @block.tensor
        def _(pe):
            pe.wait_ge(squared, 2)
            nc.tensor.matmul(ps[:, 0], C.ones, sq[:, 0], start=True, stop=False)
            nc.tensor.matmul(ps[:, 0], C.ones, sq[:, 1], start=False, stop=True)
            nc.tensor.matmul(ps[:, 1], C.ones, sq[:, 2], start=True, stop=True).then_inc(summed, 1)
            pe.wait_ge(normed, 1)
            for u in range(12):
                if u >= 6:
                    pe.wait_ge(up_copied, u - 5)
                bank = 2 + u % 6
                if u < 4:
                    nc.tensor.matmul(ps[0:MLA_QK, bank], w_uq[:, 0, u * MLA_QK:(u + 1) * MLA_QK], cq[:, 0], start=True, stop=False)
                    mm = nc.tensor.matmul(ps[0:MLA_QK, bank], w_uq[:, 1, u * MLA_QK:(u + 1) * MLA_QK], cq[:, 1], start=False, stop=True)
                elif u < 8:
                    mm = nc.tensor.matmul(ps[0:HEAD, bank], w_ukv[:, (u - 4) * P:(u - 4) * P + HEAD], ckv[:, 0], start=True, stop=True)
                else:
                    c = u - 8
                    values = w_ukv.rearrange("p (h o d) -> p h o d", h=4, o=2)[:, :, 1]
                    mm = nc.tensor.matmul(ps[:, bank, 0:4 * HEAD], ckv[:, 0, c * P:(c + 1) * P], values, start=True, stop=True)
                mm.then_inc(up_summed, 1)

        @block.vector
        def _(dve):
            dve.wait_ge(rstd_done, 1)
            for m in range(2):
                nc.vector.scalar_tensor_tensor(cq[:, m], cq[:, m], q_norm[:, m:m + 1], sq[:, 0], ALU.mult, ALU.mult)
            nc.vector.scalar_tensor_tensor(ckv[:, 0], ckv[:, 0], kv_norm, sq[:, 1], ALU.mult, ALU.mult).then_inc(normed, 1)
            for h in range(4):
                nc.vector.tensor_copy(kh[HEAD:MLA_QK, h], kr[HEAD:MLA_QK])

    cos, sin, rot = C.const("cos_mla"), C.const("sin_mla"), C.const("rot_mla")
    rope_stage(C, name + "_rope", [(qh[0:MLA_QK, h], rot, cos, sin, MLA_QK ** -0.5) for h in range(4)] + [(kh[0:MLA_QK, h], rot, cos, sin, 1.0) for h in range(4)])
    groups = []
    for h in range(4):
        maps = [(qh[0:MLA_QK, h], kh[0:MLA_QK, h], lambda i: C.const("causal"), lambda i: (i + 1) * P, None)]
        groups.append(([(maps, lambda j, h=h: v[:, j, h * HEAD:(h + 1) * HEAD])], slice(64 * (h % 2), 64 * (h % 2) + 64), out[:, h // 2] if h % 2 else None, h // 2))
    attention_stage(C, name, groups)


def gated_delta(C, ctx, name, qkv, z, beta, alpha, a_log, dt_bias, norm, out):
    nc, ps = C.nc, C.ps
    q, k, v = qkv[:, 0:2], qkv[:, 2:4], qkv[:, 4:6]
    qb = C.sb(ctx, "qb", [P, 2, 2, T])
    k_in, k_out = C.sb(ctx, "k_in", [P, 2, T]), C.sb(ctx, "k_out", [P, 2, T])
    q_in = C.sb(ctx, "q_in", [P, 2, T])
    decay = C.sb(ctx, "decay", [P, 4, NCH, 2, P])
    b_col = C.sb(ctx, "b_col", [P, NCH, 4])
    last_exp = C.sb(ctx, "last_exp", [P, 2, NCH])
    with C.stage(name + "_in", "gate_link terms_made beta_done exp_done log_done b_ready a_done turned b_copied spread_b spread_beta apart apart_exp "
                 "squared norm_summed logged rstd_done vec_link in_exp dist_done out_exp beta_used") as (sctx, blk, sems):
        (gate_link, terms_made, beta_done, exp_done, log_done, b_ready, a_done, turned, b_copied, spread_b, spread_beta, apart, apart_exp,
         squared, norm_summed, logged, rstd_done, vec_link, in_exp, dist_done, out_exp, beta_used) = sems
        sq = C.sb(sctx, "sq", [P, 4, T])
        size = C.sb(sctx, "size", [4, T])
        soft = C.sb(sctx, "soft", [4, T])
        a_neg = C.sb(sctx, "a_neg", [4, 1])
        block = sctx.enter_context(blk)

        @block.vector
        def _(dve):
            link = chain(dve, gate_link)
            link(nc.vector.tensor_scalar(alpha, alpha, dt_bias, None, ALU.add))
            nc.vector.scalar_tensor_tensor(size[:, :], alpha, -1.0, alpha, ALU.mult, ALU.max).then_inc(terms_made, 1)
            dve.wait_ge(terms_made, 1)
            link(nc.vector.tensor_scalar(alpha, alpha, 0.0, None, ALU.max))
            dve.wait_ge(log_done, 1)
            link(nc.vector.tensor_tensor(alpha, alpha, soft[:, :], ALU.add))
            dve.wait_ge(a_done, 1)
            link(nc.vector.tensor_scalar(alpha, alpha, a_neg[:, :], -1.0, ALU.mult, ALU.mult))
            link(nc.vector.tensor_tensor_scan(size[:, :], C.const("run")[0:4], alpha, 0.0, ALU.mult, ALU.add))
            dve.sem_inc(b_ready, 1)
            vlink = chain(dve, vec_link)
            dve.wait_ge(turned, 1)
            vlink(nc.vector.tensor_copy(b_col[:, :, :], ps[:, 4, 0:4 * NCH].rearrange("p (c h) -> p c h", h=4)))
            dve.wait_ge(spread_b, 1)
            for h in range(4):
                for c in range(NCH):
                    ins = nc.vector.tensor_scalar(decay[:, h, c, 0], ps[:, h, c * P:(c + 1) * P], b_col[:, c, h:h + 1], 0.0, ALU.subtract, ALU.min)
            ins.then_inc(apart, 1)
            dve.wait_ge(rstd_done, 1)
            nc.vector.scalar_tensor_tensor(qb[:, :, 0], q, HEAD ** -0.5, sq[:, 0:2], ALU.mult, ALU.mult)
            vlink(nc.vector.tensor_tensor(k, k, sq[:, 2:4], ALU.mult))
            dve.wait_ge(spread_beta, 1)
            vlink(nc.vector.tensor_tensor(qb[:, :, 1], k, ps[:, 4:6], ALU.mult))
            vlink(nc.vector.tensor_tensor(v, v, ps[:, 4:6], ALU.mult))
            for m in range(2):
                bm = sq[:, m].rearrange("p (c t) -> p c t", c=NCH)
                end = bm[:, :, P - 1:P].to_broadcast([P, NCH, P])
                dve.wait_ge(in_exp, 1)
                ins = nc.vector.tensor_tensor(sq[:, 2 + m].rearrange("p (c t) -> p c t", c=NCH), end, bm, ALU.subtract)
            ins.then_inc(dist_done, 1)
            dve.wait_ge(in_exp, 2)
            nc.vector.tensor_tensor(k_in[:, :, :], qb[:, :, 1], q_in[:, :, :], ALU.mult)
            vlink(nc.vector.tensor_copy(last_exp[:, :, :], q_in[:, :, P - 1:T:P]))
            vlink(nc.vector.tensor_tensor(q_in[:, :, :], qb[:, :, 0], q_in[:, :, :], ALU.mult))
            dve.wait_ge(out_exp, 1)
            nc.vector.tensor_tensor(k_out[:, :, :], k, sq[:, 2:4], ALU.mult)

        @block.scalar
        def _(act):
            nc.scalar.activation(z, z, ACT.Silu)
            nc.scalar.activation(beta, beta, ACT.Sigmoid).then_inc(beta_done, 1)
            nc.scalar.activation(sq[:, :, :], qkv[:, 0:4], ACT.Square).then_inc(squared, 1)
            nc.scalar.activation(a_neg[:, :], a_log, ACT.Exp).then_inc(a_done, 1)
            act.wait_ge(terms_made, 1)
            nc.scalar.activation(soft[:, :], size[:, :], ACT.Exp, scale=-1.0).then_inc(exp_done, 1)
            act.wait_ge(exp_done, 1)
            nc.scalar.activation(soft[:, :], soft[:, :], ACT.Ln, bias=C.const("one")[0:4]).then_inc(log_done, 1)
            act.wait_ge(norm_summed, 1)
            nc.scalar.activation(sq[:, :, :], ps[:, 0:4], ACT.Ln, bias=C.eps).then_inc(logged, 1)
            act.wait_ge(logged, 1)
            nc.scalar.activation(sq[:, :, :], sq[:, :, :], ACT.Exp, scale=-0.5).then_inc(rstd_done, 1)
            act.wait_ge(apart, 1)
            nc.scalar.activation(decay[:, :, :, 0], decay[:, :, :, 0], ACT.Exp).then_inc(apart_exp, 1)
            act.wait_ge(spread_beta, 1)
            act.wait_ge(vec_link, 3)
            nc.scalar.activation(sq[:, 0:2], ps[:, 6:8], ACT.Copy).then_inc(in_exp, 1)
            nc.scalar.activation(q_in[:, :, :], ps[:, 6:8], ACT.Exp).then_inc(in_exp, 1)
            act.wait_ge(dist_done, 1)
            nc.scalar.activation(sq[:, 2:4], sq[:, 2:4], ACT.Exp).then_inc(out_exp, 1)

        @block.gpsimd
        def _(pool):
            pool.wait_ge(apart_exp, 1)
            both = decay[:, :, :, :, :].rearrange("p h c o i -> p (h c) o i")
            for o, mask in ((1, "strict"), (0, "upper")):
                if o == 0:
                    pool.wait_ge(beta_used, 1)
                nc.gpsimd.tensor_tensor(both[:, :, o], both[:, :, 0], C.const(mask).unsqueeze(1).to_broadcast([P, 4 * NCH, P]), ALU.mult).then_inc(beta_used, 1)

        @block.tensor
        def _(pe):
            pe.wait_ge(squared, 1)
            for m in range(4):
                mm = nc.tensor.matmul(ps[:, m], C.const("pairs"), sq[:, m], start=True, stop=True)
            mm.then_inc(norm_summed, 1)
            pe.wait_ge(b_ready, 1)
            for c in range(NCH):
                mm = nc.tensor.transpose(ps[:, 4, 4 * c:4 * c + 4], size[:, c * P:(c + 1) * P], C.ident[0:4, 0:4])
            mm.then_inc(turned, 1)
            pe.wait_ge(logged, 1)
            for h in range(4):
                mm = nc.tensor.matmul(ps[:, h], C.const("select")[0:4, h * P:(h + 1) * P], size[:, :], start=True, stop=True)
            mm.then_inc(spread_b, 1)
            pe.wait_ge(beta_done, 1)
            pe.wait_ge(vec_link, 1)
            for m in range(2):
                nc.tensor.matmul(ps[:, 4 + m], C.const("select_pair")[0:4, m * P:(m + 1) * P], beta, start=True, stop=True)
                mm = nc.tensor.matmul(ps[:, 6 + m], C.const("select_pair")[0:4, m * P:(m + 1) * P], size[:, :], start=True, stop=True)
            mm.then_inc(spread_beta, 1)

    with C.stage(name, inverse_signals() + " mats_summed mats_ready mats_link turned turn_copied zv_summed rhs_ready d_summed d_copied state_summed state_ready y_done y_out") as (sctx, blk, sems):
        inv_sems, (mats_summed, mats_ready, mats_link, turned, turn_copied, zv_summed, rhs_ready, d_summed, d_copied, state_summed, state_ready, y_done, y_out) = sems[:8], sems[8:]
        at = C.sb(sctx, "at", [P, NCH // 2, 2, 4, 2, P])
        k_row, v_row = C.sb(sctx, "k_row", [P, NCH, 2 * P]), C.sb(sctx, "v_row", [P, NCH, 2 * P])
        xts = C.sb(sctx, "xts", [P, 2, 8, P])
        inv = Inverse(C, 8, inv_sems, [xts[:, 0], xts[:, 1]], C.sb(sctx, "x", [P, 8, P]), C.sb(sctx, "y", [P, 8, P]), C.sb(sctx, "masked", [P, 2, 8, P]))
        rhs = C.sb(sctx, "rhs", [P, 2, 2, HEAD])
        delta = C.sb(sctx, "delta", [P, 4, HEAD])
        state = C.sb(sctx, "state", [P, 2, HEAD])
        block = sctx.enter_context(blk)
        ZV, DEL, S, Y = (6, 7), 2, 1, 0

        def rows(h):
            return slice(64 * (h % 2), 64 * (h % 2) + 64)

        def mt(b):
            return at[:, b].rearrange("p c h o i -> p (c h) o i")[:, :, 1]

        @block.tensor
        def _(pe):
            for c in range(NCH):
                for m in range(2):
                    nc.tensor.transpose(ps[:, 4 + c, m * P:(m + 1) * P], k_out[:, m, c * P:(c + 1) * P], C.ident)
                    mm = nc.tensor.transpose(ps[:, 4 + c, (2 + m) * P:(3 + m) * P], v[:, m, c * P:(c + 1) * P], C.ident)
                mm.then_inc(turned, 1)
            for b in range(NCH // 2):
                for h in range(4):
                    if b:
                        pe.wait_ge(mats_ready, 4 * b)
                        pe.wait_ge(inv.xt_updated, b * ((LEVELS - 1) * inv.G + 1))
                        pe.wait_ge(inv.x_updated, b * (LEVELS - 1) * inv.G)
                        pe.wait_ge(inv.y_copied, b * (LEVELS - 1) * inv.G)
                    for o in range(2):
                        ts = slice((2 * b + o) * P, (2 * b + o + 1) * P)
                        mm = nc.tensor.matmul(ps[:, h, 2 * o * P:2 * (o + 1) * P], k[rows(h), h // 2, ts], qb[rows(h), h // 2, :, ts], start=True, stop=True)
                    mm.then_inc(mats_summed, 1)
                pe.wait_ge(mats_ready, 4 * (b + 1))
                pe.wait_ge(turn_copied, NCH)
                inv.pe(pe, b)
            for b in range(1, 3):
                pe.wait_ge(inv.xt_updated, b * ((LEVELS - 1) * inv.G + 1))
            for c in range(NCH):
                ts = slice(c * P, (c + 1) * P)
                if c:
                    pe.wait_ge(state_ready, c)
                    for h in range(4):
                        mm = nc.tensor.matmul(ps[:, ZV[h % 2], h // 2 * HEAD:(h // 2 + 1) * HEAD], k_in[rows(h), h // 2, ts], state[rows(h), h // 2], start=True, stop=True)
                    mm.then_inc(zv_summed, 1)
                pe.wait_ge(rhs_ready, c + 1)
                for h in range(4):
                    mm = nc.tensor.matmul(ps[:, DEL, h * HEAD:(h + 1) * HEAD], xts[:, c // 2, 4 * (c % 2) + h], rhs[:, h % 2, h // 2], start=True, stop=True)
                mm.then_inc(d_summed, 1)
                pe.wait_ge(d_copied, c + 1)
                for h in range(4):
                    mm = nc.tensor.matmul(ps[rows(h), S, h // 2 * HEAD:(h // 2 + 1) * HEAD], k_row[:, c, h * HEAD:(h + 1) * HEAD], delta[:, h], start=True, stop=True)
                mm.then_inc(state_summed, 1)
                if c:
                    pe.wait_ge(y_out, c)
                for h in range(4):
                    o = ps[rows(h), Y, h // 2 * P:(h // 2 + 1) * P]
                    mm = nc.tensor.matmul(o, delta[:, h], at[:, c // 2, c % 2, h, 0], start=True, stop=c == 0)
                    if c:
                        mm = nc.tensor.matmul(o, state[rows(h), h // 2], q_in[rows(h), h // 2, ts], start=False, stop=True)
                mm.then_inc(y_done, 1)

        @block.vector
        def _(dve):
            link = chain(dve, mats_link)
            for b in range(NCH // 2):
                for h in range(4):
                    dve.wait_ge(mats_summed, 4 * b + h + 1)
                    nc.vector.tensor_tensor(at[:, b, :, h], ps[:, h].rearrange("p (c o i) -> p c o i", c=2, o=2), decay[:, h, 2 * b:2 * b + 2], ALU.mult).then_inc(mats_ready, 1)
                dve.wait_ge(mats_ready, 4 * (b + 1))
                inv.dve_start(dve, link, b, mt(b))
                inv.dve(dve, b)
            for c in range(NCH):
                values = v_row[:, c].rearrange("p (m o v) -> p o m v", m=2, o=2)
                if c == 0:
                    dve.wait_ge(turn_copied, NCH)
                    nc.vector.tensor_copy(rhs[:, :, :, :], values).then_inc(rhs_ready, 1)
                else:
                    dve.wait_ge(zv_summed, c)
                    nc.vector.tensor_tensor(rhs[:, :, :, :], values, ps[:, ZV[0]:ZV[1] + 1, 0:2 * HEAD].rearrange("p o (m v) -> p o m v", m=2), ALU.subtract).then_inc(rhs_ready, 1)
                dve.wait_ge(d_summed, c + 1)
                nc.vector.tensor_copy(delta[:, :, :], ps[:, DEL, 0:4 * HEAD].rearrange("p (h v) -> p h v", h=4)).then_inc(d_copied, 1)
                dve.wait_ge(state_summed, c + 1)
                dve.wait_ge(y_done, c + 1)
                if c == 0:
                    nc.vector.tensor_copy(state[:, :, :], ps[:, S, 0:2 * HEAD].rearrange("p (m v) -> p m v", m=2)).then_inc(state_ready, 1)
                elif c < NCH - 1:
                    for m in range(2):
                        ins = nc.vector.scalar_tensor_tensor(state[:, m], state[:, m], last_exp[:, m, c:c + 1], ps[:, S, m * HEAD:(m + 1) * HEAD], ALU.mult, ALU.add)
                    ins.then_inc(state_ready, 1)

        @block.gpsimd
        def _(pool):
            for b in range(NCH // 2):
                inv.pool(pool, b, mt(b), mats_ready, 4 * (b + 1))

        @block.scalar
        def _(act):
            for c in range(NCH):
                act.wait_ge(turned, c + 1)
                nc.scalar.activation(k_row[:, c], ps[:, 4 + c, 0:2 * P], ACT.Copy)
                nc.scalar.activation(v_row[:, c], ps[:, 4 + c, 2 * P:4 * P], ACT.Copy).then_inc(turn_copied, 1)
            for b in range(NCH // 2):
                inv.act(act, b)
            for c in range(NCH):
                act.wait_ge(y_done, c + 1)
                nc.scalar.activation(out[:, :, c * P:(c + 1) * P], ps[:, Y, 0:2 * P].rearrange("p (m i) -> p m i", m=2), ACT.Copy).then_inc(y_out, 1)
    head_norm_stage(C, name + "_norm", out, out, C.const("pairs"), HEAD, C.eps, norm, z)


class Vectors:

    def __init__(self):
        self.at, self.width, self.shapes = {}, 0, {}

    def add(self, name, shape):
        self.at[name], self.shapes[name] = self.width, tuple(shape)
        self.width += int(np.prod(shape))

    def view(self, buffer, name):
        shape = self.shapes[name]
        v = buffer[:, self.at[name]:self.at[name] + int(np.prod(shape))]
        if len(shape) == 2:
            return v.rearrange("p (a b) -> p a b", b=shape[1])
        return v


def columns(a):
    return np.asarray(a).reshape(-1, P).T


def on_rows(a, rows=P):
    out = np.zeros((P, 1), np.float32)
    out[:len(a), 0] = a
    return out


def vector_arrays(inputs):
    v = {}
    for name in ("ffa_norm", "mix_norm", "ffb_norm"):
        for layer in range(2):
            v[f"{name}{layer}"] = ((8,), columns(inputs[name][layer]))
    v["final_norm"] = ((8,), columns(inputs["final_norm"]))
    for name, n in (("mu", 14), ("w0", 4), ("a0", 4), ("kk", 4), ("ka", 4), ("rk", 4), ("lnw", 4), ("lnb", 4)):
        v[name] = ((n,), columns(inputs["rwkv_" + name][0]))
    v["lam"] = ((4, HEAD), np.broadcast_to(np.asarray(inputs["diff_lam"][0]).reshape(1, -1), (P, 4 * HEAD)))
    v["subln"] = ((4,), np.repeat(columns(inputs["diff_subln"][0]), 4, 1))
    for kind in "kv":
        z = np.asarray(inputs["nsa_pe_" + kind][0]).reshape(16, 2, HEAD).transpose(2, 1, 0).reshape(HEAD, 32)
        v["pe_" + kind] = ((2, 16), np.concatenate([z, z], 0))
    v["mlstm_taps"] = ((4, 4), np.asarray(inputs["mlstm_conv_w"][0]).T.reshape(4, P, 4).transpose(1, 0, 2).reshape(P, 16))
    v["mlstm_bias"] = ((4,), columns(inputs["mlstm_conv_b"][0]))
    v["ig_b"] = ((1,), on_rows(inputs["mlstm_ig_b"][0]))
    v["fg_b"] = ((1,), on_rows(inputs["mlstm_fg_b"][0]))
    v["mlstm_norm"] = ((4,), columns(inputs["mlstm_norm"][0]))
    v["lb_logits"] = ((2, 2), columns(inputs["hgrn_lb_logits_2"]))
    for layer in range(2):
        for name in ("pre_mix_g", "post_mix_g", "pre_ffn_g", "post_ffn_g"):
            v[f"{name}{layer}"] = ((8,), columns(inputs[name + "_2"][layer]))
        norms = {name: columns(np.tile(np.asarray(inputs[name + "_norm_g_2"][layer]), 4)) for name in ("hgrn", "gla", "gdn")}
        v[f"gated_norm_g{layer}"] = ((4,), np.concatenate([norms["hgrn"], norms["gla"]], 1))
        v[f"gdn_norm_g{layer}"] = ((2,), norms["gdn"])
        v[f"gla_b{layer}"] = ((1,), columns(inputs["gla_b_gk_2"][layer]))
        v[f"mla_q_norm{layer}"] = ((2,), columns(inputs["mla_q_norm_g_2"][layer]))
        v[f"mla_kv_norm{layer}"] = ((1,), columns(inputs["mla_kv_norm_g_2"][layer]))
        v[f"gdn_taps{layer}"] = ((6, 4), np.asarray(inputs["gdn_conv_w_2"][layer]).T.reshape(6, P, 4).transpose(1, 0, 2).reshape(P, 24))
        v[f"gdn_a_log{layer}"] = ((1,), on_rows(inputs["gdn_a_log_2"][layer]))
        v[f"gdn_dt{layer}"] = ((1,), on_rows(inputs["gdn_dt_bias_2"][layer]))
        v[f"ffn_taps{layer}"] = ((FT, 3), np.asarray(inputs["ffn_conv_w_2"][layer]).T.reshape(FT, P, 3).transpose(1, 0, 2).reshape(P, FT * 3))
    return v


def starts(sizes):
    out, at = [], 0
    for s in sizes:
        out.append(at)
        at += s
    return out


AB_PIECES = [[(256 * n, 256)] for n in range(13)]


def first_mixers_even(C, V, io, mixed):
    with ExitStack() as ctx:
        pt = C.sb(ctx, "pt", [P, 14, T])
        w2a2, g2 = C.sb(ctx, "w2a2", [P, 512]), C.sb(ctx, "g2", [P, 512])
        with ExitStack() as qkv:
            qt, kt, v = (C.sb(qkv, n, [P, 4, T]) for n in ("qt", "kt", "v"))
            outs = [t_outs([z[:, 2 * n], z[:, 2 * n + 1]]) for z in (qt, kt) for n in range(2)]
            outs += [row_outs(256, [v[:, c, 256 * n:256 * n + 256] for c in range(NCH)]) for n in range(2)]
            outs += [t_outs([pt[:, 2 * n], pt[:, 2 * n + 1]]) for n in range(7)]
            proj_stage(C, "ab", V("mix_norm0"), io["ab_w_in"], list(zip(AB_PIECES, outs)),
                       [(w2a2[0:64], io["rwkv_w2"]), (w2a2[64:P], io["rwkv_a2"]), (g2, io["rwkv_g2"])])
            diff_attention(C, qkv, qt, kt, v, V("lam"), V("subln"), mixed)
        vec = {n: V(n) for n in ("mu", "w0", "a0", "kk", "ka", "rk", "lnw", "lnb")}
        rwkv(C, ctx, pt, vec, w2a2, w2a2, g2, mixed)


def cd_pieces():
    c_q, c_kc, c_vc, c_ks, c_vs, c_kw, c_vw, c_g, d_q, d_k, d_v, d_i, d_f, d_o = starts((512, 128, 128, 128, 128, 128, 128, 24, 256, 256, 512, 4, 4, 512))
    pieces = [[(c_q + 256 * o + 64 * (2 * n + m), 64) for m in range(2) for o in range(2)] for n in range(2)]
    pieces += [[(c_kc, 256)], [(c_ks, 128), (c_kw, 128)], [(c_vs, 128), (c_vw, 128)], [(c_g, 24), (d_i, 8)]]
    return pieces + [[(d_q, 256)], [(d_k, 256)], [(d_v, 256)], [(d_v + 256, 256)], [(d_o, 256)], [(d_o + 256, 256)]]


def first_mixers_odd(C, V, io, mixed):
    with ExitStack() as ctx:
        qk, og, vm = C.sb(ctx, "qk", [P, 4, T]), C.sb(ctx, "og", [P, 4, T]), C.sb(ctx, "vm", [P, NCH, 512])
        li, lf = C.sb(ctx, "li", [4, T]), C.sb(ctx, "lf", [4, T])
        qt, kc, vc, ks, kw = (C.sb(ctx, n, [P, k, T]) for n, k in (("qt", 4), ("kc", 1), ("vc", 1), ("ks", 1), ("kw", 1)))
        v_both = C.sb(ctx, "v_both", [P, NCH, 2 * P])
        vs, vw = v_both[:, :, 0:P], v_both[:, :, P:2 * P]
        gates = C.sb(ctx, "gates", [P, NCH, 24])
        outs = [t_outs([qt[:, 2 * n], qt[:, 2 * n + 1]]) for n in range(2)] + [t_outs([kc[:, 0], vc[:, 0]]), t_outs([ks[:, 0], kw[:, 0]])]
        outs += [row_outs(2 * P, [v_both[:, c] for c in range(NCH)])]
        outs += [row_outs(24, [gates[:, c] for c in range(NCH)]) + [((24, 28), None, li[:, :]), ((28, 32), None, lf[:, :])]]
        outs += [t_outs([qk[:, 2 * n], qk[:, 2 * n + 1]]) for n in range(2)]
        outs += [row_outs(256, [vm[:, c, 256 * n:256 * n + 256] for c in range(NCH)]) for n in range(2)]
        outs += [t_outs([og[:, 2 * n], og[:, 2 * n + 1]]) for n in range(2)]
        proj_stage(C, "cd", V("mix_norm1"), io["cd_w_in"], list(zip(cd_pieces(), outs)))
        taps, bias = V("mlstm_taps"), V("mlstm_bias")
        weights = [(io["nsa_w1_" + kind], io["nsa_w2_" + kind], V("pe_" + kind)) for kind in "kv"]
        sparse_attention(C, ctx, qt, kc[:, 0], vc[:, 0], ks[:, 0], vs, kw[:, 0], vw, gates, weights, mixed,
                         [(qk[:, m], qk[:, m], [taps[:, m, j:j + 1] for j in range(4)], bias[:, m:m + 1]) for m in range(4)])
        mlstm(C, ctx, qk, vm, li[:, :], lf[:, :], og[:, :, :], V("ig_b")[0:4], V("fg_b")[0:4], V("mlstm_norm"), mixed)


def second_pieces():
    s = starts((256, 256, 256, 256, 128, 128, 256, 16, 256, 256, 128, 32, 256, 256, 256, 4, 4, 256))
    whole = lambda n: [(s[n], 256)]
    pieces = [whole(0), whole(1), whole(3), whole(2), whole(4), whole(6), [(s[10], 160), (s[7], 16), (s[15], 8)], whole(8), whole(9)]
    return pieces + [whole(12), whole(13), whole(14), whole(17)]


def second_mixers(C, V, io, layer, lb, mixed):
    L = str(layer)
    with ExitStack() as ctx:
        qkv, z = C.sb(ctx, "qkv", [P, 6, T]), C.sb(ctx, "z", [P, 2, T])
        beta, alpha = C.sb(ctx, "beta", [4, T]), C.sb(ctx, "alpha", [4, T])
        with ExitStack() as inner:
            aq, af, cq = (C.sb(inner, n, [P, 2, T]) for n in ("aq", "af", "cq"))
            g_ab = C.sb(inner, "g_ab", [P, 4, T])
            ag, bg = g_ab[:, 0:2], g_ab[:, 2:4]
            bq, bk, ckv = (C.sb(inner, n, [P, 1, T]) for n in ("bq", "bk", "ckv"))
            kr, code = C.sb(inner, "kr", [P, T]), C.sb(inner, "code", [16, T])
            av, bv = C.sb(inner, "av", [P, NCH, 256]), C.sb(inner, "bv", [P, NCH, 256])
            w_gk2, w_ukv = C.sb(inner, "w_gk2", [16, P]), C.sb(inner, "w_ukv", [P, 512])
            w_uq = mixed[:, 6:8].rearrange("p m t -> p (m t)")[:, 0:768].rearrange("p (a f) -> p a f", a=2)
            outs = [t_outs([d[:, 0], d[:, 1]]) for d in (aq, af, ag)]
            outs += [row_outs(256, [av[:, c] for c in range(NCH)]), t_outs([bq[:, 0], bk[:, 0]]), row_outs(256, [bv[:, c] for c in range(NCH)])]
            outs += [[((0, P), None, ckv[:, 0]), ((P - 64, P + 32), None, kr[64:96], 64), ((160, 176), None, code[:, :]),
                      ((176, 180), None, beta[:, :]), ((180, 184), None, alpha[:, :])]]
            outs += [t_outs([d[:, 0], d[:, 1]]) for d in (bg, cq)]
            outs += [t_outs([qkv[:, 2 * n], qkv[:, 2 * n + 1]]) for n in range(3)] + [t_outs([z[:, 0], z[:, 1]])]
            proj_stage(C, "in" + L, V("pre_mix_g" + L), io["in" + L], list(zip(second_pieces(), outs)),
                       [(w_gk2, io["gla_w_gk2_2"][layer]), (w_ukv, io["mla_w_ukv_2"][layer]), (w_uq, io["mla_w_uq_2"][layer].rearrange("(a p) f -> p a f", p=P))])
            gdn_taps = V("gdn_taps" + L)
            convs = [(qkv[:, m], qkv[:, m], [gdn_taps[:, m, j:j + 1] for j in range(4)], None) for m in range(6)]
            with ExitStack() as one:
                hgrn(C, one, "hgrn" + L, aq[:, :, :], af[:, :, :], av, g_ab[:, 0:2], lb, mixed[:, 0:2], convs[0:3])
            with ExitStack() as one:
                gla(C, one, "gla" + L, bq[:, :, :], bk[:, :, :], bv, code[:, :], g_ab[:, 2:4], w_gk2[:, :], V("gla_b" + L), mixed[:, 2:4], convs[3:6])
            head_norm_stage(C, "gated_norm" + L, mixed[:, 0:4], mixed[:, 0:4], C.const("pairs"), HEAD, C.eps, V("gated_norm_g" + L), g_ab[:, :, :])
            with ExitStack() as one:
                mla(C, one, "mla" + L, cq[:, :, :], ckv[:, :, :], kr[:, :], V("mla_q_norm" + L), V("mla_kv_norm" + L), w_uq, w_ukv[:, :], mixed[:, 4:6])
        gated_delta(C, ctx, "gdn" + L, qkv, z[:, :, :], beta[:, :], alpha[:, :], V("gdn_a_log" + L)[0:4], V("gdn_dt" + L)[0:4], V("gdn_norm_g" + L), mixed[:, 6:8])


def first_chunks(io):
    ab, cd = (proj_chunks(io[n + "_w_in"], pieces)[0:2] for n, pieces in (("ab", AB_PIECES), ("cd", cd_pieces())))
    order = []
    for layer, name, proj in ((0, "ab", ab), (1, "cd", cd)):
        order += [io[f"ffa{layer}_gates"], proj, io[name + "_w_out"], io[f"ffb{layer}_gates"]]
    for layer in range(2):
        order += [proj_chunks(io[f"in{layer}"], second_pieces())[0:2], io[f"out{layer}_w"], io[f"ffn{layer}_gates"]]
    return [[w[0], w[1]] for w in order]


def build_program(nc, io, vectors):
    with ExitStack() as ctx:
        C = Core(nc, ctx)
        C.streams = first_chunks(io)
        vecs = C.sb(ctx, "vecs", [P, vectors.width])
        lb = C.sb(ctx, "lb", [P, 2])
        C.setup(io["consts"], io["x_t"], vecs[:, :], io["vecs"])

        def V(name):
            return vectors.view(vecs, name)

        for layer in range(2):
            ffn_stage(C, f"ffa{layer}", V(f"ffa_norm{layer}"), io, 0.5)
            with ExitStack() as mctx:
                mixed = C.sb(mctx, "mixed", [P, KT, T])
                (first_mixers_even, first_mixers_odd)[layer](C, V, io, mixed)
                out_stage(C, f"first_out{layer}", io[("ab", "cd")[layer] + "_w_out"], mixed)
            ffn_stage(C, f"ffb{layer}", V(f"ffb_norm{layer}"), io, 0.5, post=("replace", V("final_norm")) if layer else None)
        lower_bound_stage(C, "bounds", V("lb_logits"), lb[:, :])
        for layer in range(2):
            with ExitStack() as mctx:
                mixed = C.sb(mctx, "mixed", [P, KT, T])
                second_mixers(C, V, io, layer, lb[:, :] if layer else None, mixed)
                out_stage(C, f"second_out{layer}", io[f"out{layer}_w"], mixed, V(f"post_mix_g{layer}"))
            ffn_stage(C, f"ffn{layer}", V(f"pre_ffn_g{layer}"), io, 1.0, taps=V(f"ffn_taps{layer}"), post=("add", V(f"post_ffn_g{layer}")))
        C.store(io["out"], C.x)


WEIGHTS = ("gla_w_gk2_2", "mla_w_ukv_2", "mla_w_uq_2")
ONE_LAYER = ("rwkv_w2", "rwkv_a2", "rwkv_g2", "nsa_w1_k", "nsa_w2_k", "nsa_w1_v", "nsa_w2_v")


def launch_arrays(inputs):
    arrays = {n: inputs[n] for n in WEIGHTS}
    arrays.update({n: inputs[n][0] for n in ONE_LAYER})
    for layer in range(2):
        for name in ("ffa", "ffb"):
            arrays.update(ffn_arrays(f"{name}{layer}", *(np.asarray(inputs[f"{name}_{part}"][layer]) for part in ("gate", "up", "down"))))
        arrays.update(ffn_arrays(f"ffn{layer}", *(np.asarray(inputs[f"ffn_w_{part}_2"][layer]) for part in ("gate", "up", "down"))))
        arrays.update(proj_arrays(f"in{layer}", np.asarray(inputs["w_in_2"][layer]), second_pieces()))
        arrays.update(out_arrays(f"out{layer}_w", np.asarray(inputs["w_out_2"][layer])))
    for name, pieces in (("ab", AB_PIECES), ("cd", cd_pieces())):
        arrays.update(proj_arrays(name + "_w_in", np.asarray(inputs[name + "_w_in"][0]), pieces))
        arrays.update(out_arrays(name + "_w_out", np.asarray(inputs[name + "_w_out"][0])))
    arrays["x_t"] = np.asarray(inputs["x"])[0].T.reshape(KT, P, T).transpose(1, 0, 2)
    arrays["consts"] = const_arrays()
    vectors = Vectors()
    parts = vector_arrays(inputs)
    for name, (shape, a) in parts.items():
        vectors.add(name, shape)
    arrays["vecs"] = np.concatenate([a for _, a in parts.values()], 1)
    return {n: np.ascontiguousarray(a) for n, a in arrays.items()}, vectors


def kernel(**inputs):
    import concourse.bacc as bacc
    from concourse.bass_utils import run_bass_kernel_spmd

    nc = bacc.Bacc("TRN2", target_bir_lowering=False, num_devices=1)
    arrays, vectors = launch_arrays(inputs)
    io = {n: nc.dram_tensor("in_" + n, a.shape, F32, kind="ExternalInput").ap() for n, a in arrays.items()}
    io["out"] = nc.dram_tensor("out_0", (P, KT, T), F32, kind="ExternalOutput").ap()
    build_program(nc, io, vectors)
    r = run_bass_kernel_spmd(nc, [{"in_" + n: a for n, a in arrays.items()}], core_ids=[0])
    got = r.results[0]["out_0"]
    return np.ascontiguousarray(got.transpose(2, 1, 0).reshape(1, T, D))
```
